# Optimizing a Trainium2 kernel written in Bass

```python
import math
import jax
import jax.numpy as jnp
from jax import lax
import numpy as np

D_MODEL = 1024
BATCH = 1
SEQ = 2048
DEPTH = 1

D_MIX = D_MODEL
D_HYENA = D_MIX // 2
D_POOL = D_MIX - D_HYENA
HYENA_ORDER = 2
SHORT_CONV = 3
FILTER_EMB = 33
FILTER_HIDDEN = 64
FILTER_INNER = 2
DECAY_TARGET = 1e-2
FAST_DECAY_PCT = 0.3
SLOW_DECAY_PCT = 1.5
POOL_WINDOWS = (2, 4, 8, 16)
N_POOL_GROUPS = len(POOL_WINDOWS)
POOL_GROUP = D_POOL // N_POOL_GROUPS
D_HY_STREAMS = (HYENA_ORDER + 1) * D_HYENA
D_IN_PROJ = D_HY_STREAMS + D_HYENA + 2 * D_POOL
DEEPNORM_ALPHA = (2.0 * DEPTH) ** 0.25
DEEPNORM_BETA = (8.0 * DEPTH) ** -0.25
LN_EPS = 1e-5

kernel_name = "hybrid_hyena_pool_adaln_deepnorm_encoder"

def _layer_norm(x, g, b):
    xf = x.astype(jnp.float32)
    mu = jnp.mean(xf, axis=-1, keepdims=True)
    var = jnp.mean(jnp.square(xf - mu), axis=-1, keepdims=True)
    y = (xf - mu) * lax.rsqrt(var + LN_EPS)
    return (y * g.astype(jnp.float32) + b.astype(jnp.float32)).astype(x.dtype)

def _short_conv(u, w, b):
    L = u.shape[1]
    pad = SHORT_CONV // 2
    up = jnp.pad(u, ((0, 0), (pad, SHORT_CONV - 1 - pad), (0, 0)))
    out = b
    for j in range(SHORT_CONV):
        out = out + up[:, j:j + L] * w[j]
    return out

def _filter_pos_features(L):
    t = jnp.linspace(0.0, 1.0, L, dtype=jnp.float32)[:, None]
    bands = (FILTER_EMB - 1) // 2
    w = (2.0 * math.pi / L) * jnp.arange(L, dtype=jnp.float32)[:, None]
    f = jnp.linspace(1e-4, bands - 1, bands, dtype=jnp.float32)[None, :]
    z = jnp.concatenate([t, jnp.cos(f * w), -jnp.sin(f * w)], axis=-1)
    return t, z

def _decay_window(t):
    min_decay = math.log(DECAY_TARGET) / SLOW_DECAY_PCT
    max_decay = math.log(DECAY_TARGET) / FAST_DECAY_PCT
    deltas = jnp.linspace(min_decay, max_decay, D_HYENA, dtype=jnp.float32)
    return jnp.exp(-t * jnp.abs(deltas)[None, :])

def _hyena_filters_freq(z_pos, decay, w1, b1, w_inner, b_inner, w_out, freq):
    L = z_pos.shape[0]
    f32 = jnp.float32
    fr = freq.astype(f32)
    h = jnp.sin(fr * (z_pos @ w1.astype(f32) + b1.astype(f32)))
    for i in range(FILTER_INNER):
        h = jnp.sin(fr * (h @ w_inner[i].astype(f32) + b_inner[i].astype(f32)))
    k = (h @ w_out.astype(f32)).reshape(L, HYENA_ORDER, 2, D_HYENA)
    k = k * decay[:, None, None, :]
    k2 = jnp.concatenate([k[:, :, 0], k[::-1, :, 1]], axis=0)
    return jnp.fft.rfft(k2, n=2 * L, axis=0)

def _bidir_long_conv(u, k_freq, bias):
    L = u.shape[1]
    u_freq = jnp.fft.rfft(u, n=2 * L, axis=1)
    y = jnp.fft.irfft(u_freq * k_freq[None], n=2 * L, axis=1)[:, :L]
    return y + u * bias.astype(jnp.float32)

def _hyena_branch(streams, conv_w, conv_b, k_freq, bias):
    s = _short_conv(streams, conv_w, conv_b).astype(jnp.float32)
    v, x1, x2 = jnp.split(s, HYENA_ORDER + 1, axis=-1)
    z = v
    for o, g in enumerate((x1, x2)):
        z = g * _bidir_long_conv(z, k_freq[:, o], bias[o])
    return z

def _pool_branch(u, pool_w, pool_scale):
    B, L, _ = u.shape
    uf = u.astype(jnp.float32)
    cs = jnp.pad(jnp.cumsum(uf, axis=1), ((0, 0), (1, 0), (0, 0)))
    pos = jnp.arange(L)
    groups = []
    for g, w in enumerate(POOL_WINDOWS):
        sl = slice(g * POOL_GROUP, (g + 1) * POOL_GROUP)
        hi = jnp.minimum(pos + w // 2, L)
        lo = jnp.maximum(pos - w // 2, 0)
        cnt = (hi - lo).astype(jnp.float32)[None, :, None]
        mean = (cs[:, hi, sl] - cs[:, lo, sl]) / cnt
        groups.append(mean - uf[..., sl])
    p = jnp.stack(groups, axis=2)
    p = jnp.einsum('blgc,gcd->blgd', p, pool_w.astype(jnp.float32)).reshape(B, L, D_POOL)
    return p * pool_scale.astype(jnp.float32)

def setup_inputs(seed: int = 0) -> dict:
    key = jax.random.key(seed)
    ks = jax.random.split(key, 21)
    f32 = jnp.float32

    def nrm(k, shape, scale):
        return jax.random.normal(k, shape, f32) * scale

    n = DEPTH
    return {
        "x": nrm(ks[0], (BATCH, SEQ, D_MODEL), 1.0),
        "c": nrm(ks[1], (BATCH, D_MODEL), 1.0),
        "w_ada": nrm(ks[2], (n, D_MODEL, 3 * D_MODEL), 0.5 * D_MODEL ** -0.5),
        "b_ada": nrm(ks[3], (n, 3 * D_MODEL), 0.02),
        "w_in": nrm(ks[4], (n, D_MODEL, D_IN_PROJ), D_MODEL ** -0.5),
        "b_in": nrm(ks[5], (n, D_IN_PROJ), 0.02),
        "conv_w": nrm(ks[6], (n, SHORT_CONV, D_HY_STREAMS), SHORT_CONV ** -0.5),
        "conv_b": nrm(ks[7], (n, D_HY_STREAMS), 0.02),
        "filt_w1": nrm(ks[8], (n, FILTER_EMB, FILTER_HIDDEN), FILTER_EMB ** -0.5),
        "filt_b1": nrm(ks[9], (n, FILTER_HIDDEN), 0.1),
        "filt_w_inner": nrm(ks[10], (n, FILTER_INNER, FILTER_HIDDEN, FILTER_HIDDEN), FILTER_HIDDEN ** -0.5),
        "filt_b_inner": nrm(ks[11], (n, FILTER_INNER, FILTER_HIDDEN), 0.1),
        "filt_w_out": nrm(ks[12], (n, FILTER_HIDDEN, HYENA_ORDER * 2 * D_HYENA),
                          FILTER_HIDDEN ** -0.5 * (SEQ / 8.0) ** -0.5),
        "filt_freq": 1.0 + nrm(ks[13], (n, FILTER_HIDDEN), 0.1),
        "hyena_bias": nrm(ks[14], (n, HYENA_ORDER, D_HYENA), 1.0),
        "pool_w": nrm(ks[15], (n, N_POOL_GROUPS, POOL_GROUP, POOL_GROUP), POOL_GROUP ** -0.5),
        "pool_scale": 1.0 + nrm(ks[16], (n, D_POOL), 0.1),
        "w_out": nrm(ks[17], (n, D_MIX, D_MODEL), D_MIX ** -0.5 * DEEPNORM_BETA),
        "b_out": nrm(ks[18], (n, D_MODEL), 0.02),
        "ln_g": 1.0 + nrm(ks[19], (n, D_MODEL), 0.05),
        "ln_b": nrm(ks[20], (n, D_MODEL), 0.02),
    }

def reference(x, c, w_ada, b_ada, w_in, b_in, conv_w, conv_b, filt_w1, filt_b1,
              filt_w_inner, filt_b_inner, filt_w_out, filt_freq, hyena_bias,
              pool_w, pool_scale, w_out, b_out, ln_g, ln_b):
    L = x.shape[1]
    t, z_pos = _filter_pos_features(L)
    decay = _decay_window(t)
    splits = [D_HY_STREAMS, D_HY_STREAMS + D_HYENA, D_HY_STREAMS + D_HYENA + D_POOL]
    h = x
    for layer in range(DEPTH):
        mod = jax.nn.silu(c) @ w_ada[layer] + b_ada[layer]
        shift, scale, gate = jnp.split(mod, 3, axis=-1)
        u = h * (1.0 + scale[:, None, :]) + shift[:, None, :]
        proj = u @ w_in[layer] + b_in[layer]
        hy_streams, hy_gate, pool_in, pool_gate = jnp.split(proj, splits, axis=-1)
        k_freq = _hyena_filters_freq(z_pos, decay, filt_w1[layer], filt_b1[layer],
                                     filt_w_inner[layer], filt_b_inner[layer],
                                     filt_w_out[layer], filt_freq[layer])
        y_h = _hyena_branch(hy_streams, conv_w[layer], conv_b[layer], k_freq, hyena_bias[layer])
        y_p = _pool_branch(pool_in, pool_w[layer], pool_scale[layer])
        y = jnp.concatenate([y_h * jax.nn.silu(hy_gate.astype(jnp.float32)),
                             y_p * jax.nn.silu(pool_gate.astype(jnp.float32))],
                            axis=-1).astype(x.dtype)
        out = gate[:, None, :] * (y @ w_out[layer] + b_out[layer])
        h = _layer_norm(DEEPNORM_ALPHA * h + out, ln_g[layer], ln_b[layer])
    return h


_drawn_inputs = setup_inputs


def setup_inputs(seed=0):
    import zlib

    import numpy as np

    out = dict(_drawn_inputs(seed))
    spreads = {}
    factors = {'b_in': 3.832, 'pool_scale': 8.0, 'b_out': 8.0, 'ln_b': 2.95}
    for name, (base, spread) in spreads.items():
        noise = np.random.default_rng([zlib.crc32(name.encode()), seed]).standard_normal(out[name].shape)
        drawn = base * np.exp(spread * noise) if base else spread * noise
        out[name] = jnp.asarray(drawn.astype(out[name].dtype))
    for name, factor in factors.items():
        out[name] = (out[name] * factor).astype(out[name].dtype)
    return out
```

```python
from contextlib import ExitStack
import math

import numpy as np

import concourse.bass as bass
from concourse import mybir

F32 = mybir.dt.float32
F32R = mybir.dt.float32r
ALU = mybir.AluOpType
ACT = mybir.ActivationFunctionType

P = 128
D = 1024
L = 2048
DH = 512
NF = 2 * L
N1 = 32
KT = D // P
PROJ = 3 * DH + DH + 2 * DH
EMB, HID = 33, 64
GS = L // P
GF = NF // P
NPAIR = N1 // 2
CH = 512
ALPHA = 2.0 ** 0.25
LN_EPS = 1e-5
WINDOWS = (2, 4, 8, 16)
POOL_STEPS = [sum(w.bit_length() - 1 + (3 if w > 2 else 2) for w in WINDOWS[:i + 1]) for i in range(4)]
PAD = 8



def _round12(a):
    b = np.ascontiguousarray(a, np.float32).view(np.uint32)
    b = (b + np.uint32(0x7FF) + ((b >> np.uint32(12)) & np.uint32(1))) & np.uint32(0xFFFFF000)
    return b.view(np.float32)


def _hilo(a, axis):
    hi = _round12(a)
    lo = _round12(np.asarray(a, np.float64) - hi)
    return np.ascontiguousarray(np.stack([hi, lo], axis=axis))


def shape_tables():
    tau = 2 * np.pi

    def row(slot, t1, t2):
        q = slot // 2
        ang = tau * ((q * (P * t1 + t2)) % NF) / NF
        v = np.where(slot % 2 == 0, np.cos(ang), -np.sin(ang))
        return np.where(slot == 0, 1.0, np.where(slot == 1, 1.0 - 2.0 * (t1 % 2), v))

    p = np.arange(P)
    g = np.arange(GF)[:, None, None]
    v = row(p[None, None, :] // 4, p[None, :, None] // 4, 32 * (p[None, :, None] % 4) + g)
    same = (p[:, None] % 4) == (p[None, :] % 4)
    w1f = _hilo(v * same[None], 2)
    g = np.arange(GS)[:, None, None]
    same = (p[:, None] % 8) == (p[None, :] % 8)
    halves = []
    for m in range(2):
        v = row(16 * m + p[None, None, :] // 8, p[None, :, None] // 8, 16 * (p[None, :, None] % 8) + g)
        halves.append(v * same[None])
    w1s = _hilo(np.stack(halves, 2), 3)
    iw1 = _hilo(np.stack([h.transpose(0, 2, 1) for h in halves], 2) * (2.0 / NF), 3)
    ang = tau * ((p[:, None] * p[None, :]) % P) / P
    dft = _hilo(np.stack([np.cos(ang), np.sin(ang), -np.sin(ang)], 1), 2)
    j = np.arange(64)
    f0 = np.zeros((P, 4, P))
    a0 = tau * ((p[:, None] * j) % P) / P
    a16 = tau * ((p[:, None] * (16 + 32 * j)) % NF) / NF
    f0[:, 0, :64] = np.cos(a0)
    f0[:, 1, :64] = -np.sin(a0)
    f0[:, 1, 0] = 1.0 - 2.0 * (p % 2)
    f0[:, 2, 64:] = np.cos(a16)
    f0[:, 3, 64:] = -np.sin(a16)
    inv = np.zeros((P, 4, P))
    for i in range(2):
        for o in range(2):
            inv[:, o * 2 + i, :] = f0[:, i * 2 + o, :].T
    inv[0] *= 0.5
    f32 = np.float32
    t = np.linspace(0.0, 1.0, L, dtype=f32)[:, None]
    bands = (EMB - 1) // 2
    w = f32(2.0 * math.pi / L) * np.arange(L, dtype=f32)[:, None]
    f = np.linspace(1e-4, bands - 1, bands, dtype=f32)[None, :]
    fw = (f * w).astype(np.float64)
    z = np.concatenate([t, np.cos(fw), -np.sin(fw)], axis=-1).astype(f32)
    z2 = np.ascontiguousarray(np.concatenate([z.T, z[::-1].T], 0))
    deltas = np.linspace(math.log(1e-2) / 1.5, math.log(1e-2) / 0.3, DH, dtype=f32)
    dec = np.exp((-t * np.abs(deltas)[None, :]).astype(np.float64)).astype(f32)
    dec = np.concatenate([dec, dec[::-1]], 0).reshape(P, GF, DH).transpose(1, 0, 2)
    edge = np.ones((4, 2, PAD))
    for gi, win in enumerate(WINDOWS):
        h = win // 2
        for i in range(h):
            edge[gi, 0, i] = win / (i + h)
        for i in range(h - 1):
            edge[gi, 1, PAD - 1 - i] = win / (1 + i + h)
    return {
        "t_w1f": w1f, "t_w1s": w1s, "t_iw1": iw1, "t_dft": dft,
        "t_f0": _hilo(f0, 2), "t_i0": _hilo(inv, 2), "t_z": z2,
        "t_decay": np.ascontiguousarray(dec),
        "t_edge": np.ascontiguousarray(edge, f32), "t_eye": np.eye(P, dtype=f32),
    }



def mm3(nc, out, w, m, start, stop):
    nc.tensor.matmul(out, w[0], m[0], start=start, stop=False, skip_group_check=True)
    nc.tensor.matmul(out, w[0], m[1], start=False, stop=False, skip_group_check=True)
    return nc.tensor.matmul(out, w[1], m[0], start=False, stop=stop, skip_group_check=True)


def f32(ap):
    return ap.bitcast(F32)


def plain(eng, sem):
    eng.wait_ge(sem, 0)


class Scope:

    def __init__(self, nc, tag):
        self.nc, self.tag, self.ctx, self.semaphores = nc, tag, ExitStack(), []

    def __enter__(self):
        return self

    def __exit__(self, *a):
        self.ctx.__exit__(*a)
        if self.semaphores:
            self.nc.clear_and_free_semaphores(self.semaphores)
            self.nc.all_engine_barrier()

    def sb(self, name, shape, dt=F32):
        return self.ctx.enter_context(self.nc.sbuf_tensor(f"{self.tag}_{name}", shape, dt))

    def ps(self, name, shape):
        return self.ctx.enter_context(self.nc.psum_tensor(f"{self.tag}_{name}", shape, F32))

    def sem(self, name):
        self.semaphores.append(self.nc.alloc_semaphore(f"{self.tag}_{name}"))
        return self.semaphores[-1]

    def sems(self, name, n=2):
        return [self.sem(f"{name}{i}") for i in range(n)]

    def block(self):
        return self.ctx.enter_context(self.nc.Block())



def filter_network(nc, t, hfil):
    MAGIC = 1.5 * 2.0 ** 23
    C1, C2 = 6.28125, float(np.float32(0.0019350051879882812))
    C3 = 2 * math.pi - C1 - C2
    PI = 3.1415925
    with Scope(nc, "net") as s:
        feat = s.sb("feat", [P, L])
        wl = s.sb("wl", [P, 3, P])
        cols = s.sb("cols", [P, 4])
        arg = s.sb("arg", [P, L])
        turn = s.sb("turn", [P, L])
        h = s.sb("h", [P, L])
        ps = s.ps("ps", [P, 4, CH])
        zeroed, loaded, lin_done, sin_done, step, fold_done, split_hi, split_lo = (
            s.sem(n) for n in ("zeroed", "loaded", "lin_done", "sin_done", "step", "fold_done", "split_hi", "split_lo"))
        block = s.block()
        psf = ps[:, :, :].rearrange("p a b -> p (a b)")

        @block.sync
        def _(sp):
            n = 0
            sp.dma_start(feat[0:2 * EMB, :], t["t_z"][:, :]).then_inc(loaded, 16)
            for half in range(2):
                hs = slice(64 * half, 64 * half + 64)
                for c, src in enumerate((t["filt_b1"][0, :], t["filt_b_inner"][0, 0, :],
                                         t["filt_b_inner"][0, 1, :], t["filt_freq"][0, :])):
                    sp.dma_start(cols[hs, c:c + 1], src.rearrange("(p o) -> p o", o=1)).then_inc(loaded, 16)
            sp.wait_ge(zeroed, 1)
            for half in range(2):
                hs = slice(64 * half, 64 * half + 64)
                sp.dma_start(wl[EMB * half:EMB * half + EMB, 0, hs], t["filt_w1"][0, :, :]).then_inc(loaded, 16)
                for i in range(2):
                    sp.dma_start(wl[hs, 1 + i, hs], t["filt_w_inner"][0, i, :, :]).then_inc(loaded, 16)

        @block.gpsimd
        def _(pool):
            nc.gpsimd.memset(wl[:, :, :], 0.0).then_inc(zeroed, 1)
            pool.wait_ge(zeroed, 1)
            nc.gpsimd.memset(f32(hfil[0:64, :, 64:128, :]), 0.0).then_inc(zeroed, 1)
            pool.wait_ge(zeroed, 2)
            nc.gpsimd.memset(f32(hfil[64:128, :, 0:64, :]), 0.0).then_inc(zeroed, 1)
            pool.wait_ge(zeroed, 3)

        @block.tensor
        def _(pe):
            pe.wait_ge(loaded, 15 * 16)
            for layer in range(3):
                if layer:
                    pe.wait_ge(sin_done, layer)
                src, k = (feat, 2 * EMB) if layer == 0 else (h, P)
                for c in range(4):
                    mm = nc.tensor.matmul(ps[:, c, :], wl[0:k, layer, :], src[0:k, c * CH:(c + 1) * CH],
                                          start=True, stop=True)
                mm.then_inc(lin_done, 1)

        @block.vector
        def _(dve):
            n = 0
            for layer in range(3):
                dve.wait_ge(lin_done, layer + 1)
                if layer:
                    dve.wait_ge(sin_done, layer)
                nc.vector.tensor_scalar(arg[:, :], psf, cols[:, layer:layer + 1], cols[:, 3:4],
                                        ALU.add, ALU.mult).then_inc(step, 1)
                dve.wait_ge(step, n + 1)
                nc.vector.tensor_scalar(turn[:, :], arg[:, :], 1.0 / (2 * math.pi), MAGIC,
                                        ALU.mult, ALU.add).then_inc(step, 1)
                dve.wait_ge(step, n + 2)
                nc.vector.tensor_scalar(turn[:, :], turn[:, :], MAGIC, None, ALU.subtract).then_inc(step, 1)
                n += 3
                for c in (C1, C2, C3):
                    dve.wait_ge(step, n)
                    nc.vector.scalar_tensor_tensor(out=arg[:, :], in0=turn[:, :], scalar=-c, in1=arg[:, :],
                                                   op0=ALU.mult, op1=ALU.add).then_inc(step, 1)
                    n += 1
                dve.wait_ge(step, n)
                nc.vector.tensor_scalar(arg[:, :], arg[:, :], PI, -PI, ALU.min, ALU.max).then_inc(fold_done, 1)
            for half in range(2):
                hs = slice(64 * half, 64 * half + 64)
                dve.wait_ge(split_hi, half + 1)
                nc.vector.tensor_tensor(hfil[hs, 1, hs, :], h[hs, :].rearrange("p (c g) -> p c g", g=GF),
                                        f32(hfil[hs, 0, hs, :]), ALU.subtract).then_inc(split_lo, 1)
            dve.wait_ge(split_lo, 2)

        @block.scalar
        def _(act):
            for layer in range(3):
                act.wait_ge(fold_done, layer + 1)
                nc.scalar.activation(h[:, :], arg[:, :], ACT.Sin).then_inc(sin_done, 1)
            act.wait_ge(sin_done, 3)
            for half in range(2):
                hs = slice(64 * half, 64 * half + 64)
                nc.scalar.activation(hfil[hs, 0, hs, :], h[hs, :].rearrange("p (c g) -> p c g", g=GF),
                                     ACT.Copy).then_inc(split_hi, 1)



def filter_stage1(nc, t, hfil, xf):
    with Scope(nc, "fs1") as s:
        wfil = s.sb("wfil", [P, 2, 2, DH], F32R)
        e0 = s.sb("e0", [1, P])
        bias = s.sb("bias", [1, 2, DH])
        hs_ = [s.sb(f"hs{b}", [P, 2, P], F32R) for b in range(2)]
        tab = [s.sb(f"tab{b}", [P, 2, P], F32R) for b in range(2)]
        dec = [s.sb(f"dec{b}", [P, DH]) for b in range(2)]
        kf = [s.sb(f"k{b}", [P, 2, DH]) for b in range(2)]
        wraw = kf[0]
        khi = [s.sb(f"khi{b}", [P, 2, DH], F32R) for b in range(2)]
        klo = [s.sb(f"klo{b}", [P, 2, DH], F32R) for b in range(2)]
        gen_ps = [s.ps(f"gen{b}", [P, 2, CH]) for b in range(2)]
        s1_ps = [s.ps(f"s1{b}", [P, 2, CH]) for b in range(2)]
        loaded, e0_set, whi_done, wlo_done = (s.sem(n) for n in ("loaded", "e0_set", "whi_done", "wlo_done"))
        dec_in, tab_in, hs_ready, gen_done, k_done, hi_done, lo_done, s1_done, evac_done = (
            s.sems(n) for n in ("dec_in", "tab_in", "hs_ready", "gen_done", "k_done", "hi_done", "lo_done",
                                "s1_done", "evac_done"))
        block = s.block()
        NP = GF // 2

        @block.sync
        def _(sp):
            wsrc = t["filt_w_out"][0, :, :].rearrange("f (o r d) -> f o r d", o=2, r=2)
            for r in range(2):
                sp.dma_start(wraw[64 * r:64 * r + 64, :, :], wsrc[:, :, r, :]).then_inc(loaded, 16)
            sp.dma_start(bias[:, :, :], t["hyena_bias"][0:1, :, :]).then_inc(loaded, 16)
            with sp.Fori(0, NP) as it:
                for b in range(2):
                    sp.wait_ge(k_done[b], it)
                    sp.dma_start(dec[b][:, :], t["t_decay"][2 * it + b, :, :]).then_inc(dec_in[b], 16)

        @block.gpsimd
        def _(pool):
            nc.gpsimd.memset(e0[:, :], 0.0).then_inc(e0_set, 1)
            pool.wait_ge(e0_set, 1)
            nc.gpsimd.memset(e0[:, 0:1], 1.0).then_inc(e0_set, 1)
            for it in range(NP):
                for b in range(2):
                    pool.wait_ge(gen_done[b], it)
                    nc.gpsimd.tensor_copy(hs_[b][:, :, :], hfil[:, :, :, 2 * it + b]).then_inc(hs_ready[b], 1)
                    pool.wait_ge(s1_done[b], it)
                    pool.dma_start(tab[b][:, :, :], t["t_w1f"][2 * it + b, :, :, :]).then_inc(tab_in[b], 16)

        @block.tensor
        def _(pe):
            def gen(it, b, first=False):
                pe.wait_ge(hs_ready[b], it + 1)
                pe.wait_ge(k_done[b], it)
                for o in range(2):
                    mm = mm3(nc, gen_ps[b][:, o, :], (hs_[b][:, 0, :], hs_[b][:, 1, :]),
                             (wfil[:, 0, o, :], wfil[:, 1, o, :]), True, not first)
                    if first:
                        mm = nc.tensor.matmul(gen_ps[b][:, o, :], e0[:, :], bias[:, o, :], start=False, stop=True,
                                              skip_group_check=True)
                mm.then_inc(gen_done[b], 1)

            def stage1(it, b):
                pe.wait_ge(lo_done[b], it + 1)
                pe.wait_ge(tab_in[b], 16 * it + 16)
                pe.wait_ge(evac_done[b], it)
                for o in range(2):
                    mm = mm3(nc, s1_ps[b][:, o, :], (tab[b][:, 0, :], tab[b][:, 1, :]),
                             (khi[b][:, o, :], klo[b][:, o, :]), True, True)
                mm.then_inc(s1_done[b], 1)

            pe.wait_ge(wlo_done, 1)
            pe.wait_ge(loaded, 48)
            pe.wait_ge(e0_set, 2)
            gen(0, 0, first=True)
            with pe.Fori(0, NP - 1) as it:
                gen(it, 1)
                stage1(it, 0)
                gen(it + 1, 0)
                stage1(it, 1)
            gen(NP - 1, 1)
            stage1(NP - 1, 0)
            stage1(NP - 1, 1)

        @block.vector
        def _(dve):
            def window(it, b):
                dve.wait_ge(gen_done[b], it + 1)
                dve.wait_ge(dec_in[b], 16 * it + 16)
                dve.wait_ge(lo_done[b], it)
                nc.vector.tensor_tensor(kf[b][:, :, :], gen_ps[b][:, :, :],
                                        dec[b][:, :].unsqueeze(1).broadcast_to([P, 2, DH]),
                                        ALU.mult).then_inc(k_done[b], 1)

            def low(it, b):
                dve.wait_ge(hi_done[b], it + 1)
                dve.wait_ge(s1_done[b], it)
                nc.vector.tensor_tensor(klo[b][:, :, :], kf[b][:, :, :], f32(khi[b][:, :, :]),
                                        ALU.subtract).then_inc(lo_done[b], 1)

            dve.wait_ge(whi_done, 1)
            nc.vector.tensor_tensor(wfil[:, 1, :, :], wraw[:, :, :], f32(wfil[:, 0, :, :]),
                                    ALU.subtract).then_inc(wlo_done, 1)
            window(0, 0)
            with dve.Fori(0, NP - 1) as it:
                window(it, 1)
                low(it, 0)
                window(it + 1, 0)
                low(it, 1)
            window(NP - 1, 1)
            low(NP - 1, 0)
            low(NP - 1, 1)

        @block.scalar
        def _(act):
            def high(it, b):
                act.wait_ge(k_done[b], it + 1)
                act.wait_ge(s1_done[b], it)
                nc.scalar.activation(khi[b][:, :, :], kf[b][:, :, :], ACT.Copy).then_inc(hi_done[b], 1)

            def evac(it, b):
                act.wait_ge(s1_done[b], it + 1)
                plain(act, loaded)
                nc.scalar.activation(xf[:, :, 2 * it + b, :], s1_ps[b][:, :, :], ACT.Copy).then_inc(evac_done[b], 1)

            act.wait_ge(loaded, 48)
            nc.scalar.activation(wfil[:, 0, :, :], wraw[:, :, :], ACT.Copy).then_inc(whi_done, 1)
            high(0, 0)
            with act.Fori(0, NP - 1) as it:
                high(it, 1)
                evac(it, 0)
                high(it + 1, 0)
                evac(it, 1)
            high(NP - 1, 1)
            evac(NP - 1, 0)
            evac(NP - 1, 1)


class Dft:

    def __init__(self, s):
        self.gen = s.sb("dft", [P, 3, 2, P], F32R)
        self.fwd0 = s.sb("fwd0", [P, 4, 2, P], F32R)
        self.inv0 = s.sb("inv0", [P, 4, 2, P], F32R)

    def load(self, pool, t, sem):
        pool.dma_start(self.gen[:, :, :, :], t["t_dft"][:, :, :, :]).then_inc(sem, 16)
        pool.dma_start(self.fwd0[:, :, :, :], t["t_f0"][:, :, :, :]).then_inc(sem, 16)
        pool.dma_start(self.inv0[:, :, :, :], t["t_i0"][:, :, :, :]).then_inc(sem, 16)

    def passes(self, nc, out, hi, lo, inverse, first):
        if first:
            tabs = self.inv0 if inverse else self.fwd0
            pick = (0, 1, 2, 3)
        else:
            tabs = self.gen
            pick = (0, 1, 2, 0) if inverse else (0, 2, 1, 0)
        for o in range(2):
            for i in range(2):
                k = pick[2 * i + o]
                mm = mm3(nc, out[:, o, :], (tabs[:, k, 0, :], tabs[:, k, 1, :]),
                         (hi[:, i, :], lo[:, i, :]), i == 0, i == 1)
        return mm



def filter_stage2(nc, t, xf, kfreq):
    with Scope(nc, "fs2") as s:
        dft = Dft(s)
        a = [s.sb(f"a{b}", [P, 2, DH]) for b in range(2)]
        ahi = [s.sb(f"ahi{b}", [P, 2, DH], F32R) for b in range(2)]
        alo = [s.sb(f"alo{b}", [P, 2, DH], F32R) for b in range(2)]
        out = [s.sb(f"out{b}", [P, 2, DH]) for b in range(2)]
        ps = [s.ps(f"ps{b}", [P, 2, CH]) for b in range(2)]
        tabs_in = s.sem("tabs_in")
        a_in, hi_done, lo_done, mm_done, re_out, im_out, stored = (
            s.sems(n) for n in ("a_in", "hi_done", "lo_done", "mm_done", "re_out", "im_out", "stored"))
        block = s.block()
        UNITS = 2 * NPAIR

        @block.sync
        def _(sp):
            def load(n):
                b, it, o, q = n % 2, n // 2, n // NPAIR, n % NPAIR
                sp.wait_ge(lo_done[b], it)
                for i in range(2):
                    slot = 2 * q + i
                    sp.dma_start(a[b][:, i, :], xf[4 * slot:4 * slot + 4, o, :, :]).then_inc(a_in[b], 16)

            load(0)
            load(1)
            for n in range(UNITS):
                b, it = n % 2, n // 2
                if n + 2 < UNITS:
                    load(n + 2)
                sp.wait_ge(re_out[b], it + 1)
                sp.wait_ge(im_out[b], it + 1)
                sp.dma_start(kfreq[n // NPAIR, n % NPAIR, :, :, :], out[b][:, :, :]).then_inc(stored[b], 16)
            for b in range(2):
                sp.wait_ge(stored[b], 16 * NPAIR)

        @block.gpsimd
        def _(pool):
            dft.load(pool, t, tabs_in)
            pool.wait_ge(tabs_in, 48)

        @block.tensor
        def _(pe):
            def unit(it, b, first=False):
                pe.wait_ge(lo_done[b], it + 1)
                pe.wait_ge(re_out[b], it)
                pe.wait_ge(im_out[b], it)
                dft.passes(nc, ps[b], ahi[b], alo[b], False, first).then_inc(mm_done[b], 1)

            pe.wait_ge(tabs_in, 48)
            for o in range(2):
                unit(8 * o, 0, first=True)
                unit(8 * o, 1)
                with pe.Fori(8 * o + 1, 8 * o + 8) as it:
                    unit(it, 0)
                    unit(it, 1)

        @block.scalar
        def _(act):
            def high(it, b):
                act.wait_ge(a_in[b], 32 * it + 32)
                act.wait_ge(mm_done[b], it)
                nc.scalar.activation(ahi[b][:, :, :], a[b][:, :, :], ACT.Copy).then_inc(hi_done[b], 1)

            def evac(it, b):
                act.wait_ge(mm_done[b], it + 1)
                act.wait_ge(stored[b], 16 * it)
                nc.scalar.activation(out[b][:, 0, :], ps[b][:, 0, :], ACT.Copy).then_inc(re_out[b], 1)

            high(0, 0)
            with act.Fori(0, NPAIR - 1) as it:
                high(it, 1)
                evac(it, 0)
                high(it + 1, 0)
                evac(it, 1)
            high(NPAIR - 1, 1)
            evac(NPAIR - 1, 0)
            evac(NPAIR - 1, 1)

        @block.vector
        def _(dve):
            def low(it, b):
                dve.wait_ge(hi_done[b], it + 1)
                dve.wait_ge(mm_done[b], it)
                nc.vector.tensor_tensor(alo[b][:, :, :], a[b][:, :, :], f32(ahi[b][:, :, :]),
                                        ALU.subtract).then_inc(lo_done[b], 1)

            def evac(it, b):
                dve.wait_ge(mm_done[b], it + 1)
                dve.wait_ge(stored[b], 16 * it)
                nc.vector.tensor_copy(out[b][:, 1, :], ps[b][:, 1, :]).then_inc(im_out[b], 1)

            low(0, 0)
            with dve.Fori(0, NPAIR - 1) as it:
                low(it, 1)
                evac(it, 0)
                low(it + 1, 0)
                evac(it, 1)
            low(NPAIR - 1, 1)
            evac(NPAIR - 1, 0)
            evac(NPAIR - 1, 1)



def modulation(nc, t, scale1, shift, gate, gate_bias):
    with Scope(nc, "mod") as s:
        wa = [s.sb(f"wa{b}", [P, 3 * D]) for b in range(2)]
        acc = s.sb("acc", [P, 3 * D])
        c_in = s.sb("c_in", [P, KT])
        c_silu = s.sb("c_silu", [P, KT])
        b_cols = s.sb("b_cols", [P, 16])
        b_gate = s.sb("b_gate", [1, D])
        b_out = s.sb("b_out", [P, D])
        ones = s.sb("ones", [P, P])
        ps_cols = s.ps("ps_cols", [P, 16])
        ps_gate = s.ps("ps_gate", [P, 2, CH])
        w_in = s.sems("w_in")
        loaded, silu_done, ones_set, acc_done, mm_done, cols_done, gate_done, prod_done = (
            s.sem(n) for n in ("loaded", "silu_done", "ones_set", "acc_done", "mm_done", "cols_done",
                               "gate_done", "prod_done"))
        block = s.block()

        @block.sync
        def _(sp):
            with nc.allow_non_contiguous_dma(reason="columns of small vectors"):
                sp.dma_start(c_in[:, :], t["c"].rearrange("o (k p) -> p (o k)", p=P)).then_inc(loaded, 16)
                sp.dma_start(b_cols[:, :], t["b_ada"][0, 0:2 * D].rearrange("(k p) -> p k", p=P)).then_inc(loaded, 16)
            sp.dma_start(b_gate[:, :], t["b_ada"][:, 2 * D:3 * D]).then_inc(loaded, 16)
            sp.dma_start(b_out[:, :], t["b_out"][0, :].partition_broadcast(P)).then_inc(loaded, 16)
            for k in range(KT):
                if k >= 2:
                    sp.wait_ge(acc_done, k - 1)
                sp.dma_start(wa[k % 2][:, :], t["w_ada"][0, k * P:(k + 1) * P, :]).then_inc(w_in[k % 2], 16)

        @block.gpsimd
        def _(pool):
            nc.gpsimd.memset(ones[:, :], 1.0).then_inc(ones_set, 1)

        @block.scalar
        def _(act):
            act.wait_ge(loaded, 64)
            nc.scalar.activation(c_silu[:, :], c_in[:, :], ACT.Silu).then_inc(silu_done, 1)
            act.wait_ge(mm_done, 1)
            nc.scalar.activation(gate[:, :], ps_gate[:, :, :].rearrange("p a b -> p (a b)"),
                                 ACT.Copy).then_inc(gate_done, 1)

        @block.vector
        def _(dve):
            dve.wait_ge(silu_done, 1)
            for k in range(KT):
                dve.wait_ge(w_in[k % 2], 16 * (k // 2) + 16)
                if k == 0:
                    nc.vector.tensor_scalar(acc[:, :], wa[0][:, :], c_silu[:, 0:1], None,
                                            ALU.mult).then_inc(acc_done, 1)
                else:
                    dve.wait_ge(acc_done, k)
                    nc.vector.scalar_tensor_tensor(out=acc[:, :], in0=wa[k % 2][:, :], scalar=c_silu[:, k:k + 1],
                                                   in1=acc[:, :], op0=ALU.mult, op1=ALU.add).then_inc(acc_done, 1)
            dve.wait_ge(mm_done, 1)
            nc.vector.tensor_tensor(shift[:, :], ps_cols[:, 0:8], b_cols[:, 0:8], ALU.add)
            nc.vector.scalar_tensor_tensor(out=scale1[:, :], in0=ps_cols[:, 8:16], scalar=1.0, in1=b_cols[:, 8:16],
                                           op0=ALU.add, op1=ALU.add).then_inc(cols_done, 1)
            dve.wait_ge(gate_done, 1)
            nc.vector.tensor_tensor(gate_bias[:, :], b_out[:, :], gate[:, :], ALU.mult).then_inc(prod_done, 1)
            dve.wait_ge(prod_done, 1)

        @block.tensor
        def _(pe):
            pe.wait_ge(ones_set, 1)
            pe.wait_ge(acc_done, KT)
            pe.wait_ge(loaded, 64)
            for j in range(16):
                nc.tensor.matmul(ps_cols[:, j:j + 1], acc[:, j * P:(j + 1) * P], ones[:, 0:1], start=True, stop=True,
                                 skip_group_check=True)
            for h in range(2):
                nc.tensor.matmul(ps_gate[:, h, :], ones[:, :], acc[:, 2 * D + h * CH:2 * D + (h + 1) * CH],
                                 start=True, stop=False)
                mm = nc.tensor.matmul(ps_gate[:, h, :], ones[0:1, :], b_gate[:, h * CH:(h + 1) * CH],
                                      start=False, stop=True)
            mm.then_inc(mm_done, 1)



def transpose_input(nc, t, scale1, shift, uhi, ulo, eye):
    with Scope(nc, "tin") as s:
        xs = [s.sb(f"xs{b}", [P, 4, D]) for b in range(2)]
        ut = [s.sb(f"ut{j}", [P, CH]) for j in range(4)]
        ps = [s.ps(f"ps{j}", [P, CH]) for j in range(4)]
        eye_in = s.sem("eye_in")
        x_in = s.sems("x_in")
        tr_done, hi_done, u_done, lo_done = (s.sems(n, 4) for n in ("tr_done", "hi_done", "u_done", "lo_done"))
        block = s.block()

        @block.sync
        def _(sp):
            sp.dma_start(eye[:, :], t["t_eye"][:, :]).then_inc(eye_in, 16)
            for tc in range(4):
                if tc >= 2:
                    for j in range(4):
                        sp.wait_ge(tr_done[j], 2 * (tc - 1))
                sp.dma_start(xs[tc % 2][:, :, :],
                             t["x"][0, tc * CH:(tc + 1) * CH, :].rearrange("(j p) d -> p j d", p=P)
                             ).then_inc(x_in[tc % 2], 16)

        @block.tensor
        def _(pe):
            pe.wait_ge(eye_in, 16)
            with pe.Fori(0, 2) as it:
                for b in range(2):
                    pe.wait_ge(x_in[b], 16 * it + 16)
                    for k in range(KT):
                        j = k % 4
                        use = 4 * it + 2 * b + k // 4
                        pe.wait_ge(u_done[j], use)
                        for i in range(4):
                            mm = nc.tensor.transpose(ps[j][:, i * P:(i + 1) * P], xs[b][:, i, k * P:(k + 1) * P],
                                                     eye[:, :])
                        mm.then_inc(tr_done[j], 1)

        @block.scalar
        def _(act):
            with act.Fori(0, 4) as tc:
                for k in range(KT):
                    j = k % 4
                    act.wait_ge(u_done[j], 2 * tc + k // 4 + 1)
                    plain(act, eye_in)
                    nc.scalar.activation(uhi[:, k, bass.ds(tc * CH, CH)], ut[j][:, :], ACT.Copy).then_inc(hi_done[j], 1)

        @block.vector
        def _(dve):
            with dve.Fori(0, 4) as tc:
                for k in range(KT + 1):
                    if k < KT:
                        j, use = k % 4, 2 * tc + k // 4
                        dve.wait_ge(tr_done[j], use + 1)
                        dve.wait_ge(lo_done[j], use)
                        nc.vector.tensor_scalar(ut[j][:, :], ps[j][:, :], scale1[:, k:k + 1], shift[:, k:k + 1],
                                                ALU.mult, ALU.add).then_inc(u_done[j], 1)
                    if k:
                        j, use = (k - 1) % 4, 2 * tc + (k - 1) // 4
                        dve.wait_ge(hi_done[j], use + 1)
                        nc.vector.tensor_tensor(ulo[:, k - 1, bass.ds(tc * CH, CH)], ut[j][:, :],
                                                f32(uhi[:, k - 1, bass.ds(tc * CH, CH)]),
                                                ALU.subtract).then_inc(lo_done[j], 1)



def project(nc, t, uhi, ulo, eye, vx, g2, yp):
    with Scope(nc, "prj") as s:
        ws = [s.sb(f"ws{b}", [P, KT, P]) for b in range(2)]
        whi = [s.sb(f"whi{b}", [P, KT, P], F32R) for b in range(2)]
        wlo = [s.sb(f"wlo{b}", [P, KT, P], F32R) for b in range(2)]
        W = L + 2 * PAD
        row = s.sb("row", [P, W])
        cv = [s.sb(f"cv{b}", [P, W]) for b in range(2)]
        st = s.sb("st", [P, GS, P])
        phl = [s.sb(f"phl{b}", [P, 2, CH], F32R) for b in range(2)]
        b_in = s.sb("b_in", [P, PROJ // P])
        bcol = s.sb("bcol", [P, 2])
        cw = s.sb("cw", [P, 3, 12])
        cb = s.sb("cb", [P, 12])
        pw = s.sb("pw", [P, 4, P])
        pwhl = s.sb("pwhl", [P, 2, 4, P], F32R)
        pscale = s.sb("pscale", [P, 4])
        edge = s.sb("edge", [P, 4, 2, PAD])
        pp = [s.ps(f"pp{c}", [P, CH]) for c in range(4)]
        px = [s.ps(f"px{c}", [P, CH]) for c in range(4)]
        consts, pad_set, pwhi_done, pwlo_done = (s.sem(n) for n in ("consts", "pad_set", "pwhi_done", "pwlo_done"))
        w_in, whi_done, wlo_done, conv_step, conv_done, prj_last, bcol_set = (
            s.sems(n) for n in ("w_in", "whi_done", "wlo_done", "conv_step", "conv_done", "prj_last", "bcol_set"))
        prj_done, bank_read, tr_done, tr_read = (s.sems(n, 4) for n in ("prj_done", "bank_read", "tr_done", "tr_read"))
        st_stored, g2_done, g2_stored, pool_step, phi_done, plo_done, mix_done, yp_part, yp_stored = (
            s.sem(n) for n in ("st_stored", "g2_done", "g2_stored", "pool_step",
                               "phi_done", "plo_done", "mix_done", "yp_part", "yp_stored"))
        block = s.block()
        wsrc = t["w_in"][0, :, :].rearrange("(k p) n -> p k n", p=P)
        stf = st[:, :, :].rearrange("p g c -> p (g c)")

        @block.sync
        def _(sp):
            def load(it, b, tile):
                sp.wait_ge(wlo_done[b], it)
                sp.dma_start(ws[b][:, :, :], wsrc[:, :, bass.ds(tile * P, P)]).then_inc(w_in[b], 16)

            def store_t(n):
                for j in range(4):
                    sp.wait_ge(tr_read[j], n + 1)
                sp.dma_start(vx[:, :, bass.ds(n * P, P)], st[:, :, :]).then_inc(st_stored, 16)

            with nc.allow_non_contiguous_dma(reason="columns of small vectors"):
                sp.dma_start(b_in[:, :], t["b_in"][0, :].rearrange("(k p) -> p k", p=P)).then_inc(consts, 16)
                for j in range(3):
                    sp.dma_start(cw[:, j, :], t["conv_w"][0, j, :].rearrange("(k p) -> p k", p=P)).then_inc(consts, 16)
                sp.dma_start(cb[:, :], t["conv_b"][0, :].rearrange("(k p) -> p k", p=P)).then_inc(consts, 16)
                sp.dma_start(pscale[:, :], t["pool_scale"][0, :].rearrange("(k p) -> p k", p=P)).then_inc(consts, 16)
            sp.dma_start(pw[:, :, :], t["pool_w"][0, :, :, :].rearrange("g c d -> c g d")).then_inc(consts, 16)
            sp.dma_start(edge[:, :, :, :], t["t_edge"].partition_broadcast(P)).then_inc(consts, 16)
            load(0, 0, 0)
            load(0, 1, 1)
            with sp.Fori(0, 3) as it:
                for b in range(2):
                    load(it + 1, b, 2 * it + 2 + b)
                    store_t(2 * it + b)
            for b in range(2):
                load(4, b, 8 + 4 * b)
                store_t(6 + b)
            with sp.Fori(0, 3) as i:
                for b in range(2):
                    load(i + 5, b, i + 9 + 4 * b)
                sp.wait_ge(g2_done, i + 1)
                sp.dma_start(g2[i, :, :], cv[1][:, 0:L]).then_inc(g2_stored, 16)
            for b in range(2):
                load(8, b, 16 + 4 * b)
            sp.wait_ge(g2_done, 4)
            sp.dma_start(g2[3, :, :], cv[1][:, 0:L]).then_inc(g2_stored, 16)
            for i in range(4):
                if i < 3:
                    for b in range(2):
                        load(i + 9, b, i + 17 + 4 * b)
                sp.wait_ge(yp_part, 4 * i + 4)
                sp.dma_start(yp[i, :, :], row[:, PAD:PAD + L]).then_inc(yp_stored, 16)
            sp.wait_ge(g2_stored, 64)
            sp.wait_ge(yp_stored, 64)
            sp.wait_ge(st_stored, 128)

        @block.gpsimd
        def _(pool):
            nc.gpsimd.memset(row[:, 0:PAD], 0.0).then_inc(pad_set, 1)
            pool.wait_ge(pad_set, 1)
            nc.gpsimd.memset(row[:, PAD + L:W], 0.0).then_inc(pad_set, 1)
            for it in range(12):
                for b in range(2):
                    pool.wait_ge(w_in[b], 16 * it + 16)
                    pool.wait_ge(prj_last[b], it)
                    nc.gpsimd.tensor_copy(whi[b][:, :, :], ws[b][:, :, :]).then_inc(whi_done[b], 1)
                    pool.wait_ge(whi_done[b], it + 1)
                    nc.gpsimd.tensor_tensor(wlo[b][:, :, :], ws[b][:, :, :], f32(whi[b][:, :, :]),
                                            ALU.subtract).then_inc(wlo_done[b], 1)

        @block.tensor
        def _(pe):
            def proj(it, b):
                pe.wait_ge(wlo_done[b], it + 1)
                for c in range(4):
                    pe.wait_ge(bank_read[c], 2 * it + b)
                    for k in range(KT):
                        mm = mm3(nc, pp[c][:, :], (whi[b][:, k, :], wlo[b][:, k, :]),
                                 (uhi[:, k, c * CH:(c + 1) * CH], ulo[:, k, c * CH:(c + 1) * CH]), k == 0, k == KT - 1)
                    mm.then_inc(prj_done[c] if c < 3 else prj_last[b], 1)

            def turn(it, b):
                pe.wait_ge(conv_done[b], it + 1)
                src = cv[b][:, 0:L].rearrange("p (c g) -> p g c", g=GS)
                for j in range(4):
                    pe.wait_ge(tr_read[j], 2 * it + b)
                    for i in range(4):
                        mm = nc.tensor.transpose(px[j][:, i * P:(i + 1) * P], src[:, 4 * j + i, :], eye[:, :])
                    mm.then_inc(tr_done[j], 1)

            proj(0, 0)
            with pe.Fori(0, 3) as it:
                proj(it, 1)
                turn(it, 0)
                proj(it + 1, 0)
                turn(it, 1)
            proj(3, 1)
            turn(3, 0)
            turn(3, 1)
            with pe.Fori(4, 8) as it:
                proj(it, 0)
                proj(it, 1)
            pe.wait_ge(pwlo_done, 1)
            for i in range(4):
                proj(8 + i, 0)
                proj(8 + i, 1)
                for c in range(4):
                    pe.wait_ge(plo_done, 4 * i + c + 1)
                    if i:
                        pe.wait_ge(yp_part, 4 * (i - 1) + c + 1)
                    mm3(nc, px[c][:, :], (pwhl[:, 0, i, :], pwhl[:, 1, i, :]),
                        (phl[c % 2][:, 0, :], phl[c % 2][:, 1, :]), True, True).then_inc(mix_done, 1)

        @block.scalar
        def _(act):
            def projected(it, b, c):
                if c < 3:
                    act.wait_ge(prj_done[c], 2 * it + b + 1)
                else:
                    act.wait_ge(prj_last[b], it + 1)

            def pick_bias(it, b, tile):
                nc.scalar.activation(bcol[:, b:b + 1], b_in[:, bass.ds(tile, 1)], ACT.Copy).then_inc(bcol_set[b], 1)
                act.wait_ge(bcol_set[b], it + 1)

            def bias_row(it, b):
                for c in range(4):
                    projected(it, b, c)
                    nc.scalar.activation(row[:, PAD + c * CH:PAD + (c + 1) * CH], pp[c][:, :], ACT.Identity,
                                         bias=bcol[:, b:b + 1]).then_inc(bank_read[c], 1)

            def gate_row(it, b):
                for c in range(4):
                    projected(it, b, c)
                    nc.scalar.activation(stf[:, c * CH:(c + 1) * CH], pp[c][:, :], ACT.Silu,
                                         bias=bcol[:, b:b + 1]).then_inc(bank_read[c], 1)

            def store_turned(it, b):
                act.wait_ge(st_stored, 32 * it + 16 * b)
                for j in range(4):
                    act.wait_ge(tr_done[j], 2 * it + b + 1)
                    nc.scalar.activation(st[:, 4 * j:4 * j + 4, :], px[j][:, :], ACT.Copy).then_inc(tr_read[j], 1)

            act.wait_ge(consts, 8 * 16)
            act.wait_ge(pad_set, 2)
            nc.scalar.activation(pwhl[:, 0, :, :], pw[:, :, :], ACT.Copy).then_inc(pwhi_done, 1)
            pick_bias(0, 0, 0)
            bias_row(0, 0)
            with act.Fori(0, 3) as it:
                pick_bias(it, 1, 2 * it + 1)
                act.wait_ge(conv_done[0], it + 1)
                bias_row(it, 1)
                store_turned(it, 0)
                pick_bias(it + 1, 0, 2 * it + 2)
                act.wait_ge(conv_done[1], it + 1)
                bias_row(it + 1, 0)
                store_turned(it, 1)
            pick_bias(3, 1, 7)
            act.wait_ge(conv_done[0], 4)
            bias_row(3, 1)
            store_turned(3, 0)
            store_turned(3, 1)
            act.wait_ge(conv_done[1], 4)
            act.wait_ge(st_stored, 128)
            with act.Fori(0, 4) as i:
                pick_bias(i + 4, 0, i + 8)
                act.wait_ge(g2_done, i)
                bias_row(i + 4, 0)
                pick_bias(i + 4, 1, i + 12)
                gate_row(i + 4, 1)
            for i in range(4):
                pick_bias(i + 8, 0, i + 16)
                if i == 0:
                    act.wait_ge(g2_done, 4)
                else:
                    act.wait_ge(yp_stored, 16 * i)
                bias_row(i + 8, 0)
                pick_bias(i + 8, 1, i + 20)
                gate_row(i + 8, 1)
                pl = cv[i % 2]
                act.wait_ge(pool_step, POOL_STEPS[i])
                for c in range(4):
                    if c >= 2 or i:
                        act.wait_ge(mix_done, 4 * i + c - 1)
                    nc.scalar.activation(phl[c % 2][:, 0, :], pl[:, c * CH:(c + 1) * CH], ACT.Copy).then_inc(phi_done, 1)

        @block.vector
        def _(dve):
            def conv(it, b, n, tile, dst):
                for c in range(4):
                    dve.wait_ge(bank_read[c], n + 1)
                nc.vector.tensor_scalar(dst[:, 0:L], row[:, PAD - 1:PAD - 1 + L], cw[:, 0, bass.ds(tile, 1)],
                                        cb[:, bass.ds(tile, 1)], ALU.mult, ALU.add).then_inc(conv_step[b], 1)
                dve.wait_ge(conv_step[b], 2 * it + 1)
                nc.vector.scalar_tensor_tensor(out=dst[:, 0:L], in0=row[:, PAD:PAD + L], scalar=cw[:, 1, bass.ds(tile, 1)],
                                               in1=dst[:, 0:L], op0=ALU.mult, op1=ALU.add).then_inc(conv_step[b], 1)
                dve.wait_ge(conv_step[b], 2 * it + 2)
                nc.vector.scalar_tensor_tensor(out=dst[:, 0:L], in0=row[:, PAD + 1:PAD + 1 + L],
                                               scalar=cw[:, 2, bass.ds(tile, 1)], in1=dst[:, 0:L],
                                               op0=ALU.mult, op1=ALU.add).then_inc(conv_done[b], 1)

            dve.wait_ge(pwhi_done, 1)
            nc.vector.tensor_tensor(pwhl[:, 1, :, :], pw[:, :, :], f32(pwhl[:, 0, :, :]), ALU.subtract).then_inc(pwlo_done, 1)
            with dve.Fori(0, 4) as it:
                for b in range(2):
                    for j in range(4):
                        dve.wait_ge(tr_done[j], 2 * it)
                    conv(it, b, 2 * it + b, 2 * it + b, cv[b])
            for j in range(4):
                dve.wait_ge(tr_done[j], 8)
            with dve.Fori(0, 4) as i:
                conv(i + 4, 0, 2 * i + 8, i + 8, cv[0])
                dve.wait_ge(conv_done[0], i + 5)
                for c in range(4):
                    dve.wait_ge(bank_read[c], 2 * i + 10)
                dve.wait_ge(g2_stored, 16 * i)
                nc.vector.tensor_tensor(cv[1][:, 0:L], cv[0][:, 0:L], stf, ALU.mult).then_inc(g2_done, 1)
            dve.wait_ge(g2_stored, 64)
            step = 0
            for i, win in enumerate(WINDOWS):
                h = win // 2
                for c in range(4):
                    dve.wait_ge(bank_read[c], 2 * i + 17)
                dve.wait_ge(plo_done, 4 * i)
                src, n, k = row, 1, 0
                bufs = (cv[i % 2], cv[1 - i % 2])
                levels = win.bit_length() - 1
                lo_edge = PAD - h
                while n < win:
                    dst = bufs[(levels - k) % 2]
                    width = L + win - 2 * n
                    dve.wait_ge(pool_step, step)
                    nc.vector.tensor_tensor(dst[:, lo_edge:lo_edge + width], src[:, lo_edge:lo_edge + width],
                                            src[:, lo_edge + n:lo_edge + n + width], ALU.add).then_inc(pool_step, 1)
                    step += 1
                    src, n, k = dst, 2 * n, k + 1
                dve.wait_ge(pool_step, step)
                nc.vector.tensor_tensor(src[:, lo_edge:lo_edge + h], src[:, lo_edge:lo_edge + h],
                                        edge[:, i, 0, 0:h], ALU.mult).then_inc(pool_step, 1)
                step += 1
                if h > 1:
                    e = lo_edge + L
                    nc.vector.tensor_tensor(src[:, e - h + 1:e], src[:, e - h + 1:e],
                                            edge[:, i, 1, PAD - h + 1:PAD], ALU.mult).then_inc(pool_step, 1)
                    step += 1
                dve.wait_ge(pool_step, step)
                nc.vector.scalar_tensor_tensor(out=bufs[0][:, 0:L], in0=src[:, lo_edge:lo_edge + L], scalar=1.0 / win,
                                               in1=row[:, PAD:PAD + L], op0=ALU.mult, op1=ALU.subtract
                                               ).then_inc(pool_step, 1)
                step += 1
                assert step == POOL_STEPS[i]
                for c in range(4):
                    dve.wait_ge(phi_done, 4 * i + c + 1)
                    nc.vector.tensor_tensor(phl[c % 2][:, 1, :], bufs[0][:, c * CH:(c + 1) * CH],
                                            f32(phl[c % 2][:, 0, :]), ALU.subtract).then_inc(plo_done, 1)
                for c in range(4):
                    dve.wait_ge(mix_done, 4 * i + c + 1)
                    dve.wait_ge(bank_read[c], 18 + 2 * i)
                    nc.vector.scalar_tensor_tensor(out=row[:, PAD + c * CH:PAD + (c + 1) * CH], in0=px[c][:, :],
                                                   scalar=pscale[:, i:i + 1], in1=stf[:, c * CH:(c + 1) * CH],
                                                   op0=ALU.mult, op1=ALU.mult).then_inc(yp_part, 1)



def signal_stage1(nc, t, vx, x):
    with Scope(nc, "ss1") as s:
        z = [s.sb(f"z{b}", [P, DH]) for b in range(2)]
        zhi = [s.sb(f"zhi{b}", [P, DH], F32R) for b in range(2)]
        zlo = [s.sb(f"zlo{b}", [P, DH], F32R) for b in range(2)]
        tab = [s.sb(f"tab{b}", [P, 2, 2, P], F32R) for b in range(2)]
        ps = [s.ps(f"ps{b}", [P, 2, CH]) for b in range(2)]
        z_in, tab_in, hi_done, lo_done, mm_done, out0, out1 = (
            s.sems(n) for n in ("z_in", "tab_in", "hi_done", "lo_done", "mm_done", "out0", "out1"))
        block = s.block()
        NP = GS // 2

        @block.sync
        def _(sp):
            with sp.Fori(0, NP) as it:
                for b in range(2):
                    sp.wait_ge(lo_done[b], it)
                    sp.dma_start(z[b][:, :], vx[:, 2 * it + b, 0:DH]).then_inc(z_in[b], 16)

        @block.gpsimd
        def _(pool):
            for it in range(NP):
                for b in range(2):
                    pool.wait_ge(mm_done[b], it)
                    pool.dma_start(tab[b][:, :, :, :], t["t_w1s"][2 * it + b, :, :, :, :]).then_inc(tab_in[b], 16)

        @block.tensor
        def _(pe):
            with pe.Fori(0, NP) as it:
                for b in range(2):
                    pe.wait_ge(tab_in[b], 16 * it + 16)
                    pe.wait_ge(lo_done[b], it + 1)
                    pe.wait_ge(out0[b], it)
                    pe.wait_ge(out1[b], it)
                    for m in range(2):
                        mm = mm3(nc, ps[b][:, m, :], (tab[b][:, m, 0, :], tab[b][:, m, 1, :]),
                                 (zhi[b][:, :], zlo[b][:, :]), True, True)
                    mm.then_inc(mm_done[b], 1)

        @block.scalar
        def _(act):
            def high(it, b):
                act.wait_ge(z_in[b], 16 * it + 16)
                act.wait_ge(mm_done[b], it)
                nc.scalar.activation(zhi[b][:, :], z[b][:, :], ACT.Copy).then_inc(hi_done[b], 1)

            def evac(it, b):
                act.wait_ge(mm_done[b], it + 1)
                plain(act, tab_in[b])
                nc.scalar.activation(x[:, 0, 2 * it + b, :], ps[b][:, 0, :], ACT.Copy).then_inc(out0[b], 1)

            high(0, 0)
            with act.Fori(0, NP - 1) as it:
                high(it, 1)
                evac(it, 0)
                high(it + 1, 0)
                evac(it, 1)
            high(NP - 1, 1)
            evac(NP - 1, 0)
            evac(NP - 1, 1)

        @block.vector
        def _(dve):
            def low(it, b):
                dve.wait_ge(hi_done[b], it + 1)
                dve.wait_ge(mm_done[b], it)
                nc.vector.tensor_tensor(zlo[b][:, :], z[b][:, :], f32(zhi[b][:, :]),
                                        ALU.subtract).then_inc(lo_done[b], 1)

            def evac(it, b):
                dve.wait_ge(mm_done[b], it + 1)
                nc.vector.tensor_copy(x[:, 1, 2 * it + b, :], ps[b][:, 1, :]).then_inc(out1[b], 1)

            low(0, 0)
            with dve.Fori(0, NP - 1) as it:
                low(it, 1)
                evac(it, 0)
                low(it + 1, 0)
                evac(it, 1)
            low(NP - 1, 1)
            evac(NP - 1, 0)
            evac(NP - 1, 1)


def spectrum_product(nc, t, tag, x, kfreq):
    with Scope(nc, tag) as s:
        dft = Dft(s)
        a = [s.sb(f"a{b}", [P, 2, DH]) for b in range(2)]
        ahi = [s.sb(f"ahi{b}", [P, 2, DH], F32R) for b in range(2)]
        alo = [s.sb(f"alo{b}", [P, 2, DH], F32R) for b in range(2)]
        kf = [s.sb(f"kf{b}", [P, 2, DH]) for b in range(2)]
        by_re = s.sb("by_re", [P, 2, DH])
        by_im = s.sb("by_im", [P, 2, DH])
        y = [s.sb(f"y{b}", [P, 2, DH]) for b in range(2)]
        yhi = [s.sb(f"yhi{b}", [P, 2, DH], F32R) for b in range(2)]
        ylo = [s.sb(f"ylo{b}", [P, 2, DH], F32R) for b in range(2)]
        out = [s.sb(f"out{b}", [P, 2, DH]) for b in range(2)]
        u_ps = [s.ps(f"u{b}", [P, 2, CH]) for b in range(2)]
        b_ps = [s.ps(f"b{b}", [P, 2, CH]) for b in range(2)]
        tabs_in, part = s.sem("tabs_in"), s.sem("part")
        a_in, k_in, ahi_done, alo_done, u_done, y_done, yhi_done, ylo_done, b_done, out_done, stored = (
            s.sems(n) for n in ("a_in", "k_in", "ahi_done", "alo_done", "u_done", "y_done", "yhi_done",
                                "ylo_done", "b_done", "out_done", "stored"))
        block = s.block()
        NP = NPAIR // 2

        def rows(q, i):
            slot = 2 * q + i
            r = slot % 16
            return x[8 * r:8 * r + 8, slot // 16, :, :]

        @block.sync
        def _(sp):
            def load(q):
                b, it = q % 2, q // 2
                sp.wait_ge(alo_done[b], it)
                for i in range(2):
                    sp.dma_start(a[b][:, i, :], rows(q, i)).then_inc(a_in[b], 16)
                sp.wait_ge(y_done[b], it)
                sp.dma_start(kf[b][:, :, :], kfreq[q, :, :, :]).then_inc(k_in[b], 16)

            def store(q):
                sp.wait_ge(out_done[q % 2], q // 2 + 1)
                for i in range(2):
                    sp.dma_start(rows(q, i), out[q % 2][:, i, :]).then_inc(stored[q % 2], 16)

            load(0)
            load(1)
            load(2)
            for q in range(NPAIR):
                if q + 3 < NPAIR:
                    load(q + 3)
                store(q)
            for b in range(2):
                sp.wait_ge(stored[b], 32 * NP)

        @block.gpsimd
        def _(pool):
            dft.load(pool, t, tabs_in)
            pool.wait_ge(tabs_in, 48)

        @block.tensor
        def _(pe):
            def fwd(it, b, first=False):
                pe.wait_ge(alo_done[b], it + 1)
                pe.wait_ge(y_done[b], it)
                dft.passes(nc, u_ps[b], ahi[b], alo[b], False, first).then_inc(u_done[b], 1)

            def inv(it, b, first=False):
                pe.wait_ge(ylo_done[b], it + 1)
                pe.wait_ge(out_done[b], it)
                dft.passes(nc, b_ps[b], yhi[b], ylo[b], True, first).then_inc(b_done[b], 1)

            pe.wait_ge(tabs_in, 48)
            fwd(0, 0, first=True)
            fwd(0, 1)
            inv(0, 0, first=True)
            fwd(1, 0)
            inv(0, 1)
            with pe.Fori(1, NP - 1) as it:
                fwd(it, 1)
                inv(it, 0)
                fwd(it + 1, 0)
                inv(it, 1)
            fwd(NP - 1, 1)
            inv(NP - 1, 0)
            inv(NP - 1, 1)

        @block.scalar
        def _(act):
            def ahigh(it, b):
                act.wait_ge(a_in[b], 32 * it + 32)
                act.wait_ge(u_done[b], it)
                nc.scalar.activation(ahi[b][:, :, :], a[b][:, :, :], ACT.Copy).then_inc(ahi_done[b], 1)

            def yhigh(it, b):
                act.wait_ge(y_done[b], it + 1)
                act.wait_ge(b_done[b], it)
                nc.scalar.activation(yhi[b][:, :, :], y[b][:, :, :], ACT.Copy).then_inc(yhi_done[b], 1)

            def evac(it, b):
                act.wait_ge(b_done[b], it + 1)
                act.wait_ge(stored[b], 32 * it)
                nc.scalar.activation(out[b][:, :, :], b_ps[b][:, :, :], ACT.Copy).then_inc(out_done[b], 1)

            ahigh(0, 0)
            ahigh(0, 1)
            ahigh(1, 0)
            yhigh(0, 0)
            ahigh(1, 1)
            evac(0, 0)
            yhigh(0, 1)
            with act.Fori(1, NP - 1) as it:
                ahigh(it + 1, 0)
                evac(it - 1, 1)
                yhigh(it, 0)
                ahigh(it + 1, 1)
                evac(it, 0)
                yhigh(it, 1)
            evac(NP - 2, 1)
            yhigh(NP - 1, 0)
            evac(NP - 1, 0)
            yhigh(NP - 1, 1)
            evac(NP - 1, 1)

        @block.vector
        def _(dve):
            def alow(it, b):
                dve.wait_ge(ahi_done[b], it + 1)
                dve.wait_ge(u_done[b], it)
                nc.vector.tensor_tensor(alo[b][:, :, :], a[b][:, :, :], f32(ahi[b][:, :, :]),
                                        ALU.subtract).then_inc(alo_done[b], 1)

            def ylow(it, b):
                dve.wait_ge(yhi_done[b], it + 1)
                dve.wait_ge(b_done[b], it)
                nc.vector.tensor_tensor(ylo[b][:, :, :], y[b][:, :, :], f32(yhi[b][:, :, :]),
                                        ALU.subtract).then_inc(ylo_done[b], 1)

            def product(it, b, first=False):
                n = 8 * it + 4 * b
                dve.wait_ge(u_done[b], it + 1)
                dve.wait_ge(k_in[b], 16 * it + 16)
                dve.wait_ge(part, n)
                nc.vector.tensor_tensor(by_re[:, :, :], u_ps[b][:, :, :],
                                        kf[b][:, 0:1, :].broadcast_to([P, 2, DH]), ALU.mult).then_inc(part, 1)
                nc.vector.tensor_tensor(by_im[:, :, :], u_ps[b][:, :, :],
                                        kf[b][:, 1:2, :].broadcast_to([P, 2, DH]), ALU.mult).then_inc(part, 1)
                dve.wait_ge(part, n + 2)
                dve.wait_ge(ylo_done[b], it)
                nc.vector.tensor_tensor(y[b][:, 0, :], by_re[:, 0, :], by_im[:, 1, :], ALU.subtract).then_inc(part, 1)
                last = nc.vector.tensor_tensor(y[b][:, 1, :], by_re[:, 1, :], by_im[:, 0, :], ALU.add)
                last.then_inc(part, 1)
                dve.wait_ge(part, n + 4)
                if first:
                    nc.vector.tensor_tensor(y[b][0:1, :, :], u_ps[b][0:1, :, :], kf[b][0:1, :, :],
                                            ALU.mult).then_inc(y_done[b], 1)
                else:
                    dve.sem_inc(y_done[b], 1)

            alow(0, 0)
            alow(0, 1)
            product(0, 0, first=True)
            alow(1, 0)
            ylow(0, 0)
            product(0, 1)
            alow(1, 1)
            ylow(0, 1)
            with dve.Fori(1, NP - 1) as it:
                for b in range(2):
                    product(it, b)
                    alow(it + 1, b)
                    ylow(it, b)
            for b in range(2):
                product(NP - 1, b)
                ylow(NP - 1, b)


def between_orders(nc, t, vx, x):
    with Scope(nc, "mid") as s:
        xhi = [s.sb(f"xhi{b}", [P, 2, DH], F32R) for b in range(2)]
        xlo = [s.sb(f"xlo{b}", [P, 2, DH], F32R) for b in range(2)]
        x1 = [s.sb(f"x1{b}", [P, DH]) for b in range(2)]
        z = [s.sb(f"z{b}", [P, DH]) for b in range(2)]
        zhi = [s.sb(f"zhi{b}", [P, DH], F32R) for b in range(2)]
        zlo = [s.sb(f"zlo{b}", [P, DH], F32R) for b in range(2)]
        itab = [s.sb(f"itab{b}", [P, 2, 2, P], F32R) for b in range(2)]
        ftab = [s.sb(f"ftab{b}", [P, 2, 2, P], F32R) for b in range(2)]
        z_ps = [s.ps(f"zps{b}", [P, CH]) for b in range(2)]
        s_ps = [s.ps(f"sps{b}", [P, 2, CH]) for b in range(2)]
        x1_in, itab_in, ftab_in, xhi_done, xlo_done, inv_done, z_done, zhi_done, zlo_done, fwd_done, out0, out1 = (
            s.sems(n) for n in ("x1_in", "itab_in", "ftab_in", "xhi_done", "xlo_done", "inv_done", "z_done",
                                "zhi_done", "zlo_done", "fwd_done", "out0", "out1"))
        block = s.block()
        NP = GS // 2

        @block.sync
        def _(sp):
            with sp.Fori(0, NP) as it:
                for b in range(2):
                    sp.wait_ge(z_done[b], it)
                    sp.dma_start(x1[b][:, :], vx[:, 2 * it + b, DH:2 * DH]).then_inc(x1_in[b], 16)

        @block.gpsimd
        def _(pool):
            for it in range(NP):
                for b in range(2):
                    pool.wait_ge(inv_done[b], it)
                    pool.dma_start(itab[b][:, :, :, :], t["t_iw1"][2 * it + b, :, :, :, :]).then_inc(itab_in[b], 16)
                    pool.wait_ge(fwd_done[b], it)
                    pool.dma_start(ftab[b][:, :, :, :], t["t_w1s"][2 * it + b, :, :, :, :]).then_inc(ftab_in[b], 16)

        @block.tensor
        def _(pe):
            def inv(it, b):
                pe.wait_ge(xlo_done[b], it + 1)
                pe.wait_ge(itab_in[b], 16 * it + 16)
                pe.wait_ge(z_done[b], it)
                for m in range(2):
                    mm = mm3(nc, z_ps[b][:, :], (itab[b][:, m, 0, :], itab[b][:, m, 1, :]),
                             (xhi[b][:, m, :], xlo[b][:, m, :]), m == 0, m == 1)
                mm.then_inc(inv_done[b], 1)

            def fwd(it, b):
                pe.wait_ge(zlo_done[b], it + 1)
                pe.wait_ge(ftab_in[b], 16 * it + 16)
                pe.wait_ge(out0[b], it)
                pe.wait_ge(out1[b], it)
                for m in range(2):
                    mm = mm3(nc, s_ps[b][:, m, :], (ftab[b][:, m, 0, :], ftab[b][:, m, 1, :]),
                             (zhi[b][:, :], zlo[b][:, :]), True, True)
                mm.then_inc(fwd_done[b], 1)

            inv(0, 0)
            with pe.Fori(0, NP - 1) as it:
                inv(it, 1)
                fwd(it, 0)
                inv(it + 1, 0)
                fwd(it, 1)
            inv(NP - 1, 1)
            fwd(NP - 1, 0)
            fwd(NP - 1, 1)

        @block.scalar
        def _(act):
            def xhigh(it, b):
                act.wait_ge(inv_done[b], it)
                plain(act, itab_in[b])
                nc.scalar.activation(xhi[b][:, :, :], x[:, :, 2 * it + b, :], ACT.Copy).then_inc(xhi_done[b], 1)

            def zhigh(it, b):
                act.wait_ge(z_done[b], it + 1)
                act.wait_ge(fwd_done[b], it)
                nc.scalar.activation(zhi[b][:, :], z[b][:, :], ACT.Copy).then_inc(zhi_done[b], 1)

            def evac(it, b):
                act.wait_ge(fwd_done[b], it + 1)
                plain(act, itab_in[b])
                nc.scalar.activation(x[:, 0, 2 * it + b, :], s_ps[b][:, 0, :], ACT.Copy).then_inc(out0[b], 1)

            xhigh(0, 0)
            xhigh(0, 1)
            xhigh(1, 0)
            zhigh(0, 0)
            xhigh(1, 1)
            evac(0, 0)
            zhigh(0, 1)
            with act.Fori(1, NP - 1) as it:
                xhigh(it + 1, 0)
                evac(it - 1, 1)
                zhigh(it, 0)
                xhigh(it + 1, 1)
                evac(it, 0)
                zhigh(it, 1)
            evac(NP - 2, 1)
            zhigh(NP - 1, 0)
            evac(NP - 1, 0)
            zhigh(NP - 1, 1)
            evac(NP - 1, 1)

        @block.vector
        def _(dve):
            def xlow(it, b):
                dve.wait_ge(xhi_done[b], it + 1)
                dve.wait_ge(inv_done[b], it)
                nc.vector.tensor_tensor(xlo[b][:, :, :], x[:, :, 2 * it + b, :], f32(xhi[b][:, :, :]),
                                        ALU.subtract).then_inc(xlo_done[b], 1)

            def gate(it, b):
                dve.wait_ge(inv_done[b], it + 1)
                dve.wait_ge(x1_in[b], 16 * it + 16)
                dve.wait_ge(zlo_done[b], it)
                nc.vector.tensor_tensor(z[b][:, :], z_ps[b][:, :], x1[b][:, :], ALU.mult).then_inc(z_done[b], 1)

            def zlow(it, b):
                dve.wait_ge(zhi_done[b], it + 1)
                dve.wait_ge(fwd_done[b], it)
                nc.vector.tensor_tensor(zlo[b][:, :], z[b][:, :], f32(zhi[b][:, :]),
                                        ALU.subtract).then_inc(zlo_done[b], 1)

            def evac(it, b):
                dve.wait_ge(fwd_done[b], it + 1)
                nc.vector.tensor_copy(x[:, 1, 2 * it + b, :], s_ps[b][:, 1, :]).then_inc(out1[b], 1)

            xlow(0, 0)
            xlow(0, 1)
            gate(0, 0)
            xlow(1, 0)
            zlow(0, 0)
            gate(0, 1)
            xlow(1, 1)
            evac(0, 0)
            zlow(0, 1)
            with dve.Fori(1, NP - 1) as it:
                gate(it, 0)
                xlow(it + 1, 0)
                evac(it - 1, 1)
                zlow(it, 0)
                gate(it, 1)
                xlow(it + 1, 1)
                evac(it, 0)
                zlow(it, 1)
            gate(NP - 1, 0)
            evac(NP - 2, 1)
            zlow(NP - 1, 0)
            gate(NP - 1, 1)
            evac(NP - 1, 0)
            zlow(NP - 1, 1)
            evac(NP - 1, 1)


def last_inverse(nc, t, x, g2, yp, y):
    with Scope(nc, "fin") as s:
        xhi = [s.sb(f"xhi{b}", [P, 2, DH], F32R) for b in range(2)]
        xlo = [s.sb(f"xlo{b}", [P, 2, DH], F32R) for b in range(2)]
        tab = [s.sb(f"tab{b}", [P, 2, 2, P], F32R) for b in range(2)]
        ps = [s.ps(f"ps{b}", [P, 4, P]) for b in range(2)]
        y_in = s.sem("y_in")
        tab_in, hi_done, lo_done, mm_done, y_done = (
            s.sems(n) for n in ("tab_in", "hi_done", "lo_done", "mm_done", "y_done"))
        block = s.block()
        NP = GS // 2
        yg = y[:, 0:4, :].rearrange("p k (c g) -> p k c g", g=GS)

        @block.sync
        def _(sp):
            sp.dma_start(y[:, 0:4, :], g2.rearrange("k p t -> p k t")).then_inc(y_in, 16)
            sp.dma_start(y[:, 4:8, :], yp.rearrange("k p t -> p k t")).then_inc(y_in, 16)
            sp.wait_ge(y_in, 32)

        @block.gpsimd
        def _(pool):
            for it in range(NP):
                for b in range(2):
                    pool.wait_ge(mm_done[b], it)
                    pool.dma_start(tab[b][:, :, :, :], t["t_iw1"][2 * it + b, :, :, :, :]).then_inc(tab_in[b], 16)

        @block.tensor
        def _(pe):
            with pe.Fori(0, NP) as it:
                for b in range(2):
                    pe.wait_ge(lo_done[b], it + 1)
                    pe.wait_ge(tab_in[b], 16 * it + 16)
                    pe.wait_ge(y_done[b], it)
                    for k in range(4):
                        cols = slice(k * P, (k + 1) * P)
                        for m in range(2):
                            mm = mm3(nc, ps[b][:, k, :], (xhi[b][:, m, cols], xlo[b][:, m, cols]),
                                     (tab[b][:, m, 0, :], tab[b][:, m, 1, :]), m == 0, m == 1)
                    mm.then_inc(mm_done[b], 1)

        @block.scalar
        def _(act):
            with act.Fori(0, NP) as it:
                for b in range(2):
                    act.wait_ge(mm_done[b], it)
                    plain(act, tab_in[b])
                    nc.scalar.activation(xhi[b][:, :, :], x[:, :, 2 * it + b, :], ACT.Copy).then_inc(hi_done[b], 1)

        @block.vector
        def _(dve):
            def low(it, b):
                dve.wait_ge(hi_done[b], it + 1)
                dve.wait_ge(mm_done[b], it)
                nc.vector.tensor_tensor(xlo[b][:, :, :], x[:, :, 2 * it + b, :], f32(xhi[b][:, :, :]),
                                        ALU.subtract).then_inc(lo_done[b], 1)

            def gate(it, b):
                dve.wait_ge(mm_done[b], it + 1)
                nc.vector.tensor_tensor(yg[:, :, :, 2 * it + b], ps[b][:, :, :], yg[:, :, :, 2 * it + b],
                                        ALU.mult).then_inc(y_done[b], 1)

            dve.wait_ge(y_in, 32)
            low(0, 0)
            with dve.Fori(0, NP - 1) as it:
                low(it, 1)
                gate(it, 0)
                low(it + 1, 0)
                gate(it, 1)
            low(NP - 1, 1)
            gate(NP - 1, 0)
            gate(NP - 1, 1)



def output_norm(nc, t, y, gate, gate_bias, out):
    with Scope(nc, "out") as s:
        wf = [s.sb(f"wf{b}", [P, D]) for b in range(2)]
        whl = s.sb("whl", [P, 2, KT, D], F32R)
        yhi = [s.sb(f"yhi{b}", [P, KT, P], F32R) for b in range(2)]
        ylo = [s.sb(f"ylo{b}", [P, KT, P], F32R) for b in range(2)]
        x = [s.sb(f"x{b}", [P, D]) for b in range(2)]
        res = wf
        o = [s.sb(f"o{b}", [P, D]) for b in range(2)]
        ln_g = s.sb("ln_g", [P, D])
        ln_b = s.sb("ln_b", [P, D])
        stats = [s.sb(f"stats{b}", [P, 2, 6]) for b in range(2)]
        mv = [s.sb(f"mv{b}", [P, 2]) for b in range(2)]
        sm = [s.sb(f"sm{b}", [P, 4]) for b in range(2)]
        eps = s.sb("eps", [P, 1])
        ps = [s.ps(f"ps{b}", [P, 2, CH]) for b in range(2)]
        consts, w_scaled, whi_done, wlo_done, eps_set = (
            s.sem(n) for n in ("consts", "w_scaled", "whi_done", "wlo_done", "eps_set"))
        w_in, x_in, hi_done, lo_done, mm_done, step, var_done, root_done, norm_done, scaled, o_done, stored = (
            s.sems(n) for n in ("w_in", "x_in", "hi_done", "lo_done", "mm_done", "step", "var_done",
                                "root_done", "norm_done", "scaled", "o_done", "stored"))
        block = s.block()
        NP = GS // 2

        @block.sync
        def _(sp):
            for k in range(KT):
                if k >= 2:
                    sp.wait_ge(wlo_done, k - 1)
                sp.dma_start(wf[k % 2][:, :], t["w_out"][0, k * P:(k + 1) * P, :]).then_inc(w_in[k % 2], 16)
            sp.dma_start(ln_g[:, :], t["ln_g"][0, :].partition_broadcast(P)).then_inc(consts, 16)
            sp.dma_start(ln_b[:, :], t["ln_b"][0, :].partition_broadcast(P)).then_inc(consts, 16)
            with sp.Fori(0, NP) as it:
                for b in range(2):
                    sp.wait_ge(norm_done[b], it)
                    sp.dma_start(x[b][:, :], t["x"][0, bass.ds((2 * it + b) * P, P), :]).then_inc(x_in[b], 16)

        @block.tensor
        def _(pe):
            with pe.Fori(0, NP) as it:
                for b in range(2):
                    pe.wait_ge(lo_done[b], it + 1)
                    pe.wait_ge(norm_done[b], it)
                    for h in range(2):
                        cols = slice(h * CH, (h + 1) * CH)
                        for k in range(KT):
                            mm = mm3(nc, ps[b][:, h, :], (yhi[b][:, k, :], ylo[b][:, k, :]),
                                     (whl[:, 0, k, cols], whl[:, 1, k, cols]), k == 0, k == KT - 1)
                    mm.then_inc(mm_done[b], 1)

        @block.scalar
        def _(act):
            for k in range(KT):
                act.wait_ge(w_scaled, k + 1)
                nc.scalar.activation(whl[:, 0, k, :], wf[k % 2][:, :], ACT.Copy).then_inc(whi_done, 1)

            def high(it, b):
                act.wait_ge(mm_done[b], it)
                plain(act, eps_set)
                nc.scalar.activation(yhi[b][:, :, :], y[:, :, bass.ds((2 * it + b) * P, P)],
                                     ACT.Copy).then_inc(hi_done[b], 1)

            def root(it, b):
                act.wait_ge(var_done[b], it + 1)
                nc.scalar.activation(sm[b][:, 0:1], mv[b][:, 1:2], ACT.Sqrt, bias=eps[:, 0:1]).then_inc(root_done[b], 1)

            def store(it, b):
                act.wait_ge(o_done[b], it + 1)
                act.dma_start(out[0, bass.ds((2 * it + b) * P, P), :], o[b][:, :]).then_inc(stored[b], 16)

            act.wait_ge(eps_set, 1)
            high(0, 0)
            high(0, 1)
            with act.Fori(0, NP - 1) as it:
                high(it + 1, 0)
                root(it, 0)
                store(it, 0)
                high(it + 1, 1)
                root(it, 1)
                store(it, 1)
            for b in range(2):
                root(NP - 1, b)
                store(NP - 1, b)
            for b in range(2):
                act.wait_ge(stored[b], 16 * NP)

        @block.gpsimd
        def _(pool):
            nc.gpsimd.memset(eps[:, :], LN_EPS).then_inc(eps_set, 1)
            pool.wait_ge(consts, 32)
            for it in range(NP):
                for b in range(2):
                    pool.wait_ge(norm_done[b], it + 1)
                    pool.wait_ge(stored[b], 16 * it)
                    nc.gpsimd.tensor_tensor(o[b][:, :], res[b][:, :], ln_g[:, :], ALU.mult).then_inc(scaled[b], 1)
                    pool.wait_ge(scaled[b], it + 1)
                    nc.gpsimd.tensor_tensor(o[b][:, :], o[b][:, :], ln_b[:, :], ALU.add).then_inc(o_done[b], 1)

        @block.vector
        def _(dve):
            for k in range(KT):
                dve.wait_ge(w_in[k % 2], 16 * (k // 2) + 16)
                nc.vector.tensor_tensor(wf[k % 2][:, :], wf[k % 2][:, :], gate[:, :], ALU.mult).then_inc(w_scaled, 1)
                dve.wait_ge(whi_done, k + 1)
                nc.vector.tensor_tensor(whl[:, 1, k, :], wf[k % 2][:, :], f32(whl[:, 0, k, :]),
                                        ALU.subtract).then_inc(wlo_done, 1)
            dve.wait_ge(wlo_done, KT)

            def low(it, b):
                dve.wait_ge(hi_done[b], it + 1)
                dve.wait_ge(mm_done[b], it)
                nc.vector.tensor_tensor(ylo[b][:, :, :], y[:, :, bass.ds((2 * it + b) * P, P)],
                                        f32(yhi[b][:, :, :]), ALU.subtract).then_inc(lo_done[b], 1)

            def norm(it, b):
                STEPS = 8
                n = STEPS * it
                done = [0]

                def then(ins):
                    ins.then_inc(step[b], 1)
                    done[0] += 1
                    dve.wait_ge(step[b], n + done[0])

                dve.wait_ge(mm_done[b], it + 1)
                dve.wait_ge(x_in[b], 16 * it + 16)
                dve.wait_ge(scaled[b], it)
                then(nc.vector.scalar_tensor_tensor(out=res[b][:, :], in0=x[b][:, :], scalar=ALPHA,
                                                    in1=ps[b][:, :, :].rearrange("p a b -> p (a b)"),
                                                    op0=ALU.mult, op1=ALU.add))
                then(nc.vector.tensor_tensor(res[b][:, :], res[b][:, :], gate_bias[:, :], ALU.add))
                for h in range(2):
                    ins = nc.vector.bn_stats(stats[b][:, h, :], res[b][:, h * CH:(h + 1) * CH])
                then(ins)
                nc.vector.memset(sm[b][:, 2:4], 0.0)
                nc.vector.bn_aggr(mv[b][:, :], stats[b][:, :, :].rearrange("p a b -> p (a b)")).then_inc(var_done[b], 1)
                dve.wait_ge(root_done[b], it + 1)
                then(nc.vector.reciprocal(sm[b][:, 1:2], sm[b][:, 0:1]))
                then(nc.vector.tensor_scalar(sm[b][:, 2:3], mv[b][:, 1:2], LN_EPS, sm[b][:, 1:2], ALU.add, ALU.mult))
                then(nc.vector.tensor_tensor(sm[b][:, 2:3], sm[b][:, 2:3], sm[b][:, 1:2], ALU.mult))
                then(nc.vector.tensor_scalar(sm[b][:, 2:3], sm[b][:, 2:3], -0.5, 1.5, ALU.mult, ALU.add))
                then(nc.vector.tensor_tensor(sm[b][:, 3:4], sm[b][:, 2:3], sm[b][:, 1:2], ALU.mult))
                assert done[0] == STEPS
                nc.vector.tensor_scalar(res[b][:, :], res[b][:, :], mv[b][:, 0:1], sm[b][:, 3:4],
                                        ALU.subtract, ALU.mult).then_inc(norm_done[b], 1)

            low(0, 0)
            low(0, 1)
            with dve.Fori(0, NP - 1) as it:
                for b in range(2):
                    low(it + 1, b)
                    norm(it, b)
            for b in range(2):
                norm(NP - 1, b)


def encoder_layer(nc, t, out):
    def scratch(name, shape):
        return nc.dram_tensor(name, shape, F32, kind="Internal").ap()

    kfreq = scratch("kfreq", [2, NPAIR, P, 2, DH])
    vx = scratch("vx", [P, GS, 2 * DH])
    g2 = scratch("g2", [4, P, L])
    yp = scratch("yp", [4, P, L])

    with Scope(nc, "flt") as s:
        xf = s.sb("xf", [P, 2, GF, DH])
        with Scope(nc, "hid") as h:
            hfil = h.sb("hfil", [P, 2, P, GF], F32R)
            filter_network(nc, t, hfil)
            filter_stage1(nc, t, hfil, xf)
        filter_stage2(nc, t, xf, kfreq)
    with Scope(nc, "all") as s:
        gate = s.sb("gate", [P, D])
        gate_bias = s.sb("gate_bias", [P, D])
        scale1 = s.sb("scale1", [P, KT])
        shift = s.sb("shift", [P, KT])
        modulation(nc, t, scale1, shift, gate, gate_bias)
        with Scope(nc, "u") as u:
            eye = u.sb("eye", [P, P])
            uhi = u.sb("uhi", [P, KT, L], F32R)
            ulo = u.sb("ulo", [P, KT, L], F32R)
            transpose_input(nc, t, scale1, shift, uhi, ulo, eye)
            project(nc, t, uhi, ulo, eye, vx, g2, yp)
        x_scope = Scope(nc, "x")
        x = x_scope.sb("x", [P, 2, GS, DH])
        signal_stage1(nc, t, vx, x)
        spectrum_product(nc, t, "sp0", x, kfreq[0])
        between_orders(nc, t, vx, x)
        spectrum_product(nc, t, "sp1", x, kfreq[1])
        with nc.sbuf_tensor("y", [P, KT, L], F32, side="right") as y:
            last_inverse(nc, t, x, g2, yp, y)
            x_scope.ctx.close()
            output_norm(nc, t, y, gate, gate_bias, out)


_INS = ["x", "c", "w_ada", "b_ada", "w_in", "b_in", "conv_w", "conv_b", "filt_w1", "filt_b1", "filt_w_inner",
        "filt_b_inner", "filt_w_out", "filt_freq", "hyena_bias", "pool_w", "pool_scale", "w_out", "b_out",
        "ln_g", "ln_b"]


def kernel(**inputs):
    import numpy as _np
    import concourse.bacc as _bacc
    from concourse import mybir as _mybir
    from concourse.bass_utils import run_bass_kernel_spmd as _run

    nc = _bacc.Bacc("TRN2", target_bir_lowering=False, num_devices=1)
    arrays, args = {}, {}
    given = {name: _np.ascontiguousarray(inputs[name]) for name in _INS}
    for name, a in {**given, **shape_tables()}.items():
        arrays[f"in_{name}"] = a
        args[name] = nc.dram_tensor(f"in_{name}", a.shape, _mybir.dt.from_np(a.dtype), kind="ExternalInput").ap()
    out = nc.dram_tensor("out_0", (1, L, D), _mybir.dt.float32, kind="ExternalOutput").ap()
    encoder_layer(nc, args, out)
    r = _run(nc, [arrays], core_ids=[0])
    return r.results[0]["out_0"]
```

```python
from contextlib import ExitStack
import math

import numpy as np

import concourse.bass as bass
from concourse import mybir

F32 = mybir.dt.float32
F32R = mybir.dt.float32r
ALU = mybir.AluOpType
ACT = mybir.ActivationFunctionType

P = 128
D = 1024
L = 2048
DH = 512
NF = 2 * L
N1 = 32
KT = D // P
PROJ = 3 * DH + DH + 2 * DH
EMB, HID = 33, 64
GS = L // P
GF = NF // P
NPAIR = N1 // 2
CH = 512
ALPHA = 2.0 ** 0.25
LN_EPS = 1e-5
WINDOWS = (2, 4, 8, 16)
POOL_STEPS = [sum(w.bit_length() - 1 + (3 if w > 2 else 2) for w in WINDOWS[:i + 1]) for i in range(4)]
PAD = 8



def _round12(a):
    b = np.ascontiguousarray(a, np.float32).view(np.uint32)
    b = (b + np.uint32(0x7FF) + ((b >> np.uint32(12)) & np.uint32(1))) & np.uint32(0xFFFFF000)
    return b.view(np.float32)


def _hilo(a, axis):
    hi = _round12(a)
    lo = _round12(np.asarray(a, np.float64) - hi)
    return np.ascontiguousarray(np.stack([hi, lo], axis=axis))


def shape_tables():
    tau = 2 * np.pi

    def row(slot, t1, t2):
        q = slot // 2
        ang = tau * ((q * (P * t1 + t2)) % NF) / NF
        v = np.where(slot % 2 == 0, np.cos(ang), -np.sin(ang))
        return np.where(slot == 0, 1.0, np.where(slot == 1, 1.0 - 2.0 * (t1 % 2), v))

    p = np.arange(P)
    g = np.arange(GF)[:, None, None]
    v = row(p[None, None, :] // 4, p[None, :, None] // 4, 32 * (p[None, :, None] % 4) + g)
    same = (p[:, None] % 4) == (p[None, :] % 4)
    w1f = _hilo(v * same[None], 2)
    g = np.arange(GS)[:, None, None]
    same = (p[:, None] % 8) == (p[None, :] % 8)
    halves = []
    for m in range(2):
        v = row(16 * m + p[None, None, :] // 8, p[None, :, None] // 8, 16 * (p[None, :, None] % 8) + g)
        halves.append(v * same[None])
    w1s = _hilo(np.stack(halves, 2), 3)
    iw1 = _hilo(np.stack([h.transpose(0, 2, 1) for h in halves], 2) * (2.0 / NF), 3)
    ang = tau * ((p[:, None] * p[None, :]) % P) / P
    dft = _hilo(np.stack([np.cos(ang), np.sin(ang), -np.sin(ang)], 1), 2)
    j = np.arange(64)
    f0 = np.zeros((P, 4, P))
    a0 = tau * ((p[:, None] * j) % P) / P
    a16 = tau * ((p[:, None] * (16 + 32 * j)) % NF) / NF
    f0[:, 0, :64] = np.cos(a0)
    f0[:, 1, :64] = -np.sin(a0)
    f0[:, 1, 0] = 1.0 - 2.0 * (p % 2)
    f0[:, 2, 64:] = np.cos(a16)
    f0[:, 3, 64:] = -np.sin(a16)
    inv = np.zeros((P, 4, P))
    for i in range(2):
        for o in range(2):
            inv[:, o * 2 + i, :] = f0[:, i * 2 + o, :].T
    inv[0] *= 0.5
    f32 = np.float32
    t = np.linspace(0.0, 1.0, L, dtype=f32)[:, None]
    bands = (EMB - 1) // 2
    w = f32(2.0 * math.pi / L) * np.arange(L, dtype=f32)[:, None]
    f = np.linspace(1e-4, bands - 1, bands, dtype=f32)[None, :]
    fw = (f * w).astype(np.float64)
    z = np.concatenate([t, np.cos(fw), -np.sin(fw)], axis=-1).astype(f32)
    z2 = np.ascontiguousarray(np.concatenate([z.T, z[::-1].T], 0))
    deltas = np.linspace(math.log(1e-2) / 1.5, math.log(1e-2) / 0.3, DH, dtype=f32)
    dec = np.exp((-t * np.abs(deltas)[None, :]).astype(np.float64)).astype(f32)
    dec = np.concatenate([dec, dec[::-1]], 0).reshape(P, GF, DH).transpose(1, 0, 2)
    edge = np.ones((4, 2, PAD))
    for gi, win in enumerate(WINDOWS):
        h = win // 2
        for i in range(h):
            edge[gi, 0, i] = win / (i + h)
        for i in range(h - 1):
            edge[gi, 1, PAD - 1 - i] = win / (1 + i + h)
    return {
        "t_w1f": w1f, "t_w1s": w1s, "t_iw1": iw1, "t_dft": dft,
        "t_f0": _hilo(f0, 2), "t_i0": _hilo(inv, 2), "t_z": z2,
        "t_decay": np.ascontiguousarray(dec),
        "t_edge": np.ascontiguousarray(edge, f32), "t_eye": np.eye(P, dtype=f32),
    }



def mm3(nc, out, w, m, start, stop):
    nc.tensor.matmul(out, w[0], m[0], start=start, stop=False, skip_group_check=True)
    nc.tensor.matmul(out, w[0], m[1], start=False, stop=False, skip_group_check=True)
    return nc.tensor.matmul(out, w[1], m[0], start=False, stop=stop, skip_group_check=True)


def f32(ap):
    return ap.bitcast(F32)


def plain(eng, sem, value):
    eng.wait_ge(sem, value)


def after(eng, sem, count):
    if not (isinstance(count, int) and count <= 0):
        eng.wait_ge(sem, count)


U = 4


def at(it, b, ring):
    it, b = it + b // U, b % U
    return b % ring, (U // ring) * it + b // ring


def pipeline(eng, units, steps, peel=(0,)):
    bodies = units // U
    first = max(1, -(-max(lag for _, lag in steps) // U))

    def body(it, count=U):
        for b in range(count):
            for step, lag in steps:
                if not isinstance(it, int) or 0 <= U * it + b - lag < units:
                    step(it, b - lag)

    it = 0
    while it < bodies:
        if it < first or it in peel:
            body(it)
            it += 1
            continue
        end = min([p for p in peel if p > it] + [bodies])
        with eng.Fori(it, end) as i:
            body(i)
        it = end
    body(bodies, max(lag for _, lag in steps))


class Scope:

    def __init__(self, nc, tag):
        self.nc, self.tag, self.ctx, self.semaphores = nc, tag, ExitStack(), []

    def __enter__(self):
        return self

    def __exit__(self, *a):
        self.ctx.__exit__(*a)
        if self.semaphores:
            self.nc.clear_and_free_semaphores(self.semaphores)
            self.nc.all_engine_barrier()

    def sb(self, name, shape, dt=F32):
        return self.ctx.enter_context(self.nc.sbuf_tensor(f"{self.tag}_{name}", shape, dt))

    def ps(self, name, shape):
        return self.ctx.enter_context(self.nc.psum_tensor(f"{self.tag}_{name}", shape, F32))

    def sem(self, name):
        self.semaphores.append(self.nc.alloc_semaphore(f"{self.tag}_{name}"))
        return self.semaphores[-1]

    def sems(self, name, n=2):
        return [self.sem(f"{name}{i}") for i in range(n)]

    def block(self):
        return self.ctx.enter_context(self.nc.Block())



def front(nc, t, hfil, tabs, scale1, shift, rows):
    MAGIC = 1.5 * 2.0 ** 23
    C1 = 6.28125
    C2 = 2 * math.pi - C1
    PI = 3.1415925
    HL = L // 2
    with Scope(nc, "net") as s:
        feat = s.sb("feat", [P, L])
        wl = s.sb("wl", [P, 3, P])
        cols = s.sb("cols", [P, 4])
        arg = s.sb("arg", [P, 2, HL])
        turn = s.sb("turn", [P, 2, HL])
        h = s.sb("h", [P, 2, HL])
        wa = [s.sb(f"wa{b}", [P, 3 * D]) for b in range(2)]
        acc = s.sb("acc", [P, 3 * D])
        c_in = s.sb("c_in", [P, KT])
        c_silu = s.sb("c_silu", [P, KT])
        b_cols = s.sb("b_cols", [P, 16])
        b_gate = s.sb("b_gate", [1, D])
        b_out = s.sb("b_out", [1, D])
        gate = s.sb("gate", [1, 2, D])
        ones = s.sb("ones", [P, P])
        ps = s.ps("ps", [P, 4, CH])
        ps_cols = s.ps("ps_cols", [P, 16])
        ps_gate = s.ps("ps_gate", [P, 2, CH])
        zeroed, loaded, step, split_hi, split_lo, copied = (
            s.sem(n) for n in ("zeroed", "loaded", "step", "split_hi", "split_lo", "copied"))
        lin_done, arg_done, turn_done, fold_done, sin_done = (
            s.sems(n) for n in ("lin_done", "arg_done", "turn_done", "fold_done", "sin_done"))
        w_in = s.sems("w_in")
        c_loaded, silu_done, acc_done, sum_done, cols_done, gate_done, prod_done, rows_out = (
            s.sem(n) for n in ("c_loaded", "silu_done", "acc_done", "sum_done", "cols_done",
                               "gate_done", "prod_done", "rows_out"))
        block = s.block()
        psf = ps[:, :, :].rearrange("p (a c) b -> p a (c b)", a=2)

        @block.sync
        def _(sp):
            sp.dma_start(feat[0:2 * EMB, :], t["t_z"][:, :]).then_inc(loaded, 16)
            for half in range(2):
                hs = slice(64 * half, 64 * half + 64)
                for c, src in enumerate((t["filt_b1"][0, :], t["filt_b_inner"][0, 0, :],
                                         t["filt_b_inner"][0, 1, :], t["filt_freq"][0, :])):
                    sp.dma_start(cols[hs, c:c + 1], src.rearrange("(p o) -> p o", o=1)).then_inc(loaded, 16)
            sp.wait_ge(zeroed, 1)
            for half in range(2):
                hs = slice(64 * half, 64 * half + 64)
                sp.dma_start(wl[EMB * half:EMB * half + EMB, 0, hs], t["filt_w1"][0, :, :]).then_inc(loaded, 16)
                for i in range(2):
                    sp.dma_start(wl[hs, 1 + i, hs], t["filt_w_inner"][0, i, :, :]).then_inc(loaded, 16)
            for k in range(KT):
                if k >= 2:
                    sp.wait_ge(acc_done, k - 1)
                sp.dma_start(wa[k % 2][:, :], t["w_ada"][0, k * P:(k + 1) * P, :]).then_inc(w_in[k % 2], 16)
            for n in ("w1f", "dft", "f0", "i0"):
                sp.dma_start(tabs[n], t["t_" + n]).then_inc(copied, 16)
            sp.wait_ge(prod_done, 1)
            sp.wait_ge(gate_done, 1)
            sp.dma_start(rows, gate[:, :, :]).then_inc(rows_out, 16)
            sp.wait_ge(rows_out, 16)
            sp.wait_ge(copied, 64)

        @block.gpsimd
        def _(pool):
            nc.gpsimd.memset(wl[:, :, :], 0.0).then_inc(zeroed, 1)
            pool.wait_ge(zeroed, 1)
            nc.gpsimd.memset(f32(hfil[0:64, :, 64:128, :]), 0.0).then_inc(zeroed, 1)
            pool.wait_ge(zeroed, 2)
            nc.gpsimd.memset(f32(hfil[64:128, :, 0:64, :]), 0.0).then_inc(zeroed, 1)
            pool.wait_ge(zeroed, 3)
            nc.gpsimd.memset(ones[:, :], 1.0).then_inc(zeroed, 1)

        @block.tensor
        def _(pe):
            pe.wait_ge(loaded, 15 * 16)
            for layer in range(3):
                src, k = (feat, 2 * EMB) if layer == 0 else (h[:, :, :].rearrange("p a b -> p (a b)"), P)
                for a in range(2):
                    if layer:
                        pe.wait_ge(sin_done[a], layer)
                    for c in range(2 * a, 2 * a + 2):
                        mm = nc.tensor.matmul(ps[:, c, :], wl[0:k, layer, :], src[0:k, c * CH:(c + 1) * CH],
                                              start=True, stop=True)
                    mm.then_inc(lin_done[a], 1)
            pe.wait_ge(zeroed, 4)
            pe.wait_ge(acc_done, KT)
            pe.wait_ge(c_loaded, 64)
            for j in range(16):
                nc.tensor.matmul(ps_cols[:, j:j + 1], acc[:, j * P:(j + 1) * P], ones[:, 0:1], start=True, stop=True,
                                 skip_group_check=True)
            for q in range(2):
                mm = nc.tensor.matmul(ps_gate[0:1, q, :], ones[:, 0:1], acc[:, 2 * D + q * CH:2 * D + (q + 1) * CH],
                                      start=True, stop=True)
            mm.then_inc(sum_done, 1)

        @block.vector
        def _(dve):
            def weigh(k):
                dve.wait_ge(w_in[k % 2], 16 * (k // 2) + 16)
                if k == 0:
                    dve.wait_ge(silu_done, 1)
                    nc.vector.tensor_scalar(acc[:, :], wa[0][:, :], c_silu[:, 0:1], None,
                                            ALU.mult).then_inc(acc_done, 1)
                else:
                    dve.wait_ge(acc_done, k)
                    nc.vector.scalar_tensor_tensor(out=acc[:, :], in0=wa[k % 2][:, :], scalar=c_silu[:, k:k + 1],
                                                   in1=acc[:, :], op0=ALU.mult, op1=ALU.add).then_inc(acc_done, 1)

            n = 0
            for layer in range(3):
                for a in range(2):
                    dve.wait_ge(lin_done[a], layer + 1)
                    if layer:
                        dve.wait_ge(sin_done[a], layer)
                    nc.vector.tensor_scalar(arg[:, a, :], psf[:, a, :], cols[:, layer:layer + 1], cols[:, 3:4],
                                            ALU.add, ALU.mult).then_inc(arg_done[a], 1)
                for a in range(2):
                    dve.wait_ge(turn_done[a], 2 * layer + 2)
                    for c in (C1, C2):
                        nc.vector.scalar_tensor_tensor(out=arg[:, a, :], in0=turn[:, a, :], scalar=-c,
                                                       in1=arg[:, a, :], op0=ALU.mult, op1=ALU.add).then_inc(step, 1)
                        n += 1
                        dve.wait_ge(step, n)
                    nc.vector.tensor_scalar(arg[:, a, :], arg[:, a, :], PI, -PI, ALU.min,
                                            ALU.max).then_inc(fold_done[a], 1)
                    weigh(2 * layer + a)
            for half in range(2):
                hs = slice(64 * half, 64 * half + 64)
                dve.wait_ge(split_hi, half + 1)
                nc.vector.tensor_tensor(hfil[hs, 1, hs, :], h[hs, :, :].rearrange("p a (c g) -> p (a c) g", g=GF),
                                        f32(hfil[hs, 0, hs, :]), ALU.subtract).then_inc(split_lo, 1)
            for k in range(6, KT):
                weigh(k)
            dve.wait_ge(sum_done, 1)
            nc.vector.tensor_tensor(shift[:, :], ps_cols[:, 0:8], b_cols[:, 0:8], ALU.add).then_inc(cols_done, 1)
            nc.vector.scalar_tensor_tensor(out=scale1[:, :], in0=ps_cols[:, 8:16], scalar=1.0, in1=b_cols[:, 8:16],
                                           op0=ALU.add, op1=ALU.add).then_inc(cols_done, 1)
            nc.vector.tensor_tensor(gate[:, 0, :], ps_gate[0:1, :, :].rearrange("p a b -> p (a b)"), b_gate[:, :],
                                    ALU.add).then_inc(gate_done, 1)
            dve.wait_ge(gate_done, 1)
            nc.vector.tensor_tensor(gate[:, 1, :], b_out[:, :], gate[:, 0, :], ALU.mult).then_inc(prod_done, 1)

        @block.scalar
        def _(act):
            with nc.allow_non_contiguous_dma(reason="columns of small vectors"):
                act.dma_start(c_in[:, :], t["c"].rearrange("o (k p) -> p (o k)", p=P)).then_inc(c_loaded, 16)
                act.dma_start(b_cols[:, :], t["b_ada"][0, 0:2 * D].rearrange("(k p) -> p k", p=P)).then_inc(c_loaded, 16)
            act.dma_start(b_gate[:, :], t["b_ada"][:, 2 * D:3 * D]).then_inc(c_loaded, 16)
            act.dma_start(b_out[:, :], t["b_out"]).then_inc(c_loaded, 16)
            act.wait_ge(c_loaded, 64)
            nc.scalar.activation(c_silu[:, :], c_in[:, :], ACT.Silu).then_inc(silu_done, 1)
            for layer in range(3):
                for a in range(2):
                    act.wait_ge(arg_done[a], layer + 1)
                    nc.scalar.activation(turn[:, a, :], arg[:, a, :], ACT.Copy, scale=1.0 / (2 * math.pi),
                                         bias=MAGIC).then_inc(turn_done[a], 1)
                    act.wait_ge(turn_done[a], 2 * layer + 1)
                    nc.scalar.activation(turn[:, a, :], turn[:, a, :], ACT.Copy, bias=-MAGIC).then_inc(turn_done[a], 1)
                for a in range(2):
                    act.wait_ge(fold_done[a], layer + 1)
                    nc.scalar.activation(h[:, a, :], arg[:, a, :], ACT.Sin).then_inc(sin_done[a], 1)
            for a in range(2):
                act.wait_ge(sin_done[a], 3)
            for half in range(2):
                hs = slice(64 * half, 64 * half + 64)
                nc.scalar.activation(hfil[hs, 0, hs, :], h[hs, :, :].rearrange("p a (c g) -> p (a c) g", g=GF),
                                     ACT.Copy).then_inc(split_hi, 1)



def filter_stage1(nc, t, tabs, hfil, xf):
    with Scope(nc, "fs1") as s:
        wfil = s.sb("wfil", [P, 2, 2, DH], F32R)
        e0 = s.sb("e0", [1, P])
        hs_ = [s.sb(f"hs{b}", [P, 2, P], F32R) for b in range(2)]
        tab = [s.sb(f"tab{b}", [P, 2, P], F32R) for b in range(4)]
        dec = [s.sb(f"dec{b}", [P, DH]) for b in range(4)]
        kf = [s.sb(f"k{b}", [P, 2, DH]) for b in range(2)]
        wraw, bias = kf
        khi = [s.sb(f"khi{b}", [P, 2, DH], F32R) for b in range(2)]
        klo = [s.sb(f"klo{b}", [P, 2, DH], F32R) for b in range(2)]
        gen_ps = [s.ps(f"gen{b}", [P, 2, CH]) for b in range(2)]
        s1_ps = [s.ps(f"s1{b}", [P, 2, CH]) for b in range(2)]
        loaded, e0_set, whi_done, wlo_done = (s.sem(n) for n in ("loaded", "e0_set", "whi_done", "wlo_done"))
        dec_in, tab_in = (s.sems(n, 4) for n in ("dec_in", "tab_in"))
        hs_ready, gen_done, k_done, hi_done, lo_done, s1_done, evac_done = (
            s.sems(n) for n in ("hs_ready", "gen_done", "k_done", "hi_done", "lo_done", "s1_done", "evac_done"))
        block = s.block()

        @block.sync
        def _(sp):
            wsrc = t["filt_w_out"][0, :, :].rearrange("f (o r d) -> f o r d", o=2, r=2)
            for r in range(2):
                sp.dma_start(wraw[64 * r:64 * r + 64, :, :], wsrc[:, :, r, :]).then_inc(loaded, 16)
            sp.dma_start(bias[0:1, :, :], t["hyena_bias"][0:1, :, :]).then_inc(loaded, 16)

            def load(it, b):
                slot, used = at(it, b, 4)
                two, used2 = at(it, b - 4, 2)
                if not (isinstance(it, int) and it == 0):
                    after(sp, k_done[two], used2 + 1)
                    after(sp, s1_done[two], used2 + 1)
                sp.dma_start(dec[slot][:, :], t["t_decay"][4 * it + b, :, :]).then_inc(dec_in[slot], 16)
                sp.dma_start(f32(tab[slot][:, :, :]), tabs["w1f"][4 * it + b, :, :, :]).then_inc(tab_in[slot], 16)

            pipeline(sp, GF, [(load, 0)])

        @block.gpsimd
        def _(pool):
            nc.gpsimd.memset(e0[:, :], 0.0).then_inc(e0_set, 1)
            pool.wait_ge(e0_set, 1)
            nc.gpsimd.memset(e0[:, 0:1], 1.0).then_inc(e0_set, 1)
            pool.wait_ge(e0_set, 2)
            for n in range(GF):
                after(pool, gen_done[n % 2], n // 2)
                nc.gpsimd.tensor_copy(hs_[n % 2][:, :, :], hfil[:, :, :, n]).then_inc(hs_ready[n % 2], 1)

        @block.tensor
        def _(pe):
            def gen(it, b):
                first = isinstance(it, int) and U * it + b == 0
                r, used = at(it, b, 2)
                pe.wait_ge(hs_ready[r], used + 1)
                after(pe, k_done[r], used)
                for o in range(2):
                    mm = mm3(nc, gen_ps[r][:, o, :], (hs_[r][:, 0, :], hs_[r][:, 1, :]),
                             (wfil[:, 0, o, :], wfil[:, 1, o, :]), True, not first)
                    if first:
                        mm = nc.tensor.matmul(gen_ps[r][:, o, :], e0[:, :], bias[0:1, o, :], start=False, stop=True,
                                              skip_group_check=True)
                mm.then_inc(gen_done[r], 1)

            def stage1(it, b):
                r, used = at(it, b, 2)
                r4, used4 = at(it, b, 4)
                pe.wait_ge(lo_done[r], used + 1)
                pe.wait_ge(tab_in[r4], 16 * used4 + 16)
                after(pe, evac_done[r], used)
                for o in range(2):
                    mm = mm3(nc, s1_ps[r][:, o, :], (tab[r4][:, 0, :], tab[r4][:, 1, :]),
                             (khi[r][:, o, :], klo[r][:, o, :]), True, True)
                mm.then_inc(s1_done[r], 1)

            pe.wait_ge(wlo_done, 1)
            pe.wait_ge(loaded, 48)
            pe.wait_ge(e0_set, 2)
            pipeline(pe, GF, [(gen, 0), (stage1, 2)])

        @block.vector
        def _(dve):
            def window(it, b):
                r, used = at(it, b, 2)
                r4, used4 = at(it, b, 4)
                dve.wait_ge(gen_done[r], used + 1)
                dve.wait_ge(dec_in[r4], 16 * used4 + 16)
                after(dve, lo_done[r], used)
                nc.vector.tensor_tensor(kf[r][:, :, :], gen_ps[r][:, :, :],
                                        dec[r4][:, :].unsqueeze(1).broadcast_to([P, 2, DH]),
                                        ALU.mult).then_inc(k_done[r], 1)

            def low(it, b):
                r, used = at(it, b, 2)
                dve.wait_ge(hi_done[r], used + 1)
                after(dve, s1_done[r], used)
                nc.vector.tensor_tensor(klo[r][:, :, :], kf[r][:, :, :], f32(khi[r][:, :, :]),
                                        ALU.subtract).then_inc(lo_done[r], 1)

            dve.wait_ge(whi_done, 1)
            nc.vector.tensor_tensor(wfil[:, 1, :, :], wraw[:, :, :], f32(wfil[:, 0, :, :]),
                                    ALU.subtract).then_inc(wlo_done, 1)
            pipeline(dve, GF, [(window, 0), (low, 1)])

        @block.scalar
        def _(act):
            def high(it, b):
                r, used = at(it, b, 2)
                act.wait_ge(k_done[r], used + 1)
                after(act, s1_done[r], used)
                nc.scalar.activation(khi[r][:, :, :], kf[r][:, :, :], ACT.Copy).then_inc(hi_done[r], 1)

            def evac(it, b):
                r, used = at(it, b, 2)
                act.wait_ge(s1_done[r], used + 1)
                plain(act, loaded, 48)
                nc.scalar.activation(xf[:, :, 4 * it + b, :], s1_ps[r][:, :, :], ACT.Copy).then_inc(evac_done[r], 1)

            act.wait_ge(loaded, 48)
            nc.scalar.activation(wfil[:, 0, :, :], wraw[:, :, :], ACT.Copy).then_inc(whi_done, 1)
            pipeline(act, GF, [(high, 0), (evac, 2)])


class Dft:

    def __init__(self, s):
        self.gen = s.sb("dft", [P, 3, 2, P], F32R)
        self.fwd0 = s.sb("fwd0", [P, 4, 2, P], F32R)
        self.inv0 = s.sb("inv0", [P, 4, 2, P], F32R)

    def load(self, eng, tabs, sem):
        eng.dma_start(f32(self.fwd0[:, :, :, :]), tabs["f0"][:, :, :, :]).then_inc(sem, 16)
        eng.dma_start(f32(self.gen[:, :, :, :]), tabs["dft"][:, :, :, :]).then_inc(sem, 16)
        eng.dma_start(f32(self.inv0[:, :, :, :]), tabs["i0"][:, :, :, :]).then_inc(sem, 16)

    def passes(self, nc, out, hi, lo, inverse, first):
        if first:
            tabs = self.inv0 if inverse else self.fwd0
            pick = (0, 1, 2, 3)
        else:
            tabs = self.gen
            pick = (0, 1, 2, 0) if inverse else (0, 2, 1, 0)
        for o in range(2):
            for i in range(2):
                k = pick[2 * i + o]
                mm = mm3(nc, out[:, o, :], (tabs[:, k, 0, :], tabs[:, k, 1, :]),
                         (hi[:, i, :], lo[:, i, :]), i == 0, i == 1)
        return mm



def filter_stage2(nc, tabs, xf, kfreq):
    with Scope(nc, "fs2") as s:
        dft = Dft(s)
        a = [s.sb(f"a{b}", [P, 2, DH]) for b in range(4)]
        ahi = [s.sb(f"ahi{b}", [P, 2, DH], F32R) for b in range(4)]
        alo = [s.sb(f"alo{b}", [P, 2, DH], F32R) for b in range(4)]
        out = [s.sb(f"out{b}", [P, 2, DH]) for b in range(2)]
        ps = [s.ps(f"ps{b}", [P, 2, CH]) for b in range(2)]
        tabs_in = s.sem("tabs_in")
        a_in, hi_done, lo_done = (s.sems(n, 4) for n in ("a_in", "hi_done", "lo_done"))
        mm_done, re_out, im_out, stored = (s.sems(n) for n in ("mm_done", "re_out", "im_out", "stored"))
        block = s.block()
        UNITS = 2 * NPAIR

        @block.sync
        def _(sp):
            def load(n):
                b, o, q = n % 4, n // NPAIR, n % NPAIR
                after(sp, lo_done[b], n // 4)
                for i in range(2):
                    slot = 2 * q + i
                    sp.dma_start(a[b][:, i, :], xf[4 * slot:4 * slot + 4, o, :, :]).then_inc(a_in[b], 16)

            load(0)
            dft.load(sp, tabs, tabs_in)
            for n in range(1, 4):
                load(n)
            for n in range(UNITS):
                b, it = n % 2, n // 2
                if n + 4 < UNITS:
                    load(n + 4)
                sp.wait_ge(re_out[b], it + 1)
                sp.wait_ge(im_out[b], it + 1)
                sp.dma_start(kfreq[n // NPAIR, n % NPAIR, :, :, :], out[b][:, :, :]).then_inc(stored[b], 16)
            for b in range(2):
                sp.wait_ge(stored[b], 16 * NPAIR)

        @block.tensor
        def _(pe):
            def unit(it, b):
                r, used = at(it, b, 2)
                r4, used4 = at(it, b, 4)
                pe.wait_ge(lo_done[r4], used4 + 1)
                after(pe, re_out[r], used)
                after(pe, im_out[r], used)
                first = isinstance(it, int) and (U * it + b) % NPAIR == 0
                dft.passes(nc, ps[r], ahi[r4], alo[r4], False, first).then_inc(mm_done[r], 1)

            pe.wait_ge(tabs_in, 48)
            pipeline(pe, UNITS, [(unit, 0)], peel=(0, NPAIR // U))

        @block.scalar
        def _(act):
            def high(it, b):
                r4, used4 = at(it, b, 4)
                two, used = at(it, b - 4, 2)
                act.wait_ge(a_in[r4], 32 * used4 + 32)
                after(act, mm_done[two], used + 1)
                nc.scalar.activation(ahi[r4][:, :, :], a[r4][:, :, :], ACT.Copy).then_inc(hi_done[r4], 1)

            def evac(it, b):
                r, used = at(it, b, 2)
                act.wait_ge(mm_done[r], used + 1)
                after(act, stored[r], 16 * used)
                nc.scalar.activation(out[r][:, 0, :], ps[r][:, 0, :], ACT.Copy).then_inc(re_out[r], 1)

            pipeline(act, UNITS, [(high, 0), (evac, 2)])

        @block.vector
        def _(dve):
            def low(it, b):
                r4, used4 = at(it, b, 4)
                two, used = at(it, b - 4, 2)
                dve.wait_ge(hi_done[r4], used4 + 1)
                after(dve, mm_done[two], used + 1)
                nc.vector.tensor_tensor(alo[r4][:, :, :], a[r4][:, :, :], f32(ahi[r4][:, :, :]),
                                        ALU.subtract).then_inc(lo_done[r4], 1)

            def evac(it, b):
                r, used = at(it, b, 2)
                dve.wait_ge(mm_done[r], used + 1)
                after(dve, stored[r], 16 * used)
                nc.vector.tensor_copy(out[r][:, 1, :], ps[r][:, 1, :]).then_inc(im_out[r], 1)

            pipeline(dve, UNITS, [(low, 0), (evac, 2)])



def transpose_input(nc, t, scale1, shift, uhi, ulo, eye):
    with Scope(nc, "tin") as s:
        xs = [s.sb(f"xs{b}", [P, 4, D]) for b in range(2)]
        ut = [s.sb(f"ut{j}", [P, CH]) for j in range(4)]
        ps = [s.ps(f"ps{j}", [P, CH]) for j in range(4)]
        eye_in = s.sem("eye_in")
        x_in = s.sems("x_in")
        tr_done, hi_done, u_done, lo_done = (s.sems(n, 4) for n in ("tr_done", "hi_done", "u_done", "lo_done"))
        block = s.block()

        @block.sync
        def _(sp):
            sp.dma_start(eye[:, :], t["t_eye"][:, :]).then_inc(eye_in, 16)
            for tc in range(4):
                if tc >= 2:
                    for j in range(4):
                        sp.wait_ge(tr_done[j], 2 * (tc - 1))
                sp.dma_start(xs[tc % 2][:, :, :],
                             t["x"][0, tc * CH:(tc + 1) * CH, :].rearrange("(j p) d -> p j d", p=P)
                             ).then_inc(x_in[tc % 2], 16)

        @block.tensor
        def _(pe):
            pe.wait_ge(eye_in, 16)
            for tc in range(4):
                pe.wait_ge(x_in[tc % 2], 16 * (tc // 2) + 16)
                for k in range(KT):
                    j, use = k % 4, 2 * tc + k // 4
                    after(pe, u_done[j], use)
                    for i in range(4):
                        mm = nc.tensor.transpose(ps[j][:, i * P:(i + 1) * P], xs[tc % 2][:, i, k * P:(k + 1) * P],
                                                 eye[:, :])
                    mm.then_inc(tr_done[j], 1)

        def each_chunk(eng, body):
            body(0)
            with eng.Fori(1, 4) as tc:
                body(tc)

        @block.scalar
        def _(act):
            def body(tc):
                for k in range(KT):
                    j = k % 4
                    act.wait_ge(u_done[j], 2 * tc + k // 4 + 1)
                    plain(act, eye_in, 16)
                    nc.scalar.activation(uhi[:, k, bass.ds(tc * CH, CH)], ut[j][:, :], ACT.Copy).then_inc(hi_done[j], 1)

            act.wait_ge(eye_in, 16)
            each_chunk(act, body)

        @block.gpsimd
        def _(pool):
            for tc in range(4):
                for k in range(1, KT, 2):
                    j, use = k % 4, 2 * tc + k // 4
                    pool.wait_ge(hi_done[j], use + 1)
                    nc.gpsimd.tensor_tensor(ulo[:, k, tc * CH:(tc + 1) * CH], ut[j][:, :],
                                            f32(uhi[:, k, tc * CH:(tc + 1) * CH]), ALU.subtract).then_inc(lo_done[j], 1)

        @block.vector
        def _(dve):
            def body(tc):
                for k in range(KT + 1):
                    if k < KT:
                        j, use = k % 4, 2 * tc + k // 4
                        dve.wait_ge(tr_done[j], use + 1)
                        after(dve, lo_done[j], use)
                        nc.vector.tensor_scalar(ut[j][:, :], ps[j][:, :], scale1[:, k:k + 1], shift[:, k:k + 1],
                                                ALU.mult, ALU.add).then_inc(u_done[j], 1)
                    if k % 2:
                        j, use = (k - 1) % 4, 2 * tc + (k - 1) // 4
                        dve.wait_ge(hi_done[j], use + 1)
                        nc.vector.tensor_tensor(ulo[:, k - 1, bass.ds(tc * CH, CH)], ut[j][:, :],
                                                f32(uhi[:, k - 1, bass.ds(tc * CH, CH)]),
                                                ALU.subtract).then_inc(lo_done[j], 1)

            each_chunk(dve, body)



def project(nc, t, tabs, uhi, ulo, eye, vx, g2, yp):
    with Scope(nc, "prj") as s:
        ws = [s.sb(f"ws{b}", [P, KT, P]) for b in range(2)]
        whi = [s.sb(f"whi{b}", [P, KT, P], F32R) for b in range(2)]
        wlo = [s.sb(f"wlo{b}", [P, KT, P], F32R) for b in range(2)]
        W = L + 2 * PAD
        row = s.sb("row", [P, W])
        cv = [s.sb(f"cv{b}", [P, W]) for b in range(2)]
        st = s.sb("st", [P, GS, P])
        phl = [s.sb(f"phl{b}", [P, 2, CH], F32R) for b in range(2)]
        b_in = s.sb("b_in", [P, PROJ // P])
        bcol = s.sb("bcol", [P, 2])
        cw = s.sb("cw", [P, 3, 12])
        cb = s.sb("cb", [P, 12])
        pw = s.sb("pw", [P, 4, P])
        pwhl = s.sb("pwhl", [P, 2, 4, P], F32R)
        pscale = s.sb("pscale", [P, 4])
        edge = s.sb("edge", [P, 4, 2, PAD])
        pp = [s.ps(f"pp{c}", [P, CH]) for c in range(4)]
        px = [s.ps(f"px{c}", [P, CH]) for c in range(4)]
        consts, copied, pad_set, pwhi_done, pwlo_done = (
            s.sem(n) for n in ("consts", "copied", "pad_set", "pwhi_done", "pwlo_done"))
        w_in, whi_done, wlo_done, conv_step, conv_done, prj_last, bcol_set = (
            s.sems(n) for n in ("w_in", "whi_done", "wlo_done", "conv_step", "conv_done", "prj_last", "bcol_set"))
        prj_done, bank_read, tr_done, tr_read = (s.sems(n, 4) for n in ("prj_done", "bank_read", "tr_done", "tr_read"))
        st_stored, g2_done, g2_stored, pool_step, phi_done, plo_done, mix_done, yp_part, yp_stored = (
            s.sem(n) for n in ("st_stored", "g2_done", "g2_stored", "pool_step",
                               "phi_done", "plo_done", "mix_done", "yp_part", "yp_stored"))
        block = s.block()
        wsrc = t["w_in"][0, :, :].rearrange("(k p) n -> p k n", p=P)
        stf = st[:, :, :].rearrange("p g c -> p (g c)")

        @block.sync
        def _(sp):
            def load(it, b, tile):
                after(sp, wlo_done[b], it)
                sp.dma_start(ws[b][:, :, :], wsrc[:, :, bass.ds(tile * P, P)]).then_inc(w_in[b], 16)

            def copy_tables(g):
                for n in ("w1s", "iw1"):
                    src = t["t_" + n]
                    sp.dma_start(tabs[n][g, :, :, :, :], src[g, :, :, :, :]).then_inc(copied, 16)

            def store_t(n):
                for j in range(4):
                    sp.wait_ge(tr_read[j], n + 1)
                sp.dma_start(vx[:, :, bass.ds(n * P, P)], st[:, :, :]).then_inc(st_stored, 16)

            with nc.allow_non_contiguous_dma(reason="columns of small vectors"):
                sp.dma_start(b_in[:, :], t["b_in"][0, :].rearrange("(k p) -> p k", p=P)).then_inc(consts, 16)
                for j in range(3):
                    sp.dma_start(cw[:, j, :], t["conv_w"][0, j, :].rearrange("(k p) -> p k", p=P)).then_inc(consts, 16)
                sp.dma_start(cb[:, :], t["conv_b"][0, :].rearrange("(k p) -> p k", p=P)).then_inc(consts, 16)
                sp.dma_start(pscale[:, :], t["pool_scale"][0, :].rearrange("(k p) -> p k", p=P)).then_inc(consts, 16)
            sp.dma_start(pw[:, :, :], t["pool_w"][0, :, :, :].rearrange("g c d -> c g d")).then_inc(consts, 16)
            sp.dma_start(edge[:, :, :, :], t["t_edge"].partition_broadcast(P)).then_inc(consts, 16)
            load(0, 0, 0)
            load(0, 1, 1)

            def turned_step(it):
                for b in range(2):
                    load(it + 1, b, 2 * it + 2 + b)
                    copy_tables(2 * it + b)
                    store_t(2 * it + b)

            turned_step(0)
            with sp.Fori(1, 3) as it:
                turned_step(it)
            for b in range(2):
                load(4, b, 8 + 4 * b)
                copy_tables(6 + b)
                store_t(6 + b)
            with sp.Fori(0, 3) as i:
                for b in range(2):
                    load(i + 5, b, i + 9 + 4 * b)
                    copy_tables(2 * i + 8 + b)
                sp.wait_ge(g2_done, i + 1)
                sp.dma_start(g2[i, :, :], cv[1][:, 0:L]).then_inc(g2_stored, 16)
            for b in range(2):
                load(8, b, 16 + 4 * b)
                copy_tables(14 + b)
            sp.wait_ge(g2_done, 4)
            sp.dma_start(g2[3, :, :], cv[1][:, 0:L]).then_inc(g2_stored, 16)
            for i in range(4):
                if i < 3:
                    for b in range(2):
                        load(i + 9, b, i + 17 + 4 * b)
                sp.wait_ge(yp_part, 4 * i + 4)
                sp.dma_start(yp[i, :, :], row[:, PAD:PAD + L]).then_inc(yp_stored, 16)
            sp.wait_ge(g2_stored, 64)
            sp.wait_ge(yp_stored, 64)
            sp.wait_ge(st_stored, 128)
            sp.wait_ge(copied, 2 * 16 * GS)

        @block.gpsimd
        def _(pool):
            nc.gpsimd.memset(row[:, 0:PAD], 0.0).then_inc(pad_set, 1)
            pool.wait_ge(pad_set, 1)
            nc.gpsimd.memset(row[:, PAD + L:W], 0.0).then_inc(pad_set, 1)
            for it in range(12):
                for b in range(2):
                    pool.wait_ge(w_in[b], 16 * it + 16)
                    after(pool, prj_last[b], it)
                    nc.gpsimd.tensor_copy(whi[b][:, :, :], ws[b][:, :, :]).then_inc(whi_done[b], 1)
                    pool.wait_ge(whi_done[b], it + 1)
                    nc.gpsimd.tensor_tensor(wlo[b][:, :, :], ws[b][:, :, :], f32(whi[b][:, :, :]),
                                            ALU.subtract).then_inc(wlo_done[b], 1)

        @block.tensor
        def _(pe):
            def proj(it, b):
                pe.wait_ge(wlo_done[b], it + 1)
                for c in range(4):
                    after(pe, bank_read[c], 2 * it + b)
                    for k in range(KT):
                        mm = mm3(nc, pp[c][:, :], (whi[b][:, k, :], wlo[b][:, k, :]),
                                 (uhi[:, k, c * CH:(c + 1) * CH], ulo[:, k, c * CH:(c + 1) * CH]), k == 0, k == KT - 1)
                    mm.then_inc(prj_done[c] if c < 3 else prj_last[b], 1)

            def turn(it, b):
                pe.wait_ge(conv_done[b], it + 1)
                src = cv[b][:, 0:L].rearrange("p (c g) -> p g c", g=GS)
                for j in range(4):
                    after(pe, tr_read[j], 2 * it + b)
                    for i in range(4):
                        mm = nc.tensor.transpose(px[j][:, i * P:(i + 1) * P], src[:, 4 * j + i, :], eye[:, :])
                    mm.then_inc(tr_done[j], 1)

            def turned_step(it):
                proj(it, 1)
                turn(it, 0)
                proj(it + 1, 0)
                turn(it, 1)

            proj(0, 0)
            turned_step(0)
            with pe.Fori(1, 3) as it:
                turned_step(it)
            proj(3, 1)
            turn(3, 0)
            turn(3, 1)
            with pe.Fori(4, 8) as it:
                proj(it, 0)
                proj(it, 1)
            pe.wait_ge(pwlo_done, 1)
            for i in range(4):
                proj(8 + i, 0)
                proj(8 + i, 1)
                for c in range(4):
                    pe.wait_ge(plo_done, 4 * i + c + 1)
                    if i:
                        pe.wait_ge(yp_part, 4 * (i - 1) + c + 1)
                    mm3(nc, px[c][:, :], (pwhl[:, 0, i, :], pwhl[:, 1, i, :]),
                        (phl[c % 2][:, 0, :], phl[c % 2][:, 1, :]), True, True).then_inc(mix_done, 1)

        @block.scalar
        def _(act):
            def projected(it, b, c):
                if c < 3:
                    act.wait_ge(prj_done[c], 2 * it + b + 1)
                else:
                    act.wait_ge(prj_last[b], it + 1)

            def pick_bias(it, b, tile):
                nc.scalar.activation(bcol[:, b:b + 1], b_in[:, bass.ds(tile, 1)], ACT.Copy).then_inc(bcol_set[b], 1)
                act.wait_ge(bcol_set[b], it + 1)

            def bias_row(it, b):
                for c in range(4):
                    projected(it, b, c)
                    nc.scalar.activation(row[:, PAD + c * CH:PAD + (c + 1) * CH], pp[c][:, :], ACT.Identity,
                                         bias=bcol[:, b:b + 1]).then_inc(bank_read[c], 1)

            def gate_row(it, b):
                for c in range(4):
                    projected(it, b, c)
                    nc.scalar.activation(stf[:, c * CH:(c + 1) * CH], pp[c][:, :], ACT.Silu,
                                         bias=bcol[:, b:b + 1]).then_inc(bank_read[c], 1)

            def store_turned(it, b):
                after(act, st_stored, 32 * it + 16 * b)
                for j in range(4):
                    act.wait_ge(tr_done[j], 2 * it + b + 1)
                    nc.scalar.activation(st[:, 4 * j:4 * j + 4, :], px[j][:, :], ACT.Copy).then_inc(tr_read[j], 1)

            act.wait_ge(consts, 8 * 16)
            act.wait_ge(pad_set, 2)
            nc.scalar.activation(pwhl[:, 0, :, :], pw[:, :, :], ACT.Copy).then_inc(pwhi_done, 1)
            pick_bias(0, 0, 0)
            bias_row(0, 0)

            def turned_step(it):
                pick_bias(it, 1, 2 * it + 1)
                act.wait_ge(conv_done[0], it + 1)
                bias_row(it, 1)
                store_turned(it, 0)
                pick_bias(it + 1, 0, 2 * it + 2)
                act.wait_ge(conv_done[1], it + 1)
                bias_row(it + 1, 0)
                store_turned(it, 1)

            turned_step(0)
            with act.Fori(1, 3) as it:
                turned_step(it)
            pick_bias(3, 1, 7)
            act.wait_ge(conv_done[0], 4)
            bias_row(3, 1)
            store_turned(3, 0)
            store_turned(3, 1)
            act.wait_ge(conv_done[1], 4)
            act.wait_ge(st_stored, 128)

            def gated_step(i):
                pick_bias(i + 4, 0, i + 8)
                after(act, g2_done, i)
                bias_row(i + 4, 0)
                pick_bias(i + 4, 1, i + 12)
                gate_row(i + 4, 1)

            gated_step(0)
            with act.Fori(1, 4) as i:
                gated_step(i)
            for i in range(4):
                pick_bias(i + 8, 0, i + 16)
                if i == 0:
                    act.wait_ge(g2_done, 4)
                else:
                    act.wait_ge(yp_stored, 16 * i)
                bias_row(i + 8, 0)
                pick_bias(i + 8, 1, i + 20)
                gate_row(i + 8, 1)
                pl = cv[i % 2]
                act.wait_ge(pool_step, POOL_STEPS[i])
                for c in range(4):
                    if c >= 2 or i:
                        act.wait_ge(mix_done, 4 * i + c - 1)
                    nc.scalar.activation(phl[c % 2][:, 0, :], pl[:, c * CH:(c + 1) * CH], ACT.Copy).then_inc(phi_done, 1)

        @block.vector
        def _(dve):
            def conv(it, b, n, tile, dst):
                for c in range(4):
                    dve.wait_ge(bank_read[c], n + 1)
                nc.vector.tensor_scalar(dst[:, 0:L], row[:, PAD - 1:PAD - 1 + L], cw[:, 0, bass.ds(tile, 1)],
                                        cb[:, bass.ds(tile, 1)], ALU.mult, ALU.add).then_inc(conv_step[b], 1)
                dve.wait_ge(conv_step[b], 2 * it + 1)
                nc.vector.scalar_tensor_tensor(out=dst[:, 0:L], in0=row[:, PAD:PAD + L], scalar=cw[:, 1, bass.ds(tile, 1)],
                                               in1=dst[:, 0:L], op0=ALU.mult, op1=ALU.add).then_inc(conv_step[b], 1)
                dve.wait_ge(conv_step[b], 2 * it + 2)
                nc.vector.scalar_tensor_tensor(out=dst[:, 0:L], in0=row[:, PAD + 1:PAD + 1 + L],
                                               scalar=cw[:, 2, bass.ds(tile, 1)], in1=dst[:, 0:L],
                                               op0=ALU.mult, op1=ALU.add).then_inc(conv_done[b], 1)

            dve.wait_ge(pwhi_done, 1)
            nc.vector.tensor_tensor(pwhl[:, 1, :, :], pw[:, :, :], f32(pwhl[:, 0, :, :]), ALU.subtract).then_inc(pwlo_done, 1)

            def turned_step(it):
                for b in range(2):
                    for j in range(4):
                        after(dve, tr_done[j], 2 * (it - 1) + b + 1)
                    conv(it, b, 2 * it + b, 2 * it + b, cv[b])

            turned_step(0)
            with dve.Fori(1, 4) as it:
                turned_step(it)
            for j in range(4):
                dve.wait_ge(tr_done[j], 8)

            def gated_step(i):
                conv(i + 4, 0, 2 * i + 8, i + 8, cv[0])
                dve.wait_ge(conv_done[0], i + 5)
                for c in range(4):
                    dve.wait_ge(bank_read[c], 2 * i + 10)
                after(dve, g2_stored, 16 * i)
                nc.vector.tensor_tensor(cv[1][:, 0:L], cv[0][:, 0:L], stf, ALU.mult).then_inc(g2_done, 1)

            gated_step(0)
            with dve.Fori(1, 4) as i:
                gated_step(i)
            dve.wait_ge(g2_stored, 64)
            step = 0
            for i, win in enumerate(WINDOWS):
                h = win // 2
                for c in range(4):
                    dve.wait_ge(bank_read[c], 2 * i + 17)
                after(dve, plo_done, 4 * i)
                src, n, k = row, 1, 0
                bufs = (cv[i % 2], cv[1 - i % 2])
                levels = win.bit_length() - 1
                lo_edge = PAD - h
                while n < win:
                    dst = bufs[(levels - k) % 2]
                    width = L + win - 2 * n
                    dve.wait_ge(pool_step, step)
                    nc.vector.tensor_tensor(dst[:, lo_edge:lo_edge + width], src[:, lo_edge:lo_edge + width],
                                            src[:, lo_edge + n:lo_edge + n + width], ALU.add).then_inc(pool_step, 1)
                    step += 1
                    src, n, k = dst, 2 * n, k + 1
                dve.wait_ge(pool_step, step)
                nc.vector.tensor_tensor(src[:, lo_edge:lo_edge + h], src[:, lo_edge:lo_edge + h],
                                        edge[:, i, 0, 0:h], ALU.mult).then_inc(pool_step, 1)
                step += 1
                if h > 1:
                    e = lo_edge + L
                    nc.vector.tensor_tensor(src[:, e - h + 1:e], src[:, e - h + 1:e],
                                            edge[:, i, 1, PAD - h + 1:PAD], ALU.mult).then_inc(pool_step, 1)
                    step += 1
                dve.wait_ge(pool_step, step)
                nc.vector.scalar_tensor_tensor(out=bufs[0][:, 0:L], in0=src[:, lo_edge:lo_edge + L], scalar=1.0 / win,
                                               in1=row[:, PAD:PAD + L], op0=ALU.mult, op1=ALU.subtract
                                               ).then_inc(pool_step, 1)
                step += 1
                assert step == POOL_STEPS[i]
                for c in range(4):
                    dve.wait_ge(phi_done, 4 * i + c + 1)
                    nc.vector.tensor_tensor(phl[c % 2][:, 1, :], bufs[0][:, c * CH:(c + 1) * CH],
                                            f32(phl[c % 2][:, 0, :]), ALU.subtract).then_inc(plo_done, 1)
                for c in range(4):
                    dve.wait_ge(mix_done, 4 * i + c + 1)
                    dve.wait_ge(bank_read[c], 18 + 2 * i)
                    nc.vector.scalar_tensor_tensor(out=row[:, PAD + c * CH:PAD + (c + 1) * CH], in0=px[c][:, :],
                                                   scalar=pscale[:, i:i + 1], in1=stf[:, c * CH:(c + 1) * CH],
                                                   op0=ALU.mult, op1=ALU.mult).then_inc(yp_part, 1)



def signal_stage1(nc, vx, tabs, dft, x):
    with Scope(nc, "ss1") as s:
        z = [s.sb(f"z{b}", [P, DH]) for b in range(4)]
        zhi = [s.sb(f"zhi{b}", [P, DH], F32R) for b in range(2)]
        zlo = [s.sb(f"zlo{b}", [P, DH], F32R) for b in range(2)]
        tab = [s.sb(f"tab{b}", [P, 2, 2, P], F32R) for b in range(4)]
        ps = [s.ps(f"ps{b}", [P, 2, CH]) for b in range(2)]
        tabs_in = s.sem("tabs_in")
        z_in, tab_in = (s.sems(n, 4) for n in ("z_in", "tab_in"))
        hi_done, lo_done, mm_done, out0, out1 = (s.sems(n) for n in ("hi_done", "lo_done", "mm_done", "out0", "out1"))
        block = s.block()

        @block.sync
        def _(sp):
            def load(it, b):
                slot, _ = at(it, b, 4)
                two, used = at(it, b - 4, 2)
                if not (isinstance(it, int) and it == 0):
                    after(sp, lo_done[two], used + 1)
                    after(sp, mm_done[two], used + 1)
                sp.dma_start(z[slot][:, :], vx[:, 4 * it + b, 0:DH]).then_inc(z_in[slot], 16)
                sp.dma_start(f32(tab[slot][:, :, :, :]), tabs["w1s"][4 * it + b, :, :, :, :]).then_inc(tab_in[slot], 16)

            pipeline(sp, GS, [(load, 0)])
            dft.load(sp, tabs, tabs_in)
            sp.wait_ge(tabs_in, 48)

        @block.tensor
        def _(pe):
            def unit(it, b):
                r, used = at(it, b, 2)
                r4, used4 = at(it, b, 4)
                pe.wait_ge(tab_in[r4], 16 * used4 + 16)
                pe.wait_ge(lo_done[r], used + 1)
                after(pe, out0[r], used)
                after(pe, out1[r], used)
                for m in range(2):
                    mm = mm3(nc, ps[r][:, m, :], (tab[r4][:, m, 0, :], tab[r4][:, m, 1, :]),
                             (zhi[r][:, :], zlo[r][:, :]), True, True)
                mm.then_inc(mm_done[r], 1)

            pipeline(pe, GS, [(unit, 0)])

        @block.scalar
        def _(act):
            def high(it, b):
                r, used = at(it, b, 2)
                r4, used4 = at(it, b, 4)
                act.wait_ge(z_in[r4], 16 * used4 + 16)
                after(act, mm_done[r], used)
                nc.scalar.activation(zhi[r][:, :], z[r4][:, :], ACT.Copy).then_inc(hi_done[r], 1)

            def evac(it, b):
                r, used = at(it, b, 2)
                act.wait_ge(mm_done[r], used + 1)
                plain(act, z_in[0], 16)
                nc.scalar.activation(x[:, 0, 4 * it + b, :], ps[r][:, 0, :], ACT.Copy).then_inc(out0[r], 1)

            pipeline(act, GS, [(high, 0), (evac, 1)])

        @block.vector
        def _(dve):
            def low(it, b):
                r, used = at(it, b, 2)
                r4, _ = at(it, b, 4)
                dve.wait_ge(hi_done[r], used + 1)
                after(dve, mm_done[r], used)
                nc.vector.tensor_tensor(zlo[r][:, :], z[r4][:, :], f32(zhi[r][:, :]),
                                        ALU.subtract).then_inc(lo_done[r], 1)

            def evac(it, b):
                r, used = at(it, b, 2)
                dve.wait_ge(mm_done[r], used + 1)
                nc.vector.tensor_copy(x[:, 1, 4 * it + b, :], ps[r][:, 1, :]).then_inc(out1[r], 1)

            pipeline(dve, GS, [(low, 0), (evac, 1)])


def spectrum_product(nc, tag, dft, x, kfreq):
    with Scope(nc, tag) as s:
        a = [s.sb(f"a{b}", [P, 2, DH]) for b in range(2)]
        ahi = [s.sb(f"ahi{b}", [P, 2, DH], F32R) for b in range(2)]
        alo = [s.sb(f"alo{b}", [P, 2, DH], F32R) for b in range(2)]
        kf = [s.sb(f"kf{b}", [P, 2, DH]) for b in range(2)]
        by_re = [s.sb(f"by_re{b}", [P, 2, DH]) for b in range(2)]
        by_im = [s.sb(f"by_im{b}", [P, 2, DH]) for b in range(2)]
        y = [s.sb(f"y{b}", [P, 2, DH]) for b in range(2)]
        yhi = [s.sb(f"yhi{b}", [P, 2, DH], F32R) for b in range(2)]
        ylo = [s.sb(f"ylo{b}", [P, 2, DH], F32R) for b in range(2)]
        out = [s.sb(f"out{b}", [P, 2, DH]) for b in range(2)]
        real = s.sb("real", [1, 2, DH])
        u_ps = [s.ps(f"u{b}", [P, 2, CH]) for b in range(2)]
        b_ps = [s.ps(f"b{b}", [P, 2, CH]) for b in range(2)]
        real_bins = s.sem("real_bins")
        a_in, k_in, ahi_done, alo_done, u_done, mul_done, y_done, yhi_done, ylo_done, b_done, out_done, stored = (
            s.sems(n) for n in ("a_in", "k_in", "ahi_done", "alo_done", "u_done", "mul_done", "y_done", "yhi_done",
                                "ylo_done", "b_done", "out_done", "stored"))
        block = s.block()

        def rows(q, i):
            slot = 2 * q + i
            r = slot % 16
            return x[8 * r:8 * r + 8, slot // 16, :, :]

        @block.sync
        def _(sp):
            def load(q):
                b, it = q % 2, q // 2
                after(sp, alo_done[b], it)
                for i in range(2):
                    sp.dma_start(a[b][:, i, :], rows(q, i)).then_inc(a_in[b], 16)
                after(sp, mul_done[b], 2 * it)
                sp.dma_start(kf[b][:, :, :], kfreq[q, :, :, :]).then_inc(k_in[b], 16)

            def store(q):
                sp.wait_ge(out_done[q % 2], q // 2 + 1)
                for i in range(2):
                    sp.dma_start(rows(q, i), out[q % 2][:, i, :]).then_inc(stored[q % 2], 16)

            load(0)
            load(1)
            for q in range(2, NPAIR):
                load(q)
                if q >= 5:
                    store(q - 5)
            for q in range(NPAIR - 5, NPAIR):
                store(q)
            for b in range(2):
                sp.wait_ge(stored[b], 16 * NPAIR)

        @block.gpsimd
        def _(pool):
            for q in range(NPAIR):
                r, used = q % 2, q // 2
                pool.wait_ge(mul_done[r], 2 * used + 2)
                after(pool, ylo_done[r], used)
                nc.gpsimd.tensor_tensor(y[r][:, 0, :], by_re[r][:, 0, :], by_im[r][:, 1, :],
                                        ALU.subtract).then_inc(y_done[r], 1)
                nc.gpsimd.tensor_tensor(y[r][:, 1, :], by_re[r][:, 1, :], by_im[r][:, 0, :],
                                        ALU.add).then_inc(y_done[r], 1)

        @block.tensor
        def _(pe):
            def first(it, b):
                return isinstance(it, int) and U * it + b == 0

            def fwd(it, b):
                r, used = at(it, b, 2)
                pe.wait_ge(alo_done[r], used + 1)
                after(pe, mul_done[r], 2 * used)
                dft.passes(nc, u_ps[r], ahi[r], alo[r], False, first(it, b)).then_inc(u_done[r], 1)

            def inv(it, b):
                r, used = at(it, b, 2)
                pe.wait_ge(ylo_done[r], used + 1)
                after(pe, out_done[r], used)
                dft.passes(nc, b_ps[r], yhi[r], ylo[r], True, first(it, b)).then_inc(b_done[r], 1)

            pipeline(pe, NPAIR, [(fwd, 0), (inv, 2)])

        @block.scalar
        def _(act):
            def ahigh(it, b):
                r, used = at(it, b, 2)
                act.wait_ge(a_in[r], 32 * used + 32)
                after(act, u_done[r], used)
                nc.scalar.activation(ahi[r][:, :, :], a[r][:, :, :], ACT.Copy).then_inc(ahi_done[r], 1)

            def yhigh(it, b):
                r, used = at(it, b, 2)
                act.wait_ge(y_done[r], 2 * used + 2)
                if isinstance(it, int) and U * it + b == 0:
                    act.wait_ge(real_bins, 2)
                after(act, b_done[r], used)
                nc.scalar.activation(yhi[r][:, :, :], y[r][:, :, :], ACT.Copy).then_inc(yhi_done[r], 1)

            def evac(it, b):
                r, used = at(it, b, 2)
                act.wait_ge(b_done[r], used + 1)
                after(act, stored[r], 32 * used)
                nc.scalar.activation(out[r][:, :, :], b_ps[r][:, :, :], ACT.Copy).then_inc(out_done[r], 1)

            pipeline(act, NPAIR, [(evac, 5), (yhigh, 3), (ahigh, 0)])

        @block.vector
        def _(dve):
            def alow(it, b):
                r, used = at(it, b, 2)
                dve.wait_ge(ahi_done[r], used + 1)
                after(dve, u_done[r], used)
                nc.vector.tensor_tensor(alo[r][:, :, :], a[r][:, :, :], f32(ahi[r][:, :, :]),
                                        ALU.subtract).then_inc(alo_done[r], 1)

            def ylow(it, b):
                r, used = at(it, b, 2)
                dve.wait_ge(yhi_done[r], used + 1)
                after(dve, b_done[r], used)
                nc.vector.tensor_tensor(ylo[r][:, :, :], y[r][:, :, :], f32(yhi[r][:, :, :]),
                                        ALU.subtract).then_inc(ylo_done[r], 1)

            def multiply(it, b):
                r, used = at(it, b, 2)
                dve.wait_ge(u_done[r], used + 1)
                dve.wait_ge(k_in[r], 16 * used + 16)
                after(dve, y_done[r], 2 * used)
                pair0 = isinstance(it, int) and U * it + b == 0
                if pair0:
                    nc.vector.tensor_tensor(real[:, :, :], u_ps[r][0:1, :, :], kf[r][0:1, :, :],
                                            ALU.mult).then_inc(real_bins, 1)
                nc.vector.tensor_tensor(by_re[r][:, :, :], u_ps[r][:, :, :],
                                        kf[r][:, 0:1, :].broadcast_to([P, 2, DH]), ALU.mult).then_inc(mul_done[r], 1)
                nc.vector.tensor_tensor(by_im[r][:, :, :], u_ps[r][:, :, :],
                                        kf[r][:, 1:2, :].broadcast_to([P, 2, DH]), ALU.mult).then_inc(mul_done[r], 1)
                if pair0:
                    dve.wait_ge(real_bins, 1)
                    dve.wait_ge(y_done[r], 2)
                    nc.vector.tensor_copy(y[r][0:1, :, :], real[:, :, :]).then_inc(real_bins, 1)

            pipeline(dve, NPAIR, [(multiply, 2), (ylow, 3), (alow, 0)])


def between_orders(nc, vx, tabs, x):
    with Scope(nc, "mid") as s:
        xhi = [s.sb(f"xhi{b}", [P, 2, DH], F32R) for b in range(4)]
        xlo = [s.sb(f"xlo{b}", [P, 2, DH], F32R) for b in range(4)]
        x1 = [s.sb(f"x1{b}", [P, DH]) for b in range(4)]
        z = [s.sb(f"z{b}", [P, DH]) for b in range(4)]
        zhi = [s.sb(f"zhi{b}", [P, DH], F32R) for b in range(4)]
        zlo = [s.sb(f"zlo{b}", [P, DH], F32R) for b in range(4)]
        itab = [s.sb(f"itab{b}", [P, 2, 2, P], F32R) for b in range(4)]
        ftab = [s.sb(f"ftab{b}", [P, 2, 2, P], F32R) for b in range(4)]
        z_ps = [s.ps(f"zps{b}", [P, CH]) for b in range(2)]
        s_ps = [s.ps(f"sps{b}", [P, 2, CH]) for b in range(2)]
        x1_in, itab_in, ftab_in, xhi_done, xlo_done, inv_done, z_done, zhi_done, zlo_done, fwd_done, out0, out1 = (
            s.sems(n, 4) for n in ("x1_in", "itab_in", "ftab_in", "xhi_done", "xlo_done", "inv_done", "z_done",
                                   "zhi_done", "zlo_done", "fwd_done", "out0", "out1"))
        block = s.block()

        @block.sync
        def _(sp):
            def load(it, b):
                r, used = at(it, b, 4)
                after(sp, z_done[r], used)
                sp.dma_start(f32(itab[r][:, :, :, :]), tabs["iw1"][4 * it + b, :, :, :, :]).then_inc(itab_in[r], 16)
                sp.dma_start(x1[r][:, :], vx[:, 4 * it + b, DH:2 * DH]).then_inc(x1_in[r], 16)
                after(sp, fwd_done[r], used)
                sp.dma_start(f32(ftab[r][:, :, :, :]), tabs["w1s"][4 * it + b, :, :, :, :]).then_inc(ftab_in[r], 16)

            pipeline(sp, GS, [(load, 0)])

        @block.gpsimd
        def _(pool):
            for g in range(GS):
                r, used = g % 4, g // 4
                pool.wait_ge(xhi_done[r], used + 1)
                after(pool, inv_done[r], used)
                nc.gpsimd.tensor_tensor(xlo[r][:, :, :], x[:, :, g, :], f32(xhi[r][:, :, :]),
                                        ALU.subtract).then_inc(xlo_done[r], 1)

        @block.tensor
        def _(pe):
            def inv(it, b):
                r, used = at(it, b, 4)
                before, used_before = at(it, b - 2, 4)
                pe.wait_ge(xlo_done[r], used + 1)
                pe.wait_ge(itab_in[r], 16 * used + 16)
                after(pe, z_done[before], used_before + 1)
                for m in range(2):
                    mm = mm3(nc, z_ps[b % 2][:, :], (itab[r][:, m, 0, :], itab[r][:, m, 1, :]),
                             (xhi[r][:, m, :], xlo[r][:, m, :]), m == 0, m == 1)
                mm.then_inc(inv_done[r], 1)

            def fwd(it, b):
                r, used = at(it, b, 4)
                before, used_before = at(it, b - 2, 4)
                pe.wait_ge(zlo_done[r], used + 1)
                pe.wait_ge(ftab_in[r], 16 * used + 16)
                after(pe, out0[before], used_before + 1)
                after(pe, out1[before], used_before + 1)
                for m in range(2):
                    mm = mm3(nc, s_ps[b % 2][:, m, :], (ftab[r][:, m, 0, :], ftab[r][:, m, 1, :]),
                             (zhi[r][:, :], zlo[r][:, :]), True, True)
                mm.then_inc(fwd_done[r], 1)

            pipeline(pe, GS, [(inv, 0), (fwd, 3)])

        @block.scalar
        def _(act):
            def xhigh(it, b):
                r, used = at(it, b, 4)
                after(act, inv_done[r], used)
                if not isinstance(it, int):
                    plain(act, z_done[0], 1)
                nc.scalar.activation(xhi[r][:, :, :], x[:, :, 4 * it + b, :], ACT.Copy).then_inc(xhi_done[r], 1)

            def zhigh(it, b):
                r, used = at(it, b, 4)
                act.wait_ge(z_done[r], used + 1)
                after(act, fwd_done[r], used)
                nc.scalar.activation(zhi[r][:, :], z[r][:, :], ACT.Copy).then_inc(zhi_done[r], 1)

            def evac(it, b):
                r, used = at(it, b, 4)
                act.wait_ge(fwd_done[r], used + 1)
                plain(act, z_done[0], 1)
                nc.scalar.activation(x[:, 0, 4 * it + b, :], s_ps[b % 2][:, 0, :], ACT.Copy).then_inc(out0[r], 1)

            pipeline(act, GS, [(xhigh, 0), (zhigh, 2), (evac, 4)])

        @block.vector
        def _(dve):
            def gate(it, b):
                r, used = at(it, b, 4)
                dve.wait_ge(inv_done[r], used + 1)
                dve.wait_ge(x1_in[r], 16 * used + 16)
                after(dve, zlo_done[r], used)
                nc.vector.tensor_tensor(z[r][:, :], z_ps[b % 2][:, :], x1[r][:, :], ALU.mult).then_inc(z_done[r], 1)

            def zlow(it, b):
                r, used = at(it, b, 4)
                dve.wait_ge(zhi_done[r], used + 1)
                after(dve, fwd_done[r], used)
                nc.vector.tensor_tensor(zlo[r][:, :], z[r][:, :], f32(zhi[r][:, :]),
                                        ALU.subtract).then_inc(zlo_done[r], 1)

            def evac(it, b):
                r, used = at(it, b, 4)
                dve.wait_ge(fwd_done[r], used + 1)
                nc.vector.tensor_copy(x[:, 1, 4 * it + b, :], s_ps[b % 2][:, 1, :]).then_inc(out1[r], 1)

            pipeline(dve, GS, [(gate, 1), (zlow, 2), (evac, 4)])


def last_inverse(nc, t, tabs, x, g2, rows, ya, whl, gate_bias):
    with Scope(nc, "fin") as s:
        xhi = [s.sb(f"xhi{b}", [P, 2, DH], F32R) for b in range(2)]
        xlo = [s.sb(f"xlo{b}", [P, 2, DH], F32R) for b in range(2)]
        tab = [s.sb(f"tab{b}", [P, 2, 2, P], F32R) for b in range(4)]
        wf = [s.sb(f"wf{b}", [P, D]) for b in range(2)]
        gate = s.sb("gate", [P, D])
        eye = s.sb("eye", [P, P])
        z = [s.sb(f"z{b}", [P, DH]) for b in range(2)]
        z_ps = [s.ps(f"zps{b}", [P, CH]) for b in range(2)]
        t_ps = [s.ps(f"tps{b}", [P, 4, P]) for b in range(2)]
        eye_in, y_in, gate_in = s.sem("eye_in"), s.sem("y_in"), s.sem("gate_in")
        z_done, tr_done = s.sems("z_done"), s.sems("tr_done")
        tab_in = s.sems("tab_in", 4)
        hi_done, lo_done, mm_done, y_done, w_in, w_scaled, whi_done, wlo_done = (
            s.sems(n) for n in ("hi_done", "lo_done", "mm_done", "y_done", "w_in", "w_scaled", "whi_done", "wlo_done"))
        block = s.block()
        yg = ya[:, :, :].rearrange("p k (c g) -> p k c g", g=GS)

        @block.sync
        def _(sp):
            def load(it, b):
                slot, _ = at(it, b, 4)
                two, used = at(it, b - 4, 2)
                if not (isinstance(it, int) and it == 0):
                    after(sp, mm_done[two], used + 1)
                sp.dma_start(f32(tab[slot][:, :, :, :]), tabs["iw1"][4 * it + b, :, :, :, :]).then_inc(tab_in[slot], 16)
                if b % 2:
                    r = b // 2
                    after(sp, wlo_done[r], it)
                    row = 2 * P * it + r * P
                    src = t["w_out"][0, row:row + P, :] if isinstance(it, int) else t["w_out"][0, bass.ds(row, P), :]
                    sp.dma_start(wf[r][:, :], src).then_inc(w_in[r], 16)

            pipeline(sp, GS, [(load, 0)])

        @block.tensor
        def _(pe):
            def inv(it, b):
                r, used = at(it, b, 2)
                r4, used4 = at(it, b, 4)
                pe.wait_ge(lo_done[r], used + 1)
                pe.wait_ge(tab_in[r4], 16 * used4 + 16)
                after(pe, z_done[r], used)
                for m in range(2):
                    mm = mm3(nc, z_ps[r][:, :], (tab[r4][:, m, 0, :], tab[r4][:, m, 1, :]),
                             (xhi[r][:, m, :], xlo[r][:, m, :]), m == 0, m == 1)
                mm.then_inc(mm_done[r], 1)

            def turn(it, b):
                r, used = at(it, b, 2)
                pe.wait_ge(z_done[r], used + 1)
                after(pe, y_done[r], used)
                for k in range(4):
                    mm = nc.tensor.transpose(t_ps[r][:, k, :], z[r][:, k * P:(k + 1) * P], eye[:, :])
                mm.then_inc(tr_done[r], 1)

            pe.wait_ge(eye_in, 16)
            pipeline(pe, GS, [(inv, 0), (turn, 2)])

        @block.scalar
        def _(act):
            act.dma_start(eye[:, :], t["t_eye"][:, :]).then_inc(eye_in, 16)
            act.dma_start(ya[:, :, :], g2.rearrange("k p t -> p k t")).then_inc(y_in, 16)
            act.dma_start(gate[:, :], rows[0, :].partition_broadcast(P)).then_inc(gate_in, 16)
            act.dma_start(gate_bias[:, :], rows[1, :].partition_broadcast(P)).then_inc(gate_in, 16)

            def high(it, b):
                r, used = at(it, b, 2)
                after(act, mm_done[r], used)
                if not isinstance(it, int):
                    plain(act, y_in, 16)
                nc.scalar.activation(xhi[r][:, :, :], x[:, :, 4 * it + b, :], ACT.Copy).then_inc(hi_done[r], 1)

            def evac(it, b):
                r, used = at(it, b, 2)
                act.wait_ge(mm_done[r], used + 1)
                after(act, tr_done[r], used)
                nc.scalar.activation(z[r][:, :], z_ps[r][:, :], ACT.Copy).then_inc(z_done[r], 1)

            def whigh(it, b):
                if b % 2 == 1:
                    r = (b % U) // 2
                    k = it + b // U
                    act.wait_ge(w_scaled[r], k + 1)
                    plain(act, y_in, 16)
                    nc.scalar.activation(whl[:, 0, 2 * k + r, :], wf[r][:, :], ACT.Copy).then_inc(whi_done[r], 1)

            pipeline(act, GS, [(evac, 2), (high, 0), (whigh, 4)])
            act.wait_ge(gate_in, 32)

        @block.gpsimd
        def _(pool):
            for k in range(KT):
                r = k % 2
                pool.wait_ge(whi_done[r], k // 2 + 1)
                nc.gpsimd.tensor_tensor(whl[:, 1, k, :], wf[r][:, :], f32(whl[:, 0, k, :]),
                                        ALU.subtract).then_inc(wlo_done[r], 1)

        @block.vector
        def _(dve):
            def low(it, b):
                r, used = at(it, b, 2)
                dve.wait_ge(hi_done[r], used + 1)
                after(dve, mm_done[r], used)
                nc.vector.tensor_tensor(xlo[r][:, :, :], x[:, :, 4 * it + b, :], f32(xhi[r][:, :, :]),
                                        ALU.subtract).then_inc(lo_done[r], 1)

            def gated(it, b):
                r, used = at(it, b, 2)
                dve.wait_ge(tr_done[r], used + 1)
                dve.wait_ge(y_in, 16)
                g = 4 * it + b
                nc.vector.tensor_tensor(yg[:, :, :, g], t_ps[r][:, :, :], yg[:, :, :, g], ALU.mult).then_inc(y_done[r], 1)

            def wscale(it, b):
                if b % 2 == 1:
                    r = (b % U) // 2
                    k = it + b // U
                    dve.wait_ge(w_in[r], 16 * k + 16)
                    dve.wait_ge(gate_in, 32)
                    nc.vector.tensor_tensor(wf[r][:, :], wf[r][:, :], gate[:, :], ALU.mult).then_inc(w_scaled[r], 1)

            pipeline(dve, GS, [(low, 0), (wscale, 2), (gated, 3)])



def output_norm(nc, t, ya, yp, whl, gate_bias, out):
    with Scope(nc, "out") as s:
        yb = s.sb("yb", [P, 4, L])
        yhi = [s.sb(f"yhi{b}", [P, KT, P], F32R) for b in range(2)]
        ylo = [s.sb(f"ylo{b}", [P, KT, P], F32R) for b in range(2)]
        x = [s.sb(f"x{b}", [P, D]) for b in range(2)]
        res = [s.sb(f"res{b}", [P, D]) for b in range(2)]
        o = [s.sb(f"o{b}", [P, D]) for b in range(2)]
        ln_g = s.sb("ln_g", [P, D])
        ln_b = s.sb("ln_b", [P, D])
        stats = [s.sb(f"stats{b}", [P, 2, 6]) for b in range(2)]
        mv = [s.sb(f"mv{b}", [P, 2]) for b in range(2)]
        sm = [s.sb(f"sm{b}", [P, 4]) for b in range(2)]
        eps = s.sb("eps", [P, 1])
        ps = [s.ps(f"ps{b}", [P, 2, CH]) for b in range(2)]
        consts, eps_set = s.sem("consts"), s.sem("eps_set")
        yb_in = s.sems("yb_in", 4)
        x_in, hi_done, lo_done, mm_done, step, sum_done, var_done, root_done, norm_done, scaled, o_done, stored = (
            s.sems(n) for n in ("x_in", "hi_done", "lo_done", "mm_done", "step", "sum_done", "var_done",
                                "root_done", "norm_done", "scaled", "o_done", "stored"))
        block = s.block()

        @block.sync
        def _(sp):
            for c in range(4):
                cols = slice(c * CH, (c + 1) * CH)
                sp.dma_start(yb[:, :, cols], yp[:, :, cols].rearrange("k p t -> p k t")).then_inc(yb_in[c], 16)

            def load(it, b):
                r, used = at(it, b, 2)
                after(sp, sum_done[r], used)
                row = P * (U * it + b)
                src = t["x"][0, row:row + P, :] if isinstance(it, int) else t["x"][0, bass.ds(row, P), :]
                sp.dma_start(x[r][:, :], src).then_inc(x_in[r], 16)

            def store(it, b):
                r, used = at(it, b, 2)
                sp.wait_ge(o_done[r], used + 1)
                row = P * (U * it + b)
                dst = out[0, row:row + P, :] if isinstance(it, int) else out[0, bass.ds(row, P), :]
                sp.dma_start(dst, o[r][:, :]).then_inc(stored[r], 16)

            pipeline(sp, GS, [(load, 0), (store, 2)])
            for r in range(2):
                sp.wait_ge(stored[r], 16 * GS // 2)

        @block.tensor
        def _(pe):
            def unit(it, b):
                r, used = at(it, b, 2)
                pe.wait_ge(lo_done[r], used + 1)
                after(pe, sum_done[r], used)
                for h in range(2):
                    cols = slice(h * CH, (h + 1) * CH)
                    for k in range(KT):
                        mm = mm3(nc, ps[r][:, h, :], (yhi[r][:, k, :], ylo[r][:, k, :]),
                                 (whl[:, 0, k, cols], whl[:, 1, k, cols]), k == 0, k == KT - 1)
                mm.then_inc(mm_done[r], 1)

            pipeline(pe, GS, [(unit, 0)])

        @block.scalar
        def _(act):
            act.dma_start(ln_g[:, :], t["ln_g"][0, :].partition_broadcast(P)).then_inc(consts, 16)
            act.dma_start(ln_b[:, :], t["ln_b"][0, :].partition_broadcast(P)).then_inc(consts, 16)

            def high(it, b):
                r, used = at(it, b, 2)
                cols = bass.ds(P * (U * it + b), P)
                if isinstance(it, int):
                    if (U * it + b) % 4 == 0:
                        act.wait_ge(yb_in[it], 16)
                    after(act, mm_done[r], used)
                else:
                    act.wait_ge(mm_done[r], used)
                    plain(act, yb_in[3], 16)
                nc.scalar.activation(yhi[r][:, 0:4, :], ya[:, :, cols], ACT.Copy)
                nc.scalar.activation(yhi[r][:, 4:8, :], yb[:, :, cols], ACT.Copy).then_inc(hi_done[r], 1)

            def root(it, b):
                r, used = at(it, b, 2)
                act.wait_ge(var_done[r], used + 1)
                nc.scalar.activation(sm[r][:, 0:1], mv[r][:, 1:2], ACT.Sqrt, bias=eps[:, 0:1]).then_inc(root_done[r], 1)

            act.wait_ge(eps_set, 1)
            pipeline(act, GS, [(high, 0), (root, 2)])

        @block.gpsimd
        def _(pool):
            nc.gpsimd.memset(eps[:, :], LN_EPS).then_inc(eps_set, 1)
            pool.wait_ge(eps_set, 1)
            pool.wait_ge(consts, 32)
            for n in range(GS):
                b, it = n % 2, n // 2
                pool.wait_ge(norm_done[b], it + 1)
                after(pool, stored[b], 16 * it)
                nc.gpsimd.tensor_tensor(o[b][:, :], res[b][:, :], ln_g[:, :], ALU.mult).then_inc(scaled[b], 1)
                pool.wait_ge(scaled[b], it + 1)
                nc.gpsimd.tensor_tensor(o[b][:, :], o[b][:, :], ln_b[:, :], ALU.add).then_inc(o_done[b], 1)

        @block.vector
        def _(dve):
            def low(it, b):
                r, used = at(it, b, 2)
                cols = bass.ds(P * (U * it + b), P)
                dve.wait_ge(hi_done[r], used + 1)
                after(dve, mm_done[r], used)
                nc.vector.tensor_tensor(ylo[r][:, 0:4, :], ya[:, :, cols], f32(yhi[r][:, 0:4, :]), ALU.subtract)
                nc.vector.tensor_tensor(ylo[r][:, 4:8, :], yb[:, :, cols],
                                        f32(yhi[r][:, 4:8, :]), ALU.subtract).then_inc(lo_done[r], 1)

            def norm(it, b):
                r, used = at(it, b, 2)
                STEPS = 7
                n = STEPS * used
                done = [0]

                def then(ins):
                    ins.then_inc(step[r], 1)
                    done[0] += 1
                    dve.wait_ge(step[r], n + done[0])

                dve.wait_ge(mm_done[r], used + 1)
                dve.wait_ge(x_in[r], 16 * used + 16)
                after(dve, scaled[r], used)
                nc.vector.scalar_tensor_tensor(out=res[r][:, :], in0=x[r][:, :], scalar=ALPHA,
                                               in1=ps[r][:, :, :].rearrange("p a b -> p (a b)"),
                                               op0=ALU.mult, op1=ALU.add).then_inc(sum_done[r], 1)
                dve.wait_ge(sum_done[r], used + 1)
                then(nc.vector.tensor_tensor(res[r][:, :], res[r][:, :], gate_bias[:, :], ALU.add))
                for h in range(2):
                    ins = nc.vector.bn_stats(stats[r][:, h, :], res[r][:, h * CH:(h + 1) * CH])
                then(ins)
                nc.vector.memset(sm[r][:, 2:4], 0.0)
                nc.vector.bn_aggr(mv[r][:, :], stats[r][:, :, :].rearrange("p a b -> p (a b)")).then_inc(var_done[r], 1)
                dve.wait_ge(root_done[r], used + 1)
                then(nc.vector.reciprocal(sm[r][:, 1:2], sm[r][:, 0:1]))
                then(nc.vector.tensor_scalar(sm[r][:, 2:3], mv[r][:, 1:2], LN_EPS, sm[r][:, 1:2], ALU.add, ALU.mult))
                then(nc.vector.tensor_tensor(sm[r][:, 2:3], sm[r][:, 2:3], sm[r][:, 1:2], ALU.mult))
                then(nc.vector.tensor_scalar(sm[r][:, 2:3], sm[r][:, 2:3], -0.5, 1.5, ALU.mult, ALU.add))
                then(nc.vector.tensor_tensor(sm[r][:, 3:4], sm[r][:, 2:3], sm[r][:, 1:2], ALU.mult))
                assert done[0] == STEPS
                nc.vector.tensor_scalar(res[r][:, :], res[r][:, :], mv[r][:, 0:1], sm[r][:, 3:4],
                                        ALU.subtract, ALU.mult).then_inc(norm_done[r], 1)

            pipeline(dve, GS, [(norm, 2), (low, 0)])


def encoder_layer(nc, t, out):
    def scratch(name, shape):
        return nc.dram_tensor(name, shape, F32, kind="Internal").ap()

    kfreq = scratch("kfreq", [2, NPAIR, P, 2, DH])
    vx = scratch("vx", [P, GS, 2 * DH])
    g2 = scratch("g2", [4, P, L])
    yp = scratch("yp", [4, P, L])
    rows = scratch("rows", [2, D])
    tabs = {n: scratch("own_" + n, list(t["t_" + n].shape)) for n in ("w1f", "w1s", "iw1", "dft", "f0", "i0")}

    with Scope(nc, "all") as s:
        scale1 = s.sb("scale1", [P, KT])
        shift = s.sb("shift", [P, KT])
        with Scope(nc, "flt") as f:
            with nc.sbuf_tensor("hfil", [P, 2, P, GF], F32R, side="right") as hfil:
                front(nc, t, hfil, tabs, scale1, shift, rows)
                xf = f.sb("xf", [P, 2, GF, DH])
                filter_stage1(nc, t, tabs, hfil, xf)
            filter_stage2(nc, tabs, xf, kfreq)
        with Scope(nc, "u") as u:
            eye = u.sb("eye", [P, P])
            uhi = u.sb("uhi", [P, KT, L], F32R)
            ulo = u.sb("ulo", [P, KT, L], F32R)
            transpose_input(nc, t, scale1, shift, uhi, ulo, eye)
            project(nc, t, tabs, uhi, ulo, eye, vx, g2, yp)
        x_scope = Scope(nc, "x")
        x = x_scope.sb("x", [P, 2, GS, DH])
        with Scope(nc, "spec") as spec:
            dft = Dft(spec)
            signal_stage1(nc, vx, tabs, dft, x)
            spectrum_product(nc, "sp0", dft, x, kfreq[0])
            between_orders(nc, vx, tabs, x)
            spectrum_product(nc, "sp1", dft, x, kfreq[1])
        with (nc.sbuf_tensor("ya", [P, 4, L], F32, side="right") as ya,
              nc.sbuf_tensor("whl", [P, 2, KT, D], F32R, side="right") as whl,
              nc.sbuf_tensor("gate_bias", [P, D], F32, side="right") as gate_bias):
            last_inverse(nc, t, tabs, x, g2, rows, ya, whl, gate_bias)
            x_scope.ctx.close()
            output_norm(nc, t, ya, yp, whl, gate_bias, out)


_INS = ["x", "c", "w_ada", "b_ada", "w_in", "b_in", "conv_w", "conv_b", "filt_w1", "filt_b1", "filt_w_inner",
        "filt_b_inner", "filt_w_out", "filt_freq", "hyena_bias", "pool_w", "pool_scale", "w_out", "b_out",
        "ln_g", "ln_b"]


def kernel(**inputs):
    import numpy as _np
    import concourse.bacc as _bacc
    from concourse import mybir as _mybir
    from concourse.bass_utils import run_bass_kernel_spmd as _run

    nc = _bacc.Bacc("TRN2", target_bir_lowering=False, num_devices=1)
    arrays, args = {}, {}
    given = {name: _np.ascontiguousarray(inputs[name]) for name in _INS}
    for name, a in {**given, **shape_tables()}.items():
        arrays[f"in_{name}"] = a
        args[name] = nc.dram_tensor(f"in_{name}", a.shape, _mybir.dt.from_np(a.dtype), kind="ExternalInput").ap()
    out = nc.dram_tensor("out_0", (1, L, D), _mybir.dt.float32, kind="ExternalOutput").ap()
    encoder_layer(nc, args, out)
    r = _run(nc, [arrays], core_ids=[0])
    return r.results[0]["out_0"]
```

```python
from contextlib import ExitStack
import math

import numpy as np

import concourse.bass as bass
from concourse import mybir

F32 = mybir.dt.float32
F32R = mybir.dt.float32r
ALU = mybir.AluOpType
ACT = mybir.ActivationFunctionType

P = 128
D = 1024
L = 2048
DH = 512
NF = 2 * L
N1 = 32
KT = D // P
PROJ = 3 * DH + DH + 2 * DH
EMB, HID = 33, 64
GS = L // P
GF = NF // P
NPAIR = N1 // 2
CH = 512
ALPHA = 2.0 ** 0.25
LN_EPS = 1e-5
WINDOWS = (2, 4, 8, 16)
POOL_STEPS = [sum(w.bit_length() - 1 + (3 if w > 2 else 2) for w in WINDOWS[:i + 1]) for i in range(4)]
PAD = 8



def _round12(a):
    b = np.ascontiguousarray(a, np.float32).view(np.uint32)
    b = (b + np.uint32(0x7FF) + ((b >> np.uint32(12)) & np.uint32(1))) & np.uint32(0xFFFFF000)
    return b.view(np.float32)


def _hilo(a, axis):
    hi = _round12(a)
    lo = _round12(np.asarray(a, np.float64) - hi)
    return np.ascontiguousarray(np.stack([hi, lo], axis=axis))


def shape_tables():
    tau = 2 * np.pi

    def row(slot, t1, t2):
        q = slot // 2
        ang = tau * ((q * (P * t1 + t2)) % NF) / NF
        v = np.where(slot % 2 == 0, np.cos(ang), -np.sin(ang))
        return np.where(slot == 0, 1.0, np.where(slot == 1, 1.0 - 2.0 * (t1 % 2), v))

    p = np.arange(P)
    g = np.arange(GF)[:, None, None]
    v = row(p[None, None, :] // 4, p[None, :, None] // 4, 32 * (p[None, :, None] % 4) + g)
    same = (p[:, None] % 4) == (p[None, :] % 4)
    w1f = _hilo(v * same[None], 2)
    g = np.arange(GS)[:, None, None]
    same = (p[:, None] % 8) == (p[None, :] % 8)
    halves = []
    for m in range(2):
        v = row(16 * m + p[None, None, :] // 8, p[None, :, None] // 8, 16 * (p[None, :, None] % 8) + g)
        halves.append(v * same[None])
    w1s = _hilo(np.stack(halves, 2), 3)
    iw1 = _hilo(np.stack([h.transpose(0, 2, 1) for h in halves], 2) * (2.0 / NF), 3)
    ang = tau * ((p[:, None] * p[None, :]) % P) / P
    dft = _hilo(np.stack([np.cos(ang), np.sin(ang), -np.sin(ang)], 1), 2)
    j = np.arange(64)
    f0 = np.zeros((P, 4, P))
    a0 = tau * ((p[:, None] * j) % P) / P
    a16 = tau * ((p[:, None] * (16 + 32 * j)) % NF) / NF
    f0[:, 0, :64] = np.cos(a0)
    f0[:, 1, :64] = -np.sin(a0)
    f0[:, 1, 0] = 1.0 - 2.0 * (p % 2)
    f0[:, 2, 64:] = np.cos(a16)
    f0[:, 3, 64:] = -np.sin(a16)
    inv = np.zeros((P, 4, P))
    for i in range(2):
        for o in range(2):
            inv[:, o * 2 + i, :] = f0[:, i * 2 + o, :].T
    inv[0] *= 0.5
    f32 = np.float32
    t = np.linspace(0.0, 1.0, L, dtype=f32)[:, None]
    bands = (EMB - 1) // 2
    w = f32(2.0 * math.pi / L) * np.arange(L, dtype=f32)[:, None]
    f = np.linspace(1e-4, bands - 1, bands, dtype=f32)[None, :]
    fw = (f * w).astype(np.float64)
    z = np.concatenate([t, np.cos(fw), -np.sin(fw)], axis=-1).astype(f32)
    z2 = np.ascontiguousarray(np.concatenate([z.T, z[::-1].T], 0))
    deltas = np.linspace(math.log(1e-2) / 1.5, math.log(1e-2) / 0.3, DH, dtype=f32)
    dec = np.exp((-t * np.abs(deltas)[None, :]).astype(np.float64)).astype(f32)
    dec = np.concatenate([dec, dec[::-1]], 0).reshape(P, GF, DH).transpose(1, 0, 2)
    edge = np.ones((4, 2, PAD))
    for gi, win in enumerate(WINDOWS):
        h = win // 2
        for i in range(h):
            edge[gi, 0, i] = win / (i + h)
        for i in range(h - 1):
            edge[gi, 1, PAD - 1 - i] = win / (1 + i + h)
    return {
        "t_w1f": w1f, "t_w1s": w1s, "t_iw1": iw1, "t_dft": dft,
        "t_f0": _hilo(f0, 2), "t_i0": _hilo(inv, 2), "t_z": z2,
        "t_decay": np.ascontiguousarray(dec),
        "t_edge": np.ascontiguousarray(edge, f32), "t_eye": np.eye(P, dtype=f32),
    }



def mm3(nc, out, w, m, start, stop):
    nc.tensor.matmul(out, w[0], m[0], start=start, stop=False, skip_group_check=True)
    nc.tensor.matmul(out, w[0], m[1], start=False, stop=False, skip_group_check=True)
    return nc.tensor.matmul(out, w[1], m[0], start=False, stop=stop, skip_group_check=True)


def f32(ap):
    return ap.bitcast(F32)


def plain(eng, sem, value):
    eng.wait_ge(sem, value)


def after(eng, sem, count):
    if not (isinstance(count, int) and count <= 0):
        eng.wait_ge(sem, count)


U = 4
FIRST_TABS = U


def at(it, b, ring):
    it, b = it + b // U, b % U
    return b % ring, (U // ring) * it + b // ring


def pipeline(eng, units, steps, peel=(0,)):
    bodies = units // U
    steps = [step if len(step) == 3 else (*step, 2) for step in steps]
    first = max(1, *(-(-(lag + start) // U) for _, lag, start in steps))
    steps = [step[:2] for step in steps]

    def body(it, count=U):
        for b in range(count):
            for step, lag in steps:
                if not isinstance(it, int) or 0 <= U * it + b - lag < units:
                    step(it, b - lag)

    it = 0
    while it < bodies:
        if it < first or it in peel:
            body(it)
            it += 1
            continue
        end = min([p for p in peel if p > it] + [bodies])
        with eng.Fori(it, end) as i:
            body(i)
        it = end
    body(bodies, max(lag for _, lag in steps))


class Scope:

    def __init__(self, nc, tag):
        self.nc, self.tag, self.ctx, self.semaphores = nc, tag, ExitStack(), []

    def __enter__(self):
        return self

    def __exit__(self, *a):
        self.ctx.__exit__(*a)
        if self.semaphores:
            self.nc.clear_and_free_semaphores(self.semaphores)
            self.nc.all_engine_barrier()

    def sb(self, name, shape, dt=F32):
        return self.ctx.enter_context(self.nc.sbuf_tensor(f"{self.tag}_{name}", shape, dt))

    def ps(self, name, shape):
        return self.ctx.enter_context(self.nc.psum_tensor(f"{self.tag}_{name}", shape, F32))

    def sem(self, name):
        self.semaphores.append(self.nc.alloc_semaphore(f"{self.tag}_{name}"))
        return self.semaphores[-1]

    def sems(self, name, n=2):
        return [self.sem(f"{name}{i}") for i in range(n)]

    def block(self):
        return self.ctx.enter_context(self.nc.Block())



def front(nc, t, hfil, wfil, tabs, scale1, shift, rows):
    MAGIC = 1.5 * 2.0 ** 23
    C1 = 6.28125
    C2 = 2 * math.pi - C1
    PI = 3.1415925
    HL = L // 2
    with Scope(nc, "net") as s:
        feat = s.sb("feat", [P, L])
        wl = s.sb("wl", [P, 3, P])
        cols = s.sb("cols", [P, 4])
        arg = s.sb("arg", [P, 2, HL])
        turn = s.sb("turn", [P, 2, HL])
        h = s.sb("h", [P, 2, HL])
        wa = s.sb("wa", [P, KT, 3 * D])
        acc = s.sb("acc", [P, 2 * D])
        wraw = s.sb("wraw", [P, 2, DH])
        c_in = s.sb("c_in", [P, KT])
        c_silu = s.sb("c_silu", [P, KT])
        b_cols = s.sb("b_cols", [P, 16])
        b_gate = s.sb("b_gate", [1, D])
        b_out = s.sb("b_out", [1, D])
        gate = s.sb("gate", [1, 2, D])
        ones = s.sb("ones", [P, 1])
        ps = s.ps("ps", [P, 4, CH])
        ps_cols = s.ps("ps_cols", [P, 16])
        ps_gate = s.ps("ps_gate", [P, 2, CH])
        zeroed, loaded, step, split_hi, split_lo, copied = (
            s.sem(n) for n in ("zeroed", "loaded", "step", "split_hi", "split_lo", "copied"))
        lin_done, arg_done, turn_done, fold_done, sin_done = (
            s.sems(n) for n in ("lin_done", "arg_done", "turn_done", "fold_done", "sin_done"))
        w_in, g_in = s.sems("w_in", KT), s.sems("g_in")
        wraw_in, whi_done, wlo_done = (s.sem(n) for n in ("wraw_in", "whi_done", "wlo_done"))
        c_loaded, b_loaded, silu_done, acc_done, sum_done, cols_done, gate_done, prod_done, rows_out = (
            s.sem(n) for n in ("c_loaded", "b_loaded", "silu_done", "acc_done", "sum_done", "cols_done",
                               "gate_done", "prod_done", "rows_out"))
        block = s.block()
        psf = ps[:, :, :].rearrange("p (a c) b -> p a (c b)", a=2)

        @block.sync
        def _(sp):
            sp.dma_start(feat[0:2 * EMB, :], t["t_z"][:, :]).then_inc(loaded, 16)
            with nc.allow_non_contiguous_dma(reason="columns of small vectors"):
                for half in range(2):
                    hs = slice(64 * half, 64 * half + 64)
                    for c, src in ((0, t["filt_b1"]), (3, t["filt_freq"])):
                        sp.dma_start(cols[hs, c:c + 1], src.rearrange("o p -> p o")).then_inc(loaded, 16)
                    sp.dma_start(cols[hs, 1:3], t["filt_b_inner"][0, :, :].rearrange("i p -> p i")).then_inc(loaded, 16)
            sp.wait_ge(zeroed, 1)
            for half in range(2):
                hs = slice(64 * half, 64 * half + 64)
                sp.dma_start(wl[EMB * half:EMB * half + EMB, 0, hs], t["filt_w1"][0, :, :]).then_inc(loaded, 16)
                sp.dma_start(wl[hs, 1:3, hs], t["filt_w_inner"][0, :, :, :].rearrange("i a b -> a i b")).then_inc(loaded, 16)
            for k in range(KT):
                sp.dma_start(wa[:, k, 0:2 * D], t["w_ada"][0, k * P:(k + 1) * P, 0:2 * D]).then_inc(w_in[k], 16)
            osrc = t["filt_w_out"][0, :, :].rearrange("f (o r d) -> f o r d", o=2, r=2)
            for r in range(2):
                sp.dma_start(wraw[64 * r:64 * r + 64, :, :], osrc[:, :, r, :]).then_inc(wraw_in, 16)
            wsrc = t["w_ada"][0, :, :].rearrange("(k p) n -> p k n", p=P)
            for q in range(2):
                cols_q = slice(2 * D + q * CH, 2 * D + (q + 1) * CH)
                sp.dma_start(wa[:, :, cols_q], wsrc[:, :, cols_q]).then_inc(g_in[q], 16)
            with nc.allow_non_contiguous_dma(reason="columns of small vectors"):
                sp.dma_start(b_cols[:, :], t["b_ada"][0, 0:2 * D].rearrange("(k p) -> p k", p=P)).then_inc(b_loaded, 16)
            sp.dma_start(b_gate[:, :], t["b_ada"][:, 2 * D:3 * D]).then_inc(b_loaded, 16)
            sp.dma_start(b_out[:, :], t["b_out"]).then_inc(b_loaded, 16)
            sp.dma_start(tabs["w1f"][0:FIRST_TABS], t["t_w1f"][0:FIRST_TABS]).then_inc(copied, 16)
            sp.wait_ge(prod_done, 1)
            sp.wait_ge(gate_done, 1)
            sp.dma_start(rows, gate[:, :, :]).then_inc(rows_out, 16)
            sp.wait_ge(rows_out, 16)
            sp.wait_ge(copied, 16)

        @block.gpsimd
        def _(pool):
            nc.gpsimd.memset(wl[:, :, :], 0.0).then_inc(zeroed, 1)
            pool.wait_ge(zeroed, 1)
            nc.gpsimd.memset(f32(hfil[0:64, :, 64:128, :]), 0.0).then_inc(zeroed, 1)
            pool.wait_ge(zeroed, 2)
            nc.gpsimd.memset(f32(hfil[64:128, :, 0:64, :]), 0.0).then_inc(zeroed, 1)
            pool.wait_ge(zeroed, 3)
            nc.gpsimd.memset(ones[:, :], 1.0).then_inc(zeroed, 1)
            pool.wait_ge(whi_done, 1)
            nc.gpsimd.tensor_tensor(wfil[:, 1, :, :], wraw[:, :, :], f32(wfil[:, 0, :, :]),
                                    ALU.subtract).then_inc(wlo_done, 1)
            pool.wait_ge(wlo_done, 1)

        @block.tensor
        def _(pe):
            def layer_product(layer):
                src, k = (feat, 2 * EMB) if layer == 0 else (h[:, :, :].rearrange("p a b -> p (a b)"), P)
                for a in range(2):
                    if layer:
                        pe.wait_ge(sin_done[a], layer)
                    for c in range(2 * a, 2 * a + 2):
                        mm = nc.tensor.matmul(ps[:, c, :], wl[0:k, layer, :], src[0:k, c * CH:(c + 1) * CH],
                                              start=True, stop=True)
                    mm.then_inc(lin_done[a], 1)

            def gate_product(q):
                pe.wait_ge(g_in[q], 16)
                for k in range(KT):
                    mm = nc.tensor.matmul(ps_gate[0:1, q, :], c_silu[:, k:k + 1],
                                          wa[:, k, 2 * D + q * CH:2 * D + (q + 1) * CH], start=k == 0, stop=k == KT - 1)
                mm.then_inc(sum_done, 1)

            pe.wait_ge(loaded, 11 * 16)
            layer_product(0)
            layer_product(1)
            layer_product(2)
            pe.wait_ge(silu_done, 1)
            gate_product(0)
            gate_product(1)
            pe.wait_ge(zeroed, 4)
            pe.wait_ge(acc_done, KT)
            for j in range(16):
                mm = nc.tensor.matmul(ps_cols[:, j:j + 1], acc[:, j * P:(j + 1) * P], ones[:, :], start=True, stop=True,
                                      skip_group_check=True)
            mm.then_inc(sum_done, 1)

        @block.vector
        def _(dve):
            def weigh(k):
                dve.wait_ge(w_in[k], 16)
                if k == 0:
                    dve.wait_ge(silu_done, 1)
                    nc.vector.tensor_scalar(acc[:, :], wa[:, 0, 0:2 * D], c_silu[:, 0:1], None,
                                            ALU.mult).then_inc(acc_done, 1)
                else:
                    dve.wait_ge(acc_done, k)
                    nc.vector.scalar_tensor_tensor(out=acc[:, :], in0=wa[:, k, 0:2 * D], scalar=c_silu[:, k:k + 1],
                                                   in1=acc[:, :], op0=ALU.mult, op1=ALU.add).then_inc(acc_done, 1)

            n = 0
            for layer in range(3):
                for a in range(2):
                    dve.wait_ge(lin_done[a], layer + 1)
                    if layer:
                        dve.wait_ge(sin_done[a], layer)
                    nc.vector.tensor_scalar(arg[:, a, :], psf[:, a, :], cols[:, layer:layer + 1], cols[:, 3:4],
                                            ALU.add, ALU.mult).then_inc(arg_done[a], 1)
                weigh(3 * layer)
                for a in range(2):
                    dve.wait_ge(turn_done[a], 2 * layer + 2)
                    for c in (C1, C2):
                        nc.vector.scalar_tensor_tensor(out=arg[:, a, :], in0=turn[:, a, :], scalar=-c,
                                                       in1=arg[:, a, :], op0=ALU.mult, op1=ALU.add).then_inc(step, 1)
                        n += 1
                        dve.wait_ge(step, n)
                    nc.vector.tensor_scalar(arg[:, a, :], arg[:, a, :], PI, -PI, ALU.min,
                                            ALU.max).then_inc(fold_done[a], 1)
                for k in range(3 * layer + 1, min(3 * layer + 3, KT)):
                    weigh(k)
            for half in range(2):
                hs = slice(64 * half, 64 * half + 64)
                dve.wait_ge(split_hi, half + 1)
                nc.vector.tensor_tensor(hfil[hs, 1, hs, :], h[hs, :, :].rearrange("p a (c g) -> p (a c) g", g=GF),
                                        f32(hfil[hs, 0, hs, :]), ALU.subtract).then_inc(split_lo, 1)
            dve.wait_ge(b_loaded, 48)
            dve.wait_ge(sum_done, 3)
            nc.vector.tensor_tensor(shift[:, :], ps_cols[:, 0:8], b_cols[:, 0:8], ALU.add).then_inc(cols_done, 1)
            nc.vector.scalar_tensor_tensor(out=scale1[:, :], in0=ps_cols[:, 8:16], scalar=1.0, in1=b_cols[:, 8:16],
                                           op0=ALU.add, op1=ALU.add).then_inc(cols_done, 1)
            nc.vector.tensor_tensor(gate[:, 0, :], ps_gate[0:1, :, :].rearrange("p a b -> p (a b)"), b_gate[:, :],
                                    ALU.add).then_inc(gate_done, 1)
            dve.wait_ge(gate_done, 1)
            nc.vector.tensor_tensor(gate[:, 1, :], b_out[:, :], gate[:, 0, :], ALU.mult).then_inc(prod_done, 1)

        @block.scalar
        def _(act):
            with nc.allow_non_contiguous_dma(reason="columns of small vectors"):
                act.dma_start(c_in[:, :], t["c"].rearrange("o (k p) -> p (o k)", p=P)).then_inc(c_loaded, 16)
            act.wait_ge(c_loaded, 16)
            nc.scalar.activation(c_silu[:, :], c_in[:, :], ACT.Silu).then_inc(silu_done, 1)
            for layer in range(3):
                for a in range(2):
                    act.wait_ge(arg_done[a], layer + 1)
                    nc.scalar.activation(turn[:, a, :], arg[:, a, :], ACT.Copy, scale=1.0 / (2 * math.pi),
                                         bias=MAGIC).then_inc(turn_done[a], 1)
                    act.wait_ge(turn_done[a], 2 * layer + 1)
                    nc.scalar.activation(turn[:, a, :], turn[:, a, :], ACT.Copy, bias=-MAGIC).then_inc(turn_done[a], 1)
                for a in range(2):
                    act.wait_ge(fold_done[a], layer + 1)
                    nc.scalar.activation(h[:, a, :], arg[:, a, :], ACT.Sin).then_inc(sin_done[a], 1)
                if layer == 1:
                    act.wait_ge(wraw_in, 32)
                    nc.scalar.activation(wfil[:, 0, :, :], wraw[:, :, :], ACT.Copy).then_inc(whi_done, 1)
            for a in range(2):
                act.wait_ge(sin_done[a], 3)
            for half in range(2):
                hs = slice(64 * half, 64 * half + 64)
                nc.scalar.activation(hfil[hs, 0, hs, :], h[hs, :, :].rearrange("p a (c g) -> p (a c) g", g=GF),
                                     ACT.Copy).then_inc(split_hi, 1)



def filter_stage1(nc, t, tabs, hfil, wfil, xf):
    with Scope(nc, "fs1") as s:
        e0 = s.sb("e0", [1, P])
        hs_ = [s.sb(f"hs{b}", [P, 2, P], F32R) for b in range(2)]
        tab = [s.sb(f"tab{b}", [P, 2, P], F32R) for b in range(4)]
        dec = [s.sb(f"dec{b}", [P, DH]) for b in range(4)]
        kf = [s.sb(f"k{b}", [P, 2, DH]) for b in range(2)]
        bias = kf[1]
        khi = [s.sb(f"khi{b}", [P, 2, DH], F32R) for b in range(2)]
        klo = [s.sb(f"klo{b}", [P, 2, DH], F32R) for b in range(2)]
        gen_ps = [s.ps(f"gen{b}", [P, 2, CH]) for b in range(2)]
        s1_ps = [s.ps(f"s1{b}", [P, 2, CH]) for b in range(2)]
        loaded, copied, e0_set = (s.sem(n) for n in ("loaded", "copied", "e0_set"))
        dec_in, tab_in = (s.sems(n, 4) for n in ("dec_in", "tab_in"))
        hs_ready, gen_done, k_done, hi_done, lo_done, s1_done, evac_done = (
            s.sems(n) for n in ("hs_ready", "gen_done", "k_done", "hi_done", "lo_done", "s1_done", "evac_done"))
        block = s.block()

        @block.sync
        def _(sp):
            sp.dma_start(bias[0:1, :, :], t["hyena_bias"][0:1, :, :]).then_inc(loaded, 16)

            def load(it, b):
                slot, used = at(it, b, 4)
                two, used2 = at(it, b - 4, 2)
                if not (isinstance(it, int) and it == 0):
                    after(sp, k_done[two], used2 + 1)
                    after(sp, s1_done[two], used2 + 1)
                    sp.wait_ge(copied, 16)
                sp.dma_start(dec[slot][:, :], t["t_decay"][4 * it + b, :, :]).then_inc(dec_in[slot], 16)
                sp.dma_start(f32(tab[slot][:, :, :]), tabs["w1f"][4 * it + b, :, :, :]).then_inc(tab_in[slot], 16)
                if isinstance(it, int) and U * it + b == FIRST_TABS - 1:
                    sp.dma_start(tabs["w1f"][FIRST_TABS:], t["t_w1f"][FIRST_TABS:]).then_inc(copied, 16)

            pipeline(sp, GF, [(load, 0)])
            for n in ("dft", "f0", "i0"):
                sp.dma_start(tabs[n], t["t_" + n]).then_inc(copied, 16)
            sp.wait_ge(copied, 64)

        @block.gpsimd
        def _(pool):
            nc.gpsimd.memset(e0[:, :], 0.0).then_inc(e0_set, 1)
            pool.wait_ge(e0_set, 1)
            nc.gpsimd.memset(e0[:, 0:1], 1.0).then_inc(e0_set, 1)
            pool.wait_ge(e0_set, 2)
            for n in range(GF):
                after(pool, gen_done[n % 2], n // 2)
                nc.gpsimd.tensor_copy(hs_[n % 2][:, :, :], hfil[:, :, :, n]).then_inc(hs_ready[n % 2], 1)

        @block.tensor
        def _(pe):
            def gen(it, b):
                first = isinstance(it, int) and U * it + b == 0
                r, used = at(it, b, 2)
                pe.wait_ge(hs_ready[r], used + 1)
                after(pe, k_done[r], used)
                for o in range(2):
                    mm = mm3(nc, gen_ps[r][:, o, :], (hs_[r][:, 0, :], hs_[r][:, 1, :]),
                             (wfil[:, 0, o, :], wfil[:, 1, o, :]), True, not first)
                    if first:
                        mm = nc.tensor.matmul(gen_ps[r][:, o, :], e0[:, :], bias[0:1, o, :], start=False, stop=True,
                                              skip_group_check=True)
                mm.then_inc(gen_done[r], 1)

            def stage1(it, b):
                r, used = at(it, b, 2)
                r4, used4 = at(it, b, 4)
                pe.wait_ge(lo_done[r], used + 1)
                pe.wait_ge(tab_in[r4], 16 * used4 + 16)
                after(pe, evac_done[r], used)
                for o in range(2):
                    mm = mm3(nc, s1_ps[r][:, o, :], (tab[r4][:, 0, :], tab[r4][:, 1, :]),
                             (khi[r][:, o, :], klo[r][:, o, :]), True, True)
                mm.then_inc(s1_done[r], 1)

            pe.wait_ge(loaded, 16)
            pe.wait_ge(e0_set, 2)
            pipeline(pe, GF, [(gen, 0), (stage1, 2)])

        @block.vector
        def _(dve):
            def window(it, b):
                r, used = at(it, b, 2)
                r4, used4 = at(it, b, 4)
                dve.wait_ge(gen_done[r], used + 1)
                dve.wait_ge(dec_in[r4], 16 * used4 + 16)
                after(dve, lo_done[r], used)
                nc.vector.tensor_tensor(kf[r][:, :, :], gen_ps[r][:, :, :],
                                        dec[r4][:, :].unsqueeze(1).broadcast_to([P, 2, DH]),
                                        ALU.mult).then_inc(k_done[r], 1)

            def low(it, b):
                r, used = at(it, b, 2)
                dve.wait_ge(hi_done[r], used + 1)
                after(dve, s1_done[r], used)
                nc.vector.tensor_tensor(klo[r][:, :, :], kf[r][:, :, :], f32(khi[r][:, :, :]),
                                        ALU.subtract).then_inc(lo_done[r], 1)

            pipeline(dve, GF, [(window, 0), (low, 1)])

        @block.scalar
        def _(act):
            def high(it, b):
                r, used = at(it, b, 2)
                act.wait_ge(k_done[r], used + 1)
                after(act, s1_done[r], used)
                nc.scalar.activation(khi[r][:, :, :], kf[r][:, :, :], ACT.Copy).then_inc(hi_done[r], 1)

            def evac(it, b):
                r, used = at(it, b, 2)
                act.wait_ge(s1_done[r], used + 1)
                plain(act, loaded, 16)
                nc.scalar.activation(xf[:, :, 4 * it + b, :], s1_ps[r][:, :, :], ACT.Copy).then_inc(evac_done[r], 1)

            act.wait_ge(loaded, 16)
            pipeline(act, GF, [(high, 0), (evac, 2)])


class Dft:

    def __init__(self, s):
        self.gen = s.sb("dft", [P, 3, 2, P], F32R)
        self.fwd0 = s.sb("fwd0", [P, 4, 2, P], F32R)
        self.inv0 = s.sb("inv0", [P, 4, 2, P], F32R)

    def load(self, eng, tabs, name, sem):
        table = {"f0": self.fwd0, "dft": self.gen, "i0": self.inv0}[name]
        eng.dma_start(f32(table[:, :, :, :]), tabs[name][:, :, :, :]).then_inc(sem, 16)

    def passes(self, nc, out, hi, lo, inverse, first):
        if first:
            tabs = self.inv0 if inverse else self.fwd0
            pick = (0, 1, 2, 3)
        else:
            tabs = self.gen
            pick = (0, 1, 2, 0) if inverse else (0, 2, 1, 0)
        for o in range(2):
            for i in range(2):
                k = pick[2 * i + o]
                mm = mm3(nc, out[:, o, :], (tabs[:, k, 0, :], tabs[:, k, 1, :]),
                         (hi[:, i, :], lo[:, i, :]), i == 0, i == 1)
        return mm



def filter_stage2(nc, tabs, xf, kfreq):
    with Scope(nc, "fs2") as s:
        dft = Dft(s)
        a = [s.sb(f"a{b}", [P, 2, DH]) for b in range(4)]
        ahi = [s.sb(f"ahi{b}", [P, 2, DH], F32R) for b in range(4)]
        alo = [s.sb(f"alo{b}", [P, 2, DH], F32R) for b in range(4)]
        out = [s.sb(f"out{b}", [P, 2, DH]) for b in range(2)]
        ps = [s.ps(f"ps{b}", [P, 2, CH]) for b in range(2)]
        pair0_in, gen_in = s.sem("pair0_in"), s.sem("gen_in")
        a_in, hi_done, lo_done = (s.sems(n, 4) for n in ("a_in", "hi_done", "lo_done"))
        mm_done, re_out, im_out, stored = (s.sems(n) for n in ("mm_done", "re_out", "im_out", "stored"))
        block = s.block()
        UNITS = 2 * NPAIR

        @block.sync
        def _(sp):
            def load(n):
                b, o, q = n % 4, n // NPAIR, n % NPAIR
                after(sp, lo_done[b], n // 4)
                for i in range(2):
                    slot = 2 * q + i
                    sp.dma_start(a[b][:, i, :], xf[4 * slot:4 * slot + 4, o, :, :]).then_inc(a_in[b], 16)

            load(0)
            dft.load(sp, tabs, "f0", pair0_in)
            load(1)
            dft.load(sp, tabs, "dft", gen_in)
            for n in range(2, 4):
                load(n)
            for n in range(UNITS):
                b, it = n % 2, n // 2
                if n + 4 < UNITS:
                    load(n + 4)
                sp.wait_ge(re_out[b], it + 1)
                sp.wait_ge(im_out[b], it + 1)
                sp.dma_start(kfreq[n // NPAIR, n % NPAIR, :, :, :], out[b][:, :, :]).then_inc(stored[b], 16)
            for b in range(2):
                sp.wait_ge(stored[b], 16 * NPAIR)

        @block.tensor
        def _(pe):
            def unit(it, b):
                r, used = at(it, b, 2)
                r4, used4 = at(it, b, 4)
                pe.wait_ge(lo_done[r4], used4 + 1)
                after(pe, re_out[r], used)
                after(pe, im_out[r], used)
                first = isinstance(it, int) and (U * it + b) % NPAIR == 0
                if isinstance(it, int) and U * it + b == 1:
                    pe.wait_ge(gen_in, 16)
                dft.passes(nc, ps[r], ahi[r4], alo[r4], False, first).then_inc(mm_done[r], 1)

            pe.wait_ge(pair0_in, 16)
            pipeline(pe, UNITS, [(unit, 0)], peel=(0, NPAIR // U))

        @block.scalar
        def _(act):
            def high(it, b):
                r4, used4 = at(it, b, 4)
                two, used = at(it, b - 4, 2)
                act.wait_ge(a_in[r4], 32 * used4 + 32)
                after(act, mm_done[two], used + 1)
                nc.scalar.activation(ahi[r4][:, :, :], a[r4][:, :, :], ACT.Copy).then_inc(hi_done[r4], 1)

            def evac(it, b):
                r, used = at(it, b, 2)
                act.wait_ge(mm_done[r], used + 1)
                after(act, stored[r], 16 * used)
                nc.scalar.activation(out[r][:, 0, :], ps[r][:, 0, :], ACT.Copy).then_inc(re_out[r], 1)

            pipeline(act, UNITS, [(high, 0), (evac, 2)])

        @block.vector
        def _(dve):
            def low(it, b):
                r4, used4 = at(it, b, 4)
                two, used = at(it, b - 4, 2)
                dve.wait_ge(hi_done[r4], used4 + 1)
                after(dve, mm_done[two], used + 1)
                nc.vector.tensor_tensor(alo[r4][:, :, :], a[r4][:, :, :], f32(ahi[r4][:, :, :]),
                                        ALU.subtract).then_inc(lo_done[r4], 1)

            def evac(it, b):
                r, used = at(it, b, 2)
                dve.wait_ge(mm_done[r], used + 1)
                after(dve, stored[r], 16 * used)
                nc.vector.tensor_copy(out[r][:, 1, :], ps[r][:, 1, :]).then_inc(im_out[r], 1)

            pipeline(dve, UNITS, [(low, 0), (evac, 2)])



def project(nc, t, tabs, scale1, shift, uhi, ulo, vx, g2, yp):
    with Scope(nc, "prj") as s:
        ws = [s.sb(f"ws{b}", [P, KT, P]) for b in range(2)]
        whi = [s.sb(f"whi{b}", [P, KT, P], F32R) for b in range(2)]
        wlo = [s.sb(f"wlo{b}", [P, KT, P], F32R) for b in range(2)]
        W = L + 2 * PAD
        eye = s.sb("eye", [P, P])
        ut = [s.sb(f"ut{j}", [P, CH]) for j in range(4)]
        row = s.sb("row", [P, W])
        cv = [s.sb(f"cv{b}", [P, W]) for b in range(2)]
        st = s.sb("st", [P, GS, P])
        phl = [s.sb(f"phl{b}", [P, 2, CH], F32R) for b in range(2)]
        b_in = s.sb("b_in", [P, PROJ // P])
        bcol = s.sb("bcol", [P, 2])
        cw = s.sb("cw", [P, 3, 12])
        cb = s.sb("cb", [P, 12])
        pw = s.sb("pw", [P, 4, P])
        pwhl = s.sb("pwhl", [P, 2, 4, P], F32R)
        pscale = s.sb("pscale", [P, 4])
        edge = s.sb("edge", [P, 4, 2, PAD])
        pp = [s.ps(f"pp{c}", [P, CH]) for c in range(4)]
        px = [s.ps(f"px{c}", [P, CH]) for c in range(4)]
        xs = [cv[b][:, 0:L].rearrange("p (j d) -> p j d", d=D) for b in range(2)]
        xs.append(st[:, :, :].rearrange("p (j e) c -> p j (e c)", j=2))
        eye_in = s.sem("eye_in")
        x_low, x_high = s.sems("x_low", 3), s.sems("x_high", 3)
        xt_done, u_done, uhi_done, ulo_done = (s.sems(n, 4) for n in ("xt_done", "u_done", "uhi_done", "ulo_done"))
        consts, copied, pad_set, pwhi_done, pwlo_done = (
            s.sem(n) for n in ("consts", "copied", "pad_set", "pwhi_done", "pwlo_done"))
        w_in, whi_done, wlo_done, conv_step, conv_done, prj_last, bcol_set = (
            s.sems(n) for n in ("w_in", "whi_done", "wlo_done", "conv_step", "conv_done", "prj_last", "bcol_set"))
        prj_done, bank_read, tr_done, tr_read = (s.sems(n, 4) for n in ("prj_done", "bank_read", "tr_done", "tr_read"))
        st_stored, g2_done, g2_stored, pool_step, phi_done, plo_done, mix_done, yp_part, yp_stored = (
            s.sem(n) for n in ("st_stored", "g2_done", "g2_stored", "pool_step",
                               "phi_done", "plo_done", "mix_done", "yp_part", "yp_stored"))
        block = s.block()
        wsrc = t["w_in"][0, :, :].rearrange("(k p) n -> p k n", p=P)
        stf = st[:, :, :].rearrange("p g c -> p (g c)")

        @block.sync
        def _(sp):
            def load(it, b, tile):
                after(sp, wlo_done[b], it)
                sp.dma_start(ws[b][:, :, :], wsrc[:, :, bass.ds(tile * P, P)]).then_inc(w_in[b], 16)

            def copy_tables(g):
                for n in ("w1s", "iw1"):
                    src = t["t_" + n]
                    sp.dma_start(tabs[n][g, :, :, :, :], src[g, :, :, :, :]).then_inc(copied, 16)

            def store_t(n):
                for j in range(4):
                    sp.wait_ge(tr_read[j], n + 1)
                sp.dma_start(vx[:, :, bass.ds(n * P, P)], st[:, :, :]).then_inc(st_stored, 16)

            def load_x_columns(h, sem):
                cols = slice(0, D // 2) if sem is x_low else slice(D // 2, D)
                sp.dma_start(xs[h % 3][:, :, cols], t["x"][0, 2 * P * h:2 * P * (h + 1), cols].rearrange(
                    "(j p) d -> p j d", p=P)).then_inc(sem[h % 3], 16)

            def load_x(h):
                if h >= 3:
                    for j in range(4):
                        sp.wait_ge(xt_done[j], 2 * ((h - 3) // 2 + 1))
                load_x_columns(h, x_low)
                load_x_columns(h, x_high)

            sp.dma_start(eye[:, :], t["t_eye"][:, :]).then_inc(eye_in, 16)
            for sem in (x_low, x_high):
                for h in range(2):
                    load_x_columns(h, sem)
            load(0, 0, 0)
            load_x(2)
            load(0, 1, 1)
            load_x(3)
            with nc.allow_non_contiguous_dma(reason="columns of small vectors"):
                sp.dma_start(b_in[:, :], t["b_in"][0, :].rearrange("(k p) -> p k", p=P)).then_inc(consts, 16)
                for j in range(3):
                    sp.dma_start(cw[:, j, :], t["conv_w"][0, j, :].rearrange("(k p) -> p k", p=P)).then_inc(consts, 16)
                sp.dma_start(cb[:, :], t["conv_b"][0, :].rearrange("(k p) -> p k", p=P)).then_inc(consts, 16)
                sp.dma_start(pscale[:, :], t["pool_scale"][0, :].rearrange("(k p) -> p k", p=P)).then_inc(consts, 16)
            sp.dma_start(pw[:, :, :], t["pool_w"][0, :, :, :].rearrange("g c d -> c g d")).then_inc(consts, 16)
            sp.dma_start(edge[:, :, :, :], t["t_edge"].partition_broadcast(P)).then_inc(consts, 16)
            for h in range(4, 8):
                load_x(h)

            def turned_step(it):
                for b in range(2):
                    load(it + 1, b, 2 * it + 2 + b)
                    copy_tables(2 * it + b)
                    store_t(2 * it + b)

            turned_step(0)
            with sp.Fori(1, 3) as it:
                turned_step(it)
            for b in range(2):
                load(4, b, 8 + 4 * b)
                copy_tables(6 + b)
                store_t(6 + b)
            with sp.Fori(0, 3) as i:
                for b in range(2):
                    load(i + 5, b, i + 9 + 4 * b)
                    copy_tables(2 * i + 8 + b)
                sp.wait_ge(g2_done, i + 1)
                sp.dma_start(g2[i, :, :], cv[1][:, 0:L]).then_inc(g2_stored, 16)
            for b in range(2):
                load(8, b, 16 + 4 * b)
                copy_tables(14 + b)
            sp.wait_ge(g2_done, 4)
            sp.dma_start(g2[3, :, :], cv[1][:, 0:L]).then_inc(g2_stored, 16)
            for i in range(4):
                if i < 3:
                    for b in range(2):
                        load(i + 9, b, i + 17 + 4 * b)
                sp.wait_ge(yp_part, 4 * i + 4)
                sp.dma_start(yp[i, :, :], cv[1 - i % 2][:, 0:L]).then_inc(yp_stored, 16)
            sp.wait_ge(g2_stored, 64)
            sp.wait_ge(yp_stored, 64)
            sp.wait_ge(st_stored, 128)
            sp.wait_ge(copied, 2 * 16 * GS)

        @block.gpsimd
        def _(pool):
            nc.gpsimd.memset(row[:, 0:PAD], 0.0).then_inc(pad_set, 1)
            pool.wait_ge(pad_set, 1)
            nc.gpsimd.memset(row[:, PAD + L:W], 0.0).then_inc(pad_set, 1)

            def low_weights(it, b):
                pool.wait_ge(whi_done[b], it + 1)
                nc.gpsimd.tensor_tensor(wlo[b][:, :, :], ws[b][:, :, :], f32(whi[b][:, :, :]),
                                        ALU.subtract).then_inc(wlo_done[b], 1)

            for tc in range(4):
                for k in range(1, KT, 2):
                    j, use = k % 4, 2 * tc + k // 4
                    pool.wait_ge(uhi_done[j], use + 1)
                    nc.gpsimd.tensor_tensor(ulo[:, k, tc * CH:(tc + 1) * CH], ut[j][:, :],
                                            f32(uhi[:, k, tc * CH:(tc + 1) * CH]), ALU.subtract).then_inc(ulo_done[j], 1)
                if tc < 2:
                    low_weights(0, tc)
            for it in range(1, 12):
                for b in range(2):
                    pool.wait_ge(w_in[b], 16 * it + 16)
                    after(pool, prj_last[b], it)
                    nc.gpsimd.tensor_copy(whi[b][:, :, :], ws[b][:, :, :]).then_inc(whi_done[b], 1)
                    low_weights(it, b)

        @block.tensor
        def _(pe):
            def turn_x(tc):
                for k in range(KT):
                    if k in (0, KT // 2):
                        for h in (2 * tc, 2 * tc + 1):
                            pe.wait_ge((x_high if k else x_low)[h % 3], 16 * (h // 3) + 16)
                    j, use = k % 4, 2 * tc + k // 4
                    after(pe, u_done[j], use)
                    for i in range(4):
                        mm = nc.tensor.transpose(px[j][:, i * P:(i + 1) * P],
                                                 xs[(2 * tc + i // 2) % 3][:, i % 2, k * P:(k + 1) * P], eye[:, :])
                    mm.then_inc(xt_done[j], 1)

            def proj_chunk(it, b, c):
                if c == 0:
                    pe.wait_ge(wlo_done[b], it + 1)
                after(pe, bank_read[c], 2 * it + b)
                for k in range(KT):
                    mm = mm3(nc, pp[c][:, :], (whi[b][:, k, :], wlo[b][:, k, :]),
                             (uhi[:, k, c * CH:(c + 1) * CH], ulo[:, k, c * CH:(c + 1) * CH]), k == 0, k == KT - 1)
                mm.then_inc(prj_done[c] if c < 3 else prj_last[b], 1)

            def proj(it, b):
                for c in range(4):
                    proj_chunk(it, b, c)

            def turn(it, b):
                pe.wait_ge(conv_done[b], it + 1)
                src = cv[b][:, 0:L].rearrange("p (c g) -> p g c", g=GS)
                for j in range(4):
                    after(pe, tr_read[j], 2 * it + b)
                    for i in range(4):
                        mm = nc.tensor.transpose(px[j][:, i * P:(i + 1) * P], src[:, 4 * j + i, :], eye[:, :])
                    mm.then_inc(tr_done[j], 1)

            def turned_step(it):
                proj(it, 1)
                turn(it, 0)
                proj(it + 1, 0)
                turn(it, 1)

            def mix(i, c):
                pe.wait_ge(plo_done, 4 * i + c + 1)
                if i:
                    pe.wait_ge(yp_part, 4 * (i - 1) + c + 1)
                mm3(nc, px[c][:, :], (pwhl[:, 0, i, :], pwhl[:, 1, i, :]),
                    (phl[c % 2][:, 0, :], phl[c % 2][:, 1, :]), True, True).then_inc(mix_done, 1)

            pe.wait_ge(eye_in, 16)
            turn_x(0)
            for tc in range(4):
                if tc < 3:
                    turn_x(tc + 1)
                for j in range(4):
                    pe.wait_ge(ulo_done[j], 2 * tc + 2)
                proj_chunk(0, 0, tc)
            turned_step(0)
            with pe.Fori(1, 4) as it:
                turned_step(it)
            proj(4, 1)
            with pe.Fori(5, 8) as it:
                proj(it, 0)
                proj(it, 1)
            pe.wait_ge(pwlo_done, 1)
            for i in range(4):
                for c in range(4):
                    proj_chunk(8 + i, 0, c)
                    if i:
                        mix(i - 1, c)
                proj(8 + i, 1)
            for c in range(4):
                mix(3, c)

        @block.scalar
        def _(act):
            def projected(it, b, c):
                if c < 3:
                    act.wait_ge(prj_done[c], 2 * it + b + 1)
                else:
                    act.wait_ge(prj_last[b], it + 1)

            def pick_bias(it, b, tile):
                nc.scalar.activation(bcol[:, b:b + 1], b_in[:, bass.ds(tile, 1)], ACT.Copy).then_inc(bcol_set[b], 1)
                act.wait_ge(bcol_set[b], it + 1)

            def bias_chunk(it, b, c):
                projected(it, b, c)
                nc.scalar.activation(row[:, PAD + c * CH:PAD + (c + 1) * CH], pp[c][:, :], ACT.Identity,
                                     bias=bcol[:, b:b + 1]).then_inc(bank_read[c], 1)

            def bias_row(it, b):
                for c in range(4):
                    bias_chunk(it, b, c)

            def gate_chunk(it, b, c):
                projected(it, b, c)
                nc.scalar.activation(stf[:, c * CH:(c + 1) * CH], pp[c][:, :], ACT.Silu,
                                     bias=bcol[:, b:b + 1]).then_inc(bank_read[c], 1)

            def gate_row(it, b):
                for c in range(4):
                    gate_chunk(it, b, c)

            def store_turned(it, b):
                after(act, st_stored, 32 * it + 16 * b)
                for j in range(4):
                    act.wait_ge(tr_done[j], 2 * it + b + 1)
                    nc.scalar.activation(st[:, 4 * j:4 * j + 4, :], px[j][:, :], ACT.Copy).then_inc(tr_read[j], 1)

            def high_u(tc):
                for k in range(KT):
                    j = k % 4
                    act.wait_ge(u_done[j], 2 * tc + k // 4 + 1)
                    nc.scalar.activation(uhi[:, k, tc * CH:(tc + 1) * CH], ut[j][:, :], ACT.Copy).then_inc(uhi_done[j], 1)

            def turned_step(it):
                pick_bias(it, 1, 2 * it + 1)
                act.wait_ge(conv_done[0], it + 1)
                bias_row(it, 1)
                store_turned(it, 0)
                pick_bias(it + 1, 0, 2 * it + 2)
                act.wait_ge(conv_done[1], it + 1)
                bias_row(it + 1, 0)
                store_turned(it, 1)

            high_u(0)
            def high_weights(b):
                act.wait_ge(w_in[b], 16)
                nc.scalar.activation(whi[b][:, :, :], ws[b][:, :, :], ACT.Copy).then_inc(whi_done[b], 1)

            high_weights(0)
            high_u(1)
            high_weights(1)
            act.wait_ge(consts, 8 * 16)
            act.wait_ge(pad_set, 2)
            pick_bias(0, 0, 0)
            bias_chunk(0, 0, 0)
            for tc in range(1, 4):
                if tc < 3:
                    high_u(tc + 1)
                bias_chunk(0, 0, tc)
            nc.scalar.activation(pwhl[:, 0, :, :], pw[:, :, :], ACT.Copy).then_inc(pwhi_done, 1)
            turned_step(0)
            with act.Fori(1, 4) as it:
                turned_step(it)
            act.wait_ge(st_stored, 128)

            def hyena_gate(i):
                pick_bias(i + 4, 1, i + 12)
                gate_row(i + 4, 1)

            hyena_gate(0)
            with act.Fori(1, 4) as i:
                pick_bias(i + 4, 0, i + 8)
                act.wait_ge(g2_done, i)
                bias_row(i + 4, 0)
                hyena_gate(i)

            def high_pooled(i, c):
                if c >= 2 or i:
                    act.wait_ge(mix_done, 4 * i + c - 1)
                nc.scalar.activation(phl[c % 2][:, 0, :], cv[i % 2][:, c * CH:(c + 1) * CH],
                                     ACT.Copy).then_inc(phi_done, 1)

            for i in range(4):
                pick_bias(i + 8, 0, i + 16)
                if i == 0:
                    act.wait_ge(g2_done, 4)
                else:
                    act.wait_ge(pool_step, POOL_STEPS[i - 1])
                for c in range(4):
                    if i:
                        high_pooled(i - 1, c)
                    bias_chunk(i + 8, 0, c)
                pick_bias(i + 8, 1, i + 20)
                for c in range(4):
                    if i:
                        act.wait_ge(yp_part, 4 * (i - 1) + c + 1)
                    gate_chunk(i + 8, 1, c)
            act.wait_ge(pool_step, POOL_STEPS[3])
            for c in range(4):
                high_pooled(3, c)

        @block.vector
        def _(dve):
            def conv(it, b, n, tile, dst):
                for c in range(4):
                    dve.wait_ge(bank_read[c], n + 1)
                nc.vector.tensor_scalar(dst[:, 0:L], row[:, PAD - 1:PAD - 1 + L], cw[:, 0, bass.ds(tile, 1)],
                                        cb[:, bass.ds(tile, 1)], ALU.mult, ALU.add).then_inc(conv_step[b], 1)
                dve.wait_ge(conv_step[b], 2 * it + 1)
                nc.vector.scalar_tensor_tensor(out=dst[:, 0:L], in0=row[:, PAD:PAD + L], scalar=cw[:, 1, bass.ds(tile, 1)],
                                               in1=dst[:, 0:L], op0=ALU.mult, op1=ALU.add).then_inc(conv_step[b], 1)
                dve.wait_ge(conv_step[b], 2 * it + 2)
                nc.vector.scalar_tensor_tensor(out=dst[:, 0:L], in0=row[:, PAD + 1:PAD + 1 + L],
                                               scalar=cw[:, 2, bass.ds(tile, 1)], in1=dst[:, 0:L],
                                               op0=ALU.mult, op1=ALU.add).then_inc(conv_done[b], 1)

            for tc in range(4):
                for k in range(KT + 1):
                    if k < KT:
                        j, use = k % 4, 2 * tc + k // 4
                        dve.wait_ge(xt_done[j], use + 1)
                        after(dve, ulo_done[j], use)
                        nc.vector.tensor_scalar(ut[j][:, :], px[j][:, :], scale1[:, k:k + 1], shift[:, k:k + 1],
                                                ALU.mult, ALU.add).then_inc(u_done[j], 1)
                    if k % 2:
                        j, use = (k - 1) % 4, 2 * tc + (k - 1) // 4
                        dve.wait_ge(uhi_done[j], use + 1)
                        nc.vector.tensor_tensor(ulo[:, k - 1, tc * CH:(tc + 1) * CH], ut[j][:, :],
                                                f32(uhi[:, k - 1, tc * CH:(tc + 1) * CH]),
                                                ALU.subtract).then_inc(ulo_done[j], 1)
            dve.wait_ge(pwhi_done, 1)
            nc.vector.tensor_tensor(pwhl[:, 1, :, :], pw[:, :, :], f32(pwhl[:, 0, :, :]), ALU.subtract).then_inc(pwlo_done, 1)

            def turned_step(it):
                for b in range(2):
                    for j in range(4):
                        after(dve, tr_done[j], 2 * (it - 1) + b + 1)
                    conv(it, b, 2 * it + b, 2 * it + b, cv[b])

            turned_step(0)
            with dve.Fori(1, 4) as it:
                turned_step(it)
            for j in range(4):
                dve.wait_ge(tr_done[j], 7)

            def gated_step(i):
                conv(i + 4, 0, 2 * i + 8, i + 8, cv[0])
                dve.wait_ge(conv_done[0], i + 5)
                for c in range(4):
                    dve.wait_ge(bank_read[c], 2 * i + 10)
                if isinstance(i, int):
                    for j in range(4):
                        dve.wait_ge(tr_done[j], 8)
                after(dve, g2_stored, 16 * i)
                nc.vector.tensor_tensor(cv[1][:, 0:L], cv[0][:, 0:L], stf, ALU.mult).then_inc(g2_done, 1)

            gated_step(0)
            with dve.Fori(1, 4) as i:
                gated_step(i)
            dve.wait_ge(g2_stored, 64)
            step = 0
            for i, win in enumerate(WINDOWS):
                h = win // 2
                for c in range(4):
                    dve.wait_ge(bank_read[c], 2 * i + 17)
                if i:
                    dve.wait_ge(yp_stored, 16 * i)
                src, n, k = row, 1, 0
                bufs = (cv[i % 2], cv[1 - i % 2])
                levels = win.bit_length() - 1
                lo_edge = PAD - h
                while n < win:
                    dst = bufs[(levels - k) % 2]
                    width = L + win - 2 * n
                    dve.wait_ge(pool_step, step)
                    nc.vector.tensor_tensor(dst[:, lo_edge:lo_edge + width], src[:, lo_edge:lo_edge + width],
                                            src[:, lo_edge + n:lo_edge + n + width], ALU.add).then_inc(pool_step, 1)
                    step += 1
                    src, n, k = dst, 2 * n, k + 1
                dve.wait_ge(pool_step, step)
                nc.vector.tensor_tensor(src[:, lo_edge:lo_edge + h], src[:, lo_edge:lo_edge + h],
                                        edge[:, i, 0, 0:h], ALU.mult).then_inc(pool_step, 1)
                step += 1
                if h > 1:
                    e = lo_edge + L
                    nc.vector.tensor_tensor(src[:, e - h + 1:e], src[:, e - h + 1:e],
                                            edge[:, i, 1, PAD - h + 1:PAD], ALU.mult).then_inc(pool_step, 1)
                    step += 1
                dve.wait_ge(pool_step, step)
                nc.vector.scalar_tensor_tensor(out=bufs[0][:, 0:L], in0=src[:, lo_edge:lo_edge + L], scalar=1.0 / win,
                                               in1=row[:, PAD:PAD + L], op0=ALU.mult, op1=ALU.subtract
                                               ).then_inc(pool_step, 1)
                step += 1
                assert step == POOL_STEPS[i]

                def low_pooled(c):
                    dve.wait_ge(phi_done, 4 * i + c + 1)
                    nc.vector.tensor_tensor(phl[c % 2][:, 1, :], bufs[0][:, c * CH:(c + 1) * CH],
                                            f32(phl[c % 2][:, 0, :]), ALU.subtract).then_inc(plo_done, 1)

                low_pooled(0)
                low_pooled(1)
                for c in range(4):
                    dve.wait_ge(mix_done, 4 * i + c + 1)
                    dve.wait_ge(bank_read[c], 18 + 2 * i)
                    nc.vector.scalar_tensor_tensor(out=bufs[1][:, c * CH:(c + 1) * CH], in0=px[c][:, :],
                                                   scalar=pscale[:, i:i + 1], in1=stf[:, c * CH:(c + 1) * CH],
                                                   op0=ALU.mult, op1=ALU.mult).then_inc(yp_part, 1)
                    if c < 2:
                        low_pooled(c + 2)



def signal_stage1(nc, vx, tabs, dft, x):
    with Scope(nc, "ss1") as s:
        z = [s.sb(f"z{b}", [P, DH]) for b in range(4)]
        zhi = [s.sb(f"zhi{b}", [P, DH], F32R) for b in range(2)]
        zlo = [s.sb(f"zlo{b}", [P, DH], F32R) for b in range(2)]
        tab = [s.sb(f"tab{b}", [P, 2, 2, P], F32R) for b in range(4)]
        ps = [s.ps(f"ps{b}", [P, 2, CH]) for b in range(2)]
        tabs_in = s.sem("tabs_in")
        z_in, tab_in = (s.sems(n, 4) for n in ("z_in", "tab_in"))
        hi_done, lo_done, mm_done, out0, out1 = (s.sems(n) for n in ("hi_done", "lo_done", "mm_done", "out0", "out1"))
        block = s.block()

        @block.sync
        def _(sp):
            def load(it, b):
                slot, _ = at(it, b, 4)
                two, used = at(it, b - 4, 2)
                if not (isinstance(it, int) and it == 0):
                    after(sp, lo_done[two], used + 1)
                    after(sp, mm_done[two], used + 1)
                sp.dma_start(z[slot][:, :], vx[:, 4 * it + b, 0:DH]).then_inc(z_in[slot], 16)
                sp.dma_start(f32(tab[slot][:, :, :, :]), tabs["w1s"][4 * it + b, :, :, :, :]).then_inc(tab_in[slot], 16)

            pipeline(sp, GS, [(load, 0)])
            for n in ("f0", "dft", "i0"):
                dft.load(sp, tabs, n, tabs_in)
            sp.wait_ge(tabs_in, 48)

        @block.tensor
        def _(pe):
            def unit(it, b):
                r, used = at(it, b, 2)
                r4, used4 = at(it, b, 4)
                pe.wait_ge(tab_in[r4], 16 * used4 + 16)
                pe.wait_ge(lo_done[r], used + 1)
                after(pe, out0[r], used)
                after(pe, out1[r], used)
                for m in range(2):
                    mm = mm3(nc, ps[r][:, m, :], (tab[r4][:, m, 0, :], tab[r4][:, m, 1, :]),
                             (zhi[r][:, :], zlo[r][:, :]), True, True)
                mm.then_inc(mm_done[r], 1)

            pipeline(pe, GS, [(unit, 0)])

        @block.scalar
        def _(act):
            def high(it, b):
                r, used = at(it, b, 2)
                r4, used4 = at(it, b, 4)
                act.wait_ge(z_in[r4], 16 * used4 + 16)
                after(act, mm_done[r], used)
                nc.scalar.activation(zhi[r][:, :], z[r4][:, :], ACT.Copy).then_inc(hi_done[r], 1)

            def evac(it, b):
                r, used = at(it, b, 2)
                act.wait_ge(mm_done[r], used + 1)
                plain(act, z_in[0], 16)
                nc.scalar.activation(x[:, 0, 4 * it + b, :], ps[r][:, 0, :], ACT.Copy).then_inc(out0[r], 1)

            pipeline(act, GS, [(high, 0), (evac, 1)])

        @block.vector
        def _(dve):
            def low(it, b):
                r, used = at(it, b, 2)
                r4, _ = at(it, b, 4)
                dve.wait_ge(hi_done[r], used + 1)
                after(dve, mm_done[r], used)
                nc.vector.tensor_tensor(zlo[r][:, :], z[r4][:, :], f32(zhi[r][:, :]),
                                        ALU.subtract).then_inc(lo_done[r], 1)

            def evac(it, b):
                r, used = at(it, b, 2)
                dve.wait_ge(mm_done[r], used + 1)
                nc.vector.tensor_copy(x[:, 1, 4 * it + b, :], ps[r][:, 1, :]).then_inc(out1[r], 1)

            pipeline(dve, GS, [(low, 0), (evac, 1)])


def spectrum_product(nc, tag, dft, x, kfreq, prefetch=()):
    with Scope(nc, tag) as s:
        a = [s.sb(f"a{b}", [P, 2, DH]) for b in range(4)]
        ahi = [s.sb(f"ahi{b}", [P, 2, DH], F32R) for b in range(2)]
        alo = [s.sb(f"alo{b}", [P, 2, DH], F32R) for b in range(2)]
        kf = [s.sb(f"kf{b}", [P, 2, DH]) for b in range(2)]
        by_re = [s.sb(f"by_re{b}", [P, 2, DH]) for b in range(2)]
        by_im = [s.sb(f"by_im{b}", [P, 2, DH]) for b in range(2)]
        y = [s.sb(f"y{b}", [P, 2, DH]) for b in range(2)]
        yhi = [s.sb(f"yhi{b}", [P, 2, DH], F32R) for b in range(2)]
        ylo = [s.sb(f"ylo{b}", [P, 2, DH], F32R) for b in range(2)]
        out = [s.sb(f"out{b}", [P, 2, DH]) for b in range(2)]
        real = s.sb("real", [1, 2, DH])
        u_ps = [s.ps(f"u{b}", [P, 2, CH]) for b in range(2)]
        b_ps = [s.ps(f"b{b}", [P, 2, CH]) for b in range(2)]
        real_bins, fetched = s.sem("real_bins"), s.sem("fetched")
        a_in = s.sems("a_in", 4)
        k_in, ahi_done, alo_done, u_done, mul_done, y_done, yhi_done, ylo_done, b_done, out_done, stored = (
            s.sems(n) for n in ("k_in", "ahi_done", "alo_done", "u_done", "mul_done", "y_done", "yhi_done",
                                "ylo_done", "b_done", "out_done", "stored"))
        block = s.block()

        def rows(q, i):
            slot = 2 * q + i
            r = slot % 16
            return x[8 * r:8 * r + 8, slot // 16, :, :]

        @block.sync
        def _(sp):
            def load_a(q):
                if q >= 4:
                    sp.wait_ge(alo_done[q % 2], q // 2 - 1)
                for i in range(2):
                    sp.dma_start(a[q % 4][:, i, :], rows(q, i)).then_inc(a_in[q % 4], 16)

            def load_k(q):
                b, it = q % 2, q // 2
                after(sp, mul_done[b], 2 * it)
                sp.dma_start(kf[b][:, :, :], kfreq[q, :, :, :]).then_inc(k_in[b], 16)

            def store(q):
                sp.wait_ge(out_done[q % 2], q // 2 + 1)
                for i in range(2):
                    sp.dma_start(rows(q, i), out[q % 2][:, i, :]).then_inc(stored[q % 2], 16)

            load_a(0)
            load_a(1)
            for q in range(2):
                load_k(q)
                load_a(q + 2)
            for q in range(2, NPAIR):
                load_k(q)
                if q + 2 < NPAIR:
                    load_a(q + 2)
                if 3 <= q < 3 + len(prefetch):
                    sp.dma_start(*prefetch[q - 3]).then_inc(fetched, 16)
                if q >= 5:
                    store(q - 5)
            for q in range(NPAIR - 5, NPAIR):
                store(q)
            for b in range(2):
                sp.wait_ge(stored[b], 16 * NPAIR)
            if prefetch:
                sp.wait_ge(fetched, 16 * len(prefetch))

        @block.gpsimd
        def _(pool):
            for q in range(NPAIR):
                r, used = q % 2, q // 2
                pool.wait_ge(mul_done[r], 2 * used + 2)
                after(pool, ylo_done[r], used)
                nc.gpsimd.tensor_tensor(y[r][:, 0, :], by_re[r][:, 0, :], by_im[r][:, 1, :],
                                        ALU.subtract).then_inc(y_done[r], 1)
                nc.gpsimd.tensor_tensor(y[r][:, 1, :], by_re[r][:, 1, :], by_im[r][:, 0, :],
                                        ALU.add).then_inc(y_done[r], 1)

        @block.tensor
        def _(pe):
            def first(it, b):
                return isinstance(it, int) and U * it + b == 0

            def fwd(it, b):
                r, used = at(it, b, 2)
                pe.wait_ge(alo_done[r], used + 1)
                after(pe, mul_done[r], 2 * used)
                dft.passes(nc, u_ps[r], ahi[r], alo[r], False, first(it, b)).then_inc(u_done[r], 1)

            def inv(it, b):
                r, used = at(it, b, 2)
                pe.wait_ge(ylo_done[r], used + 1)
                after(pe, out_done[r], used)
                dft.passes(nc, b_ps[r], yhi[r], ylo[r], True, first(it, b)).then_inc(b_done[r], 1)

            pipeline(pe, NPAIR, [(fwd, 0), (inv, 2)])

        @block.scalar
        def _(act):
            def ahigh(it, b):
                r, used = at(it, b, 2)
                r4, used4 = at(it, b, 4)
                act.wait_ge(a_in[r4], 32 * used4 + 32)
                after(act, u_done[r], used)
                nc.scalar.activation(ahi[r][:, :, :], a[r4][:, :, :], ACT.Copy).then_inc(ahi_done[r], 1)

            def yhigh(it, b):
                r, used = at(it, b, 2)
                act.wait_ge(y_done[r], 2 * used + 2)
                if isinstance(it, int) and U * it + b == 0:
                    act.wait_ge(real_bins, 2)
                after(act, b_done[r], used)
                nc.scalar.activation(yhi[r][:, :, :], y[r][:, :, :], ACT.Copy).then_inc(yhi_done[r], 1)

            def evac(it, b):
                r, used = at(it, b, 2)
                act.wait_ge(b_done[r], used + 1)
                after(act, stored[r], 32 * used)
                nc.scalar.activation(out[r][:, :, :], b_ps[r][:, :, :], ACT.Copy).then_inc(out_done[r], 1)

            pipeline(act, NPAIR, [(evac, 5), (yhigh, 3), (ahigh, 0)])

        @block.vector
        def _(dve):
            def alow(it, b):
                r, used = at(it, b, 2)
                r4, _ = at(it, b, 4)
                dve.wait_ge(ahi_done[r], used + 1)
                after(dve, u_done[r], used)
                nc.vector.tensor_tensor(alo[r][:, :, :], a[r4][:, :, :], f32(ahi[r][:, :, :]),
                                        ALU.subtract).then_inc(alo_done[r], 1)

            def ylow(it, b):
                r, used = at(it, b, 2)
                dve.wait_ge(yhi_done[r], used + 1)
                after(dve, b_done[r], used)
                nc.vector.tensor_tensor(ylo[r][:, :, :], y[r][:, :, :], f32(yhi[r][:, :, :]),
                                        ALU.subtract).then_inc(ylo_done[r], 1)

            def multiply(it, b):
                r, used = at(it, b, 2)
                dve.wait_ge(u_done[r], used + 1)
                dve.wait_ge(k_in[r], 16 * used + 16)
                after(dve, y_done[r], 2 * used)
                pair0 = isinstance(it, int) and U * it + b == 0
                if pair0:
                    nc.vector.tensor_tensor(real[:, :, :], u_ps[r][0:1, :, :], kf[r][0:1, :, :],
                                            ALU.mult).then_inc(real_bins, 1)
                nc.vector.tensor_tensor(by_re[r][:, :, :], u_ps[r][:, :, :],
                                        kf[r][:, 0:1, :].broadcast_to([P, 2, DH]), ALU.mult).then_inc(mul_done[r], 1)
                nc.vector.tensor_tensor(by_im[r][:, :, :], u_ps[r][:, :, :],
                                        kf[r][:, 1:2, :].broadcast_to([P, 2, DH]), ALU.mult).then_inc(mul_done[r], 1)

            def real_to_y(it, b):
                if isinstance(it, int) and U * it + b == 0:
                    dve.wait_ge(real_bins, 1)
                    dve.wait_ge(y_done[0], 2)
                    nc.vector.tensor_copy(y[0][0:1, :, :], real[:, :, :]).then_inc(real_bins, 1)

            pipeline(dve, NPAIR, [(multiply, 2), (ylow, 3), (alow, 0), (real_to_y, 2, 0)])


def between_orders(nc, vx, tabs, x):
    with Scope(nc, "mid") as s:
        xhi = [s.sb(f"xhi{b}", [P, 2, DH], F32R) for b in range(4)]
        xlo = [s.sb(f"xlo{b}", [P, 2, DH], F32R) for b in range(4)]
        x1 = [s.sb(f"x1{b}", [P, DH]) for b in range(4)]
        z = [s.sb(f"z{b}", [P, DH]) for b in range(4)]
        zhi = [s.sb(f"zhi{b}", [P, DH], F32R) for b in range(4)]
        zlo = [s.sb(f"zlo{b}", [P, DH], F32R) for b in range(4)]
        itab = [s.sb(f"itab{b}", [P, 2, 2, P], F32R) for b in range(4)]
        ftab = [s.sb(f"ftab{b}", [P, 2, 2, P], F32R) for b in range(4)]
        z_ps = [s.ps(f"zps{b}", [P, CH]) for b in range(2)]
        s_ps = [s.ps(f"sps{b}", [P, 2, CH]) for b in range(2)]
        x1_in, itab_in, ftab_in, xhi_done, xlo_done, inv_done, z_done, zhi_done, zlo_done, fwd_done, out0, out1 = (
            s.sems(n, 4) for n in ("x1_in", "itab_in", "ftab_in", "xhi_done", "xlo_done", "inv_done", "z_done",
                                   "zhi_done", "zlo_done", "fwd_done", "out0", "out1"))
        block = s.block()

        @block.sync
        def _(sp):
            def load_inv(it, b):
                r, used = at(it, b, 4)
                after(sp, z_done[r], used)
                sp.dma_start(f32(itab[r][:, :, :, :]), tabs["iw1"][4 * it + b, :, :, :, :]).then_inc(itab_in[r], 16)
                sp.dma_start(x1[r][:, :], vx[:, 4 * it + b, DH:2 * DH]).then_inc(x1_in[r], 16)

            def load_fwd(it, b):
                r, used = at(it, b, 4)
                after(sp, fwd_done[r], used)
                sp.dma_start(f32(ftab[r][:, :, :, :]), tabs["w1s"][4 * it + b, :, :, :, :]).then_inc(ftab_in[r], 16)

            pipeline(sp, GS, [(load_inv, 0, 4), (load_fwd, 2, 4)])

        @block.gpsimd
        def _(pool):
            for g in range(GS):
                r, used = g % 4, g // 4
                pool.wait_ge(zhi_done[r], used + 1)
                after(pool, fwd_done[r], used)
                nc.gpsimd.tensor_tensor(zlo[r][:, :], z[r][:, :], f32(zhi[r][:, :]),
                                        ALU.subtract).then_inc(zlo_done[r], 1)

        @block.tensor
        def _(pe):
            def inv(it, b):
                r, used = at(it, b, 4)
                before, used_before = at(it, b - 2, 4)
                pe.wait_ge(xlo_done[r], used + 1)
                pe.wait_ge(itab_in[r], 16 * used + 16)
                after(pe, z_done[before], used_before + 1)
                for m in range(2):
                    mm = mm3(nc, z_ps[b % 2][:, :], (itab[r][:, m, 0, :], itab[r][:, m, 1, :]),
                             (xhi[r][:, m, :], xlo[r][:, m, :]), m == 0, m == 1)
                mm.then_inc(inv_done[r], 1)

            def fwd(it, b):
                r, used = at(it, b, 4)
                before, used_before = at(it, b - 2, 4)
                pe.wait_ge(zlo_done[r], used + 1)
                pe.wait_ge(ftab_in[r], 16 * used + 16)
                after(pe, out0[before], used_before + 1)
                after(pe, out1[before], used_before + 1)
                for m in range(2):
                    mm = mm3(nc, s_ps[b % 2][:, m, :], (ftab[r][:, m, 0, :], ftab[r][:, m, 1, :]),
                             (zhi[r][:, :], zlo[r][:, :]), True, True)
                mm.then_inc(fwd_done[r], 1)

            pipeline(pe, GS, [(inv, 0), (fwd, 4)])

        @block.scalar
        def _(act):
            def xhigh(it, b):
                r, used = at(it, b, 4)
                after(act, inv_done[r], used)
                if not isinstance(it, int):
                    plain(act, z_done[0], 1)
                nc.scalar.activation(xhi[r][:, :, :], x[:, :, 4 * it + b, :], ACT.Copy).then_inc(xhi_done[r], 1)

            def zhigh(it, b):
                r, used = at(it, b, 4)
                act.wait_ge(z_done[r], used + 1)
                after(act, fwd_done[r], used)
                nc.scalar.activation(zhi[r][:, :], z[r][:, :], ACT.Copy).then_inc(zhi_done[r], 1)

            def evac(it, b):
                r, used = at(it, b, 4)
                act.wait_ge(fwd_done[r], used + 1)
                plain(act, z_done[0], 1)
                nc.scalar.activation(x[:, 0, 4 * it + b, :], s_ps[b % 2][:, 0, :], ACT.Copy).then_inc(out0[r], 1)

            pipeline(act, GS, [(xhigh, 0, 4), (zhigh, 2, 4), (evac, 5, 0)])

        @block.vector
        def _(dve):
            def gate(it, b):
                r, used = at(it, b, 4)
                dve.wait_ge(inv_done[r], used + 1)
                dve.wait_ge(x1_in[r], 16 * used + 16)
                after(dve, zlo_done[r], used)
                nc.vector.tensor_tensor(z[r][:, :], z_ps[b % 2][:, :], x1[r][:, :], ALU.mult).then_inc(z_done[r], 1)

            def xlow(it, b):
                r, used = at(it, b, 4)
                dve.wait_ge(xhi_done[r], used + 1)
                after(dve, inv_done[r], used)
                nc.vector.tensor_tensor(xlo[r][:, :, :], x[:, :, 4 * it + b, :], f32(xhi[r][:, :, :]),
                                        ALU.subtract).then_inc(xlo_done[r], 1)

            def evac(it, b):
                r, used = at(it, b, 4)
                dve.wait_ge(fwd_done[r], used + 1)
                nc.vector.tensor_copy(x[:, 1, 4 * it + b, :], s_ps[b % 2][:, 1, :]).then_inc(out1[r], 1)

            pipeline(dve, GS, [(xlow, 0, 4), (gate, 1, 4), (evac, 5, 0)])


def last_inverse(nc, t, tabs, x, rows, ya, whl):
    with Scope(nc, "fin") as s:
        xhi = [s.sb(f"xhi{b}", [P, 2, DH], F32R) for b in range(2)]
        xlo = [s.sb(f"xlo{b}", [P, 2, DH], F32R) for b in range(2)]
        tab = [s.sb(f"tab{b}", [P, 2, 2, P], F32R) for b in range(4)]
        wf = [s.sb(f"wf{b}", [P, D]) for b in range(2)]
        gate = s.sb("gate", [P, D])
        eye = s.sb("eye", [P, P])
        z = [s.sb(f"z{b}", [P, DH]) for b in range(2)]
        z_ps = [s.ps(f"zps{b}", [P, CH]) for b in range(2)]
        t_ps = [s.ps(f"tps{b}", [P, 4, P]) for b in range(2)]
        eye_in, gate_in = s.sem("eye_in"), s.sem("gate_in")
        z_done, tr_done = s.sems("z_done"), s.sems("tr_done")
        tab_in = s.sems("tab_in", 4)
        hi_done, lo_done, mm_done, y_done, w_in, w_scaled, whi_done, wlo_done = (
            s.sems(n) for n in ("hi_done", "lo_done", "mm_done", "y_done", "w_in", "w_scaled", "whi_done", "wlo_done"))
        block = s.block()
        yg = ya[:, :, :].rearrange("p k (c g) -> p k c g", g=GS)

        @block.sync
        def _(sp):
            def load(it, b):
                slot, _ = at(it, b, 4)
                two, used = at(it, b - 4, 2)
                if not (isinstance(it, int) and it == 0):
                    after(sp, mm_done[two], used + 1)
                sp.dma_start(f32(tab[slot][:, :, :, :]), tabs["iw1"][4 * it + b, :, :, :, :]).then_inc(tab_in[slot], 16)

            pipeline(sp, GS, [(load, 0)])

        @block.tensor
        def _(pe):
            def inv(it, b):
                r, used = at(it, b, 2)
                r4, used4 = at(it, b, 4)
                pe.wait_ge(lo_done[r], used + 1)
                pe.wait_ge(tab_in[r4], 16 * used4 + 16)
                after(pe, z_done[r], used)
                for m in range(2):
                    mm = mm3(nc, z_ps[r][:, :], (tab[r4][:, m, 0, :], tab[r4][:, m, 1, :]),
                             (xhi[r][:, m, :], xlo[r][:, m, :]), m == 0, m == 1)
                mm.then_inc(mm_done[r], 1)

            def turn(it, b):
                r, used = at(it, b, 2)
                pe.wait_ge(z_done[r], used + 1)
                after(pe, y_done[r], used)
                for k in range(4):
                    mm = nc.tensor.transpose(t_ps[r][:, k, :], z[r][:, k * P:(k + 1) * P], eye[:, :])
                mm.then_inc(tr_done[r], 1)

            pe.wait_ge(eye_in, 16)
            pipeline(pe, GS, [(inv, 0), (turn, 2)])

        @block.scalar
        def _(act):
            act.dma_start(eye[:, :], t["t_eye"][:, :]).then_inc(eye_in, 16)
            act.dma_start(gate[:, :], rows[0, :].partition_broadcast(P)).then_inc(gate_in, 16)

            def high(it, b):
                r, used = at(it, b, 2)
                after(act, mm_done[r], used)
                if not isinstance(it, int):
                    plain(act, gate_in, 16)
                nc.scalar.activation(xhi[r][:, :, :], x[:, :, 4 * it + b, :], ACT.Copy).then_inc(hi_done[r], 1)

            def evac(it, b):
                r, used = at(it, b, 2)
                act.wait_ge(mm_done[r], used + 1)
                after(act, tr_done[r], used)
                nc.scalar.activation(z[r][:, :], z_ps[r][:, :], ACT.Copy).then_inc(z_done[r], 1)

            def whigh(it, b):
                if b % 2 == 1:
                    r = (b % U) // 2
                    k = it + b // U
                    act.wait_ge(w_scaled[r], k + 1)
                    plain(act, gate_in, 16)
                    nc.scalar.activation(whl[:, 0, 2 * k + r, :], wf[r][:, :], ACT.Copy).then_inc(whi_done[r], 1)

            pipeline(act, GS, [(evac, 2), (high, 0), (whigh, 2)])

        @block.gpsimd
        def _(pool):
            def load(k):
                pool.dma_start(wf[k % 2][:, :], t["w_out"][0, k * P:(k + 1) * P, :]).then_inc(w_in[k % 2], 16)

            load(0)
            load(1)
            for k in range(KT):
                r = k % 2
                pool.wait_ge(whi_done[r], k // 2 + 1)
                nc.gpsimd.tensor_tensor(whl[:, 1, k, :], wf[r][:, :], f32(whl[:, 0, k, :]),
                                        ALU.subtract).then_inc(wlo_done[r], 1)
                if k + 2 < KT:
                    pool.wait_ge(wlo_done[r], k // 2 + 1)
                    load(k + 2)

        @block.vector
        def _(dve):
            def low(it, b):
                r, used = at(it, b, 2)
                dve.wait_ge(hi_done[r], used + 1)
                after(dve, mm_done[r], used)
                nc.vector.tensor_tensor(xlo[r][:, :, :], x[:, :, 4 * it + b, :], f32(xhi[r][:, :, :]),
                                        ALU.subtract).then_inc(lo_done[r], 1)

            def gated(it, b):
                r, used = at(it, b, 2)
                dve.wait_ge(tr_done[r], used + 1)
                g = 4 * it + b
                nc.vector.tensor_tensor(yg[:, :, :, g], t_ps[r][:, :, :], yg[:, :, :, g], ALU.mult).then_inc(y_done[r], 1)

            def wscale(it, b):
                if b % 2 == 1:
                    r = (b % U) // 2
                    k = it + b // U
                    dve.wait_ge(w_in[r], 16 * k + 16)
                    dve.wait_ge(gate_in, 16)
                    nc.vector.tensor_tensor(wf[r][:, :], wf[r][:, :], gate[:, :], ALU.mult).then_inc(w_scaled[r], 1)

            pipeline(dve, GS, [(low, 0), (wscale, 1, 0), (gated, 3, 0)])



def output_norm(nc, t, ya, yp, whl, gate_bias, out):
    with Scope(nc, "out") as s:
        yb = s.sb("yb", [P, 4, L])
        yhi = [s.sb(f"yhi{b}", [P, KT, P], F32R) for b in range(2)]
        ylo = [s.sb(f"ylo{b}", [P, KT, P], F32R) for b in range(2)]
        x = [s.sb(f"x{b}", [P, D]) for b in range(2)]
        res = [s.sb(f"res{b}", [P, D]) for b in range(2)]
        o = [s.sb(f"o{b}", [P, D]) for b in range(2)]
        ln_g = s.sb("ln_g", [P, D])
        ln_b = s.sb("ln_b", [P, D])
        stats = [s.sb(f"stats{b}", [P, 2, 6]) for b in range(2)]
        mv = [s.sb(f"mv{b}", [P, 2]) for b in range(2)]
        sm = [s.sb(f"sm{b}", [P, 4]) for b in range(2)]
        eps = s.sb("eps", [P, 1])
        ps = [s.ps(f"ps{b}", [P, 2, CH]) for b in range(2)]
        consts, eps_set = s.sem("consts"), s.sem("eps_set")
        yb_in = s.sems("yb_in", 4)
        x_in, hi_done, lo_done, mm_done, step, skip_done, sum_done, var_done, root_done, norm_done, scaled, o_done, stored = (
            s.sems(n) for n in ("x_in", "hi_done", "lo_done", "mm_done", "step", "skip_done", "sum_done", "var_done",
                                "root_done", "norm_done", "scaled", "o_done", "stored"))
        block = s.block()

        @block.sync
        def _(sp):
            def load_yb(c):
                cols = slice(c * CH, (c + 1) * CH)
                sp.dma_start(yb[:, :, cols], yp[:, :, cols].rearrange("k p t -> p k t")).then_inc(yb_in[c], 16)

            def load(it, b):
                r, used = at(it, b, 2)
                after(sp, skip_done[r], used)
                row = P * (U * it + b)
                src = t["x"][0, row:row + P, :] if isinstance(it, int) else t["x"][0, bass.ds(row, P), :]
                sp.dma_start(x[r][:, :], src).then_inc(x_in[r], 16)
                if isinstance(it, int) and U * it + b == 1:
                    sp.dma_start(ln_g[:, :], t["ln_g"][0, :].partition_broadcast(P)).then_inc(consts, 16)
                    sp.dma_start(ln_b[:, :], t["ln_b"][0, :].partition_broadcast(P)).then_inc(consts, 16)
                    for c in range(1, 4):
                        load_yb(c)

            def store(it, b):
                r, used = at(it, b, 2)
                sp.wait_ge(o_done[r], used + 1)
                row = P * (U * it + b)
                dst = out[0, row:row + P, :] if isinstance(it, int) else out[0, bass.ds(row, P), :]
                sp.dma_start(dst, o[r][:, :]).then_inc(stored[r], 16)

            load_yb(0)
            pipeline(sp, GS, [(load, 0), (store, 2)])
            for r in range(2):
                sp.wait_ge(stored[r], 16 * GS // 2)

        @block.tensor
        def _(pe):
            def unit(it, b):
                r, used = at(it, b, 2)
                after(pe, sum_done[r], used)
                for part in range(2):
                    pe.wait_ge(lo_done[r], 2 * used + part + 1)
                    for h in range(2):
                        cols = slice(h * CH, (h + 1) * CH)
                        for k in range(4 * part, 4 * part + 4):
                            mm = mm3(nc, ps[r][:, h, :], (yhi[r][:, k, :], ylo[r][:, k, :]),
                                     (whl[:, 0, k, cols], whl[:, 1, k, cols]), k == 0, k == KT - 1)
                mm.then_inc(mm_done[r], 1)

            pipeline(pe, GS, [(unit, 0)])

        @block.scalar
        def _(act):
            def high(it, b):
                r, used = at(it, b, 2)
                cols = bass.ds(P * (U * it + b), P)
                after(act, mm_done[r], used)
                if not isinstance(it, int):
                    plain(act, yb_in[3], 16)
                nc.scalar.activation(yhi[r][:, 0:4, :], ya[:, :, cols], ACT.Copy).then_inc(hi_done[r], 1)
                if isinstance(it, int) and b == 0:
                    act.wait_ge(yb_in[it], 16)
                nc.scalar.activation(yhi[r][:, 4:8, :], yb[:, :, cols], ACT.Copy).then_inc(hi_done[r], 1)

            def root(it, b):
                r, used = at(it, b, 2)
                act.wait_ge(var_done[r], used + 1)
                nc.scalar.activation(sm[r][:, 0:1], mv[r][:, 1:2], ACT.Sqrt, bias=eps[:, 0:1]).then_inc(root_done[r], 1)

            act.wait_ge(eps_set, 1)
            pipeline(act, GS, [(high, 0), (root, 2)])

        @block.gpsimd
        def _(pool):
            nc.gpsimd.memset(eps[:, :], LN_EPS).then_inc(eps_set, 1)
            pool.wait_ge(eps_set, 1)
            pool.wait_ge(consts, 32)
            for n in range(GS):
                b, it = n % 2, n // 2
                pool.wait_ge(norm_done[b], it + 1)
                after(pool, stored[b], 16 * it)
                nc.gpsimd.tensor_tensor(o[b][:, :], res[b][:, :], ln_g[:, :], ALU.mult).then_inc(scaled[b], 1)
                pool.wait_ge(scaled[b], it + 1)
                nc.gpsimd.tensor_tensor(o[b][:, :], o[b][:, :], ln_b[:, :], ALU.add).then_inc(o_done[b], 1)

        @block.vector
        def _(dve):
            def low(it, b):
                r, used = at(it, b, 2)
                cols = bass.ds(P * (U * it + b), P)
                dve.wait_ge(hi_done[r], 2 * used + 1)
                after(dve, mm_done[r], used)
                nc.vector.tensor_tensor(ylo[r][:, 0:4, :], ya[:, :, cols],
                                        f32(yhi[r][:, 0:4, :]), ALU.subtract).then_inc(lo_done[r], 1)
                dve.wait_ge(hi_done[r], 2 * used + 2)
                nc.vector.tensor_tensor(ylo[r][:, 4:8, :], yb[:, :, cols],
                                        f32(yhi[r][:, 4:8, :]), ALU.subtract).then_inc(lo_done[r], 1)

            def skip(it, b):
                r, used = at(it, b, 2)
                dve.wait_ge(x_in[r], 16 * used + 16)
                after(dve, scaled[r], used)
                nc.vector.scalar_tensor_tensor(out=res[r][:, :], in0=x[r][:, :], scalar=ALPHA, in1=gate_bias[:, :],
                                               op0=ALU.mult, op1=ALU.add).then_inc(skip_done[r], 1)

            def norm(it, b):
                r, used = at(it, b, 2)
                STEPS = 6
                n = STEPS * used
                done = [0]

                def then(ins):
                    ins.then_inc(step[r], 1)
                    done[0] += 1
                    dve.wait_ge(step[r], n + done[0])

                dve.wait_ge(skip_done[r], used + 1)
                dve.wait_ge(mm_done[r], used + 1)
                nc.vector.tensor_tensor(res[r][:, :], ps[r][:, :, :].rearrange("p a b -> p (a b)"), res[r][:, :],
                                        ALU.add).then_inc(sum_done[r], 1)
                dve.wait_ge(sum_done[r], used + 1)
                for h in range(2):
                    ins = nc.vector.bn_stats(stats[r][:, h, :], res[r][:, h * CH:(h + 1) * CH])
                then(ins)
                nc.vector.memset(sm[r][:, 2:4], 0.0)
                nc.vector.bn_aggr(mv[r][:, :], stats[r][:, :, :].rearrange("p a b -> p (a b)")).then_inc(var_done[r], 1)
                dve.wait_ge(root_done[r], used + 1)
                then(nc.vector.reciprocal(sm[r][:, 1:2], sm[r][:, 0:1]))
                then(nc.vector.tensor_scalar(sm[r][:, 2:3], mv[r][:, 1:2], LN_EPS, sm[r][:, 1:2], ALU.add, ALU.mult))
                then(nc.vector.tensor_tensor(sm[r][:, 2:3], sm[r][:, 2:3], sm[r][:, 1:2], ALU.mult))
                then(nc.vector.tensor_scalar(sm[r][:, 2:3], sm[r][:, 2:3], -0.5, 1.5, ALU.mult, ALU.add))
                then(nc.vector.tensor_tensor(sm[r][:, 3:4], sm[r][:, 2:3], sm[r][:, 1:2], ALU.mult))
                assert done[0] == STEPS
                nc.vector.tensor_scalar(res[r][:, :], res[r][:, :], mv[r][:, 0:1], sm[r][:, 3:4],
                                        ALU.subtract, ALU.mult).then_inc(norm_done[r], 1)

            pipeline(dve, GS, [(low, 0), (skip, 0), (norm, 1)])


def encoder_layer(nc, t, out):
    def scratch(name, shape):
        return nc.dram_tensor(name, shape, F32, kind="Internal").ap()

    kfreq = scratch("kfreq", [2, NPAIR, P, 2, DH])
    vx = scratch("vx", [P, GS, 2 * DH])
    g2 = scratch("g2", [4, P, L])
    yp = scratch("yp", [4, P, L])
    rows = scratch("rows", [2, D])
    tabs = {n: scratch("own_" + n, list(t["t_" + n].shape)) for n in ("w1f", "w1s", "iw1", "dft", "f0", "i0")}

    with Scope(nc, "all") as s:
        scale1 = s.sb("scale1", [P, KT])
        shift = s.sb("shift", [P, KT])
        with Scope(nc, "flt") as f:
            with (nc.sbuf_tensor("hfil", [P, 2, P, GF], F32R, side="right") as hfil,
                  nc.sbuf_tensor("wfil", [P, 2, 2, DH], F32R, side="right") as wfil):
                front(nc, t, hfil, wfil, tabs, scale1, shift, rows)
                xf = f.sb("xf", [P, 2, GF, DH])
                filter_stage1(nc, t, tabs, hfil, wfil, xf)
            filter_stage2(nc, tabs, xf, kfreq)
        with Scope(nc, "u") as u:
            uhi = u.sb("uhi", [P, KT, L], F32R)
            ulo = u.sb("ulo", [P, KT, L], F32R)
            project(nc, t, tabs, scale1, shift, uhi, ulo, vx, g2, yp)
        x_scope = Scope(nc, "x")
        x = x_scope.sb("x", [P, 2, GS, DH])
        spec = Scope(nc, "spec")
        dft = Dft(spec)
        signal_stage1(nc, vx, tabs, dft, x)
        spectrum_product(nc, "sp0", dft, x, kfreq[0])
        between_orders(nc, vx, tabs, x)
        with (nc.sbuf_tensor("ya", [P, 4, L], F32, side="right") as ya,
              nc.sbuf_tensor("gate_bias", [P, D], F32, side="right") as gate_bias):
            spectrum_product(nc, "sp1", dft, x, kfreq[1],
                             prefetch=[(ya[:, k, h * D:(h + 1) * D], g2[k, :, h * D:(h + 1) * D])
                                       for k in range(4) for h in range(2)]
                             + [(gate_bias[:, :], rows[1, :].partition_broadcast(P))])
            spec.ctx.close()
            with nc.sbuf_tensor("whl", [P, 2, KT, D], F32R, side="right") as whl:
                last_inverse(nc, t, tabs, x, rows, ya, whl)
                x_scope.ctx.close()
                output_norm(nc, t, ya, yp, whl, gate_bias, out)


_INS = ["x", "c", "w_ada", "b_ada", "w_in", "b_in", "conv_w", "conv_b", "filt_w1", "filt_b1", "filt_w_inner",
        "filt_b_inner", "filt_w_out", "filt_freq", "hyena_bias", "pool_w", "pool_scale", "w_out", "b_out",
        "ln_g", "ln_b"]


def kernel(**inputs):
    import numpy as _np
    import concourse.bacc as _bacc
    from concourse import mybir as _mybir
    from concourse.bass_utils import run_bass_kernel_spmd as _run

    nc = _bacc.Bacc("TRN2", target_bir_lowering=False, num_devices=1)
    arrays, args = {}, {}
    given = {name: _np.ascontiguousarray(inputs[name]) for name in _INS}
    for name, a in {**given, **shape_tables()}.items():
        arrays[f"in_{name}"] = a
        args[name] = nc.dram_tensor(f"in_{name}", a.shape, _mybir.dt.from_np(a.dtype), kind="ExternalInput").ap()
    out = nc.dram_tensor("out_0", (1, L, D), _mybir.dt.float32, kind="ExternalOutput").ap()
    encoder_layer(nc, args, out)
    r = _run(nc, [arrays], core_ids=[0])
    return r.results[0]["out_0"]
```
